# Optimizing a Trainium2 kernel written in Bass

```python
import math
import jax, jax.numpy as jnp
from jax import lax
import numpy as np

'''Two layers of a hybrid autoregressive decoder trunk (Hymba-style parallel head groups).

Each layer:
  adaLN(c) -> sandwich RMSNorm -> ONE combined input projection whose columns are split into
  [differential-attention q/k/v | RWKV-7 r/k/v + low-rank decay/a/gate inputs | chunked gMLP u/v].
  The three mixers run in parallel on the same normalised input; their outputs are concatenated
  over head groups (512 + 256 + 256 = D_MODEL) into ONE output projection, post-normed, gated, added.
  Then adaLN(c) -> sandwich RMSNorm -> DeepSeek-V3-style fine-grained MoE (sigmoid top-8 of 64,
  group-limited routing, one shared expert) -> post-norm -> gate -> residual add.
Inputs: x (BATCH, SEQ, D_MODEL), c (BATCH, D_MODEL), per-layer parameters stacked on a leading DEPTH axis,
  one T5 relative-position bias table (32, 4) shared by both layers.
Output: (BATCH, SEQ, D_MODEL).
'''

D_MODEL = 1024
BATCH = 1
SEQ = 1024
DEPTH = 1

A_HEADS = 4
A_QK_DIM = 64
A_WIDTH = A_HEADS * 2 * A_QK_DIM
Q_BLOCK = 128
N_BUCKETS = 32
MAX_DISTANCE = 128
B_HEADS = 4
B_HEAD_DIM = 64
B_WIDTH = B_HEADS * B_HEAD_DIM
B_DECAY_LORA = 64
B_AAA_LORA = 64
B_GATE_LORA = 128
B_LNX_EPS = 64e-5
C_GROUPS = 4
C_GROUP_DIM = 64
C_WIDTH = C_GROUPS * C_GROUP_DIM
CHUNK = 128
A_COLS = 3 * A_WIDTH
B_COLS = 3 * B_WIDTH + B_DECAY_LORA + B_AAA_LORA + B_GATE_LORA
C_COLS = 2 * C_WIDTH
IN_COLS = A_COLS + B_COLS + C_COLS
MIX_WIDTH = A_WIDTH + B_WIDTH + C_WIDTH
N_EXPERTS = 64
TOP_K = 8
N_GROUPS = 8
TOPK_GROUPS = 4
EXPERTS_PER_GROUP = N_EXPERTS // N_GROUPS
D_EXPERT = 256
D_SHARED = 256
ROUTED_SCALE = 2.5
EXPERT_BLOCK = 256
RMS_EPS = 1e-6

kernel_name = 'hybrid_diffattn_rwkv7_gmlp_moe_block'

def rmsnorm(x, g):
    xf = x.astype(jnp.float32)
    y = xf * lax.rsqrt(jnp.mean(xf * xf, axis=-1, keepdims=True) + RMS_EPS) * g.astype(jnp.float32)
    return y.astype(x.dtype)

def layernorm(x, g, b, eps=1e-5):
    xf = x.astype(jnp.float32)
    mu = jnp.mean(xf, axis=-1, keepdims=True)
    var = jnp.mean((xf - mu) ** 2, axis=-1, keepdims=True)
    y = (xf - mu) * lax.rsqrt(var + eps) * g.astype(jnp.float32) + b.astype(jnp.float32)
    return y.astype(x.dtype)

def t5_bucket(dist):
    n = jnp.maximum(dist, 0)
    max_exact = N_BUCKETS // 2
    nf = jnp.maximum(n, 1).astype(jnp.float32)
    large = max_exact + (jnp.log(nf / max_exact) / math.log(MAX_DISTANCE / max_exact)
                         * (N_BUCKETS - max_exact)).astype(jnp.int32)
    large = jnp.minimum(large, N_BUCKETS - 1)
    return jnp.where(n < max_exact, n, large)

def diff_attention(pa, table, lam_par, subln_g, lambda_init):
    Bn, S, _ = pa.shape
    q = pa[..., :A_WIDTH].reshape(Bn, S, A_HEADS, 2, A_QK_DIM)
    k = pa[..., A_WIDTH:2 * A_WIDTH].reshape(Bn, S, A_HEADS, 2, A_QK_DIM)
    v = pa[..., 2 * A_WIDTH:].reshape(Bn, S, A_HEADS, 2 * A_QK_DIM)
    lp = lam_par.astype(jnp.float32)
    lam = jnp.exp(jnp.sum(lp[0] * lp[1])) - jnp.exp(jnp.sum(lp[2] * lp[3])) + lambda_init
    scale = A_QK_DIM ** -0.5
    outs = []
    for i in range(S // Q_BLOCK):
        q0 = i * Q_BLOCK
        L = q0 + Q_BLOCK
        dist = jnp.arange(q0, L)[:, None] - jnp.arange(L)[None, :]
        bias = jnp.transpose(table[t5_bucket(dist)].astype(jnp.float32), (2, 0, 1))
        logits = jnp.einsum('bqhmd,bkhmd->bmhqk', q[:, q0:L], k[:, :L]).astype(jnp.float32) * scale + bias
        logits = jnp.where(dist >= 0, logits, -jnp.inf)
        probs = jax.nn.softmax(logits, axis=-1)
        attn = (probs[:, 0] - lam * probs[:, 1]).astype(v.dtype)
        outs.append(jnp.einsum('bhqk,bkhe->bqhe', attn, v[:, :L]))
    o = jnp.concatenate(outs, axis=1)
    o = rmsnorm(o, subln_g) * (1.0 - lambda_init)
    return o.reshape(Bn, S, A_WIDTH)

def _rwkv7_step(state, inp):
    r, w, k, v, a, b = inp
    sa = jnp.einsum('bhij,bhj->bhi', state, a)
    state = state * w[:, :, None, :] + sa[..., None] * b[:, :, None, :] + v[..., None] * k[:, :, None, :]
    y = jnp.einsum('bhij,bhj->bhi', state, r)
    return state, y

def rwkv7_time_mix(pb, mu, w0, w2, a0, a2, g2, k_k, k_a, r_k, lnx_g, lnx_b):
    Bn, S, _ = pb.shape
    prev = jnp.pad(pb[:, :-1], ((0, 0), (1, 0), (0, 0)))
    p = pb + (prev - pb) * mu
    o1, o2, o3 = B_WIDTH, 2 * B_WIDTH, 3 * B_WIDTH
    o4 = o3 + B_DECAY_LORA
    o5 = o4 + B_AAA_LORA
    r, k, v = p[..., :o1], p[..., o1:o2], p[..., o2:o3]
    wd, ad, gd = p[..., o3:o4], p[..., o4:o5], p[..., o5:]
    w = -jax.nn.softplus(-(w0 + jnp.tanh(wd) @ w2)) - 0.5
    decay = jnp.exp(-jnp.exp(w.astype(jnp.float32)))
    a = jax.nn.sigmoid(a0 + ad @ a2)
    g = jax.nn.sigmoid(gd) @ g2
    hs = lambda t: t.reshape(Bn, S, B_HEADS, B_HEAD_DIM).astype(jnp.float32)
    kk = hs(k * k_k)
    kk = kk * lax.rsqrt(jnp.maximum(jnp.sum(kk * kk, axis=-1, keepdims=True), 1e-24))
    k = k * (1 + (a - 1) * k_a)
    rh, kh, vh, ah, wh = hs(r), hs(k), hs(v), hs(a), hs(decay)
    xs = tuple(jnp.moveaxis(t, 1, 0) for t in (rh, wh, kh, vh, -kk, kk * ah))
    state0 = jnp.zeros((Bn, B_HEADS, B_HEAD_DIM, B_HEAD_DIM), jnp.float32)
    _, y = lax.scan(_rwkv7_step, state0, xs)
    y = jnp.moveaxis(y, 0, 1)
    mean = jnp.mean(y, axis=-1, keepdims=True)
    var = jnp.mean((y - mean) ** 2, axis=-1, keepdims=True)
    y = ((y - mean) * lax.rsqrt(var + B_LNX_EPS)).reshape(Bn, S, B_WIDTH) * lnx_g.astype(jnp.float32) \
        + lnx_b.astype(jnp.float32)
    bonus = jnp.sum(rh * kh * r_k.astype(jnp.float32), axis=-1, keepdims=True) * vh
    y = y + bonus.reshape(Bn, S, B_WIDTH)
    return (y * g.astype(jnp.float32)).astype(pb.dtype)

def chunk_gmlp(pc, ln_g, ln_b, w_s, b_s):
    Bn, S, _ = pc.shape
    z = jax.nn.gelu(pc)
    u, v = z[..., :C_WIDTH], z[..., C_WIDTH:]
    v = layernorm(v, ln_g, ln_b)
    vc = v.reshape(Bn, S // CHUNK, CHUNK, C_GROUPS, C_GROUP_DIM)
    ws = w_s * jnp.tril(jnp.ones((CHUNK, CHUNK), w_s.dtype))
    sv = jnp.einsum('gts,bcsgd->bctgd', ws, vc) + jnp.transpose(b_s)[None, None, :, :, None]
    return u * sv.reshape(Bn, S, C_WIDTH)

def moe_ffn(h, w_router, e_bias, w1, w3, w2, ws1, ws3, ws2):
    Bn, S, D = h.shape
    T = Bn * S
    xt = h.reshape(T, D)
    scores = jax.nn.sigmoid((xt @ w_router).astype(jnp.float32))
    biased = scores + e_bias.astype(jnp.float32)
    grp_score = jnp.sum(lax.top_k(biased.reshape(T, N_GROUPS, EXPERTS_PER_GROUP), 2)[0], axis=-1)
    _, top_g = lax.top_k(grp_score, TOPK_GROUPS)
    gmask = jnp.any(top_g[:, :, None] == jnp.arange(N_GROUPS)[None, None, :], axis=1)
    masked = jnp.where(jnp.repeat(gmask, EXPERTS_PER_GROUP, axis=1), biased, -jnp.inf)
    _, top_idx = lax.top_k(masked, TOP_K)
    top_s = jnp.take_along_axis(scores, top_idx, axis=1)
    top_w = top_s / (jnp.sum(top_s, axis=-1, keepdims=True) + 1e-20) * ROUTED_SCALE
    M = T * TOP_K
    flat_e = top_idx.reshape(M)
    flat_w = top_w.reshape(M)
    order = jnp.argsort(flat_e)
    se = flat_e[order]
    counts = jnp.bincount(flat_e, length=N_EXPERTS)
    padded = (counts + EXPERT_BLOCK - 1) // EXPERT_BLOCK * EXPERT_BLOCK
    pad_end = jnp.cumsum(padded)
    pad_start = pad_end - padded
    grp_start = jnp.cumsum(counts) - counts
    dest = pad_start[se] + jnp.arange(M) - grp_start[se]
    n_blocks = -(-M // EXPERT_BLOCK) + N_EXPERTS
    P = n_blocks * EXPERT_BLOCK
    row_tok = jnp.zeros((P,), jnp.int32).at[dest].set((order // TOP_K).astype(jnp.int32))
    row_w = jnp.zeros((P,), jnp.float32).at[dest].set(flat_w[order])
    blk_e = jnp.minimum(jnp.searchsorted(pad_end, jnp.arange(n_blocks) * EXPERT_BLOCK, side='right'),
                        N_EXPERTS - 1)

    def expert_block(args):
        tok, e = args
        xb = xt[tok]
        hb = jax.nn.silu(xb @ w1[e]) * (xb @ w3[e])
        return hb @ w2[e]

    yb = lax.map(expert_block, (row_tok.reshape(n_blocks, EXPERT_BLOCK), blk_e))
    routed = jnp.zeros_like(xt).at[row_tok].add((yb.reshape(P, D) * row_w[:, None]).astype(xt.dtype))
    shared = (jax.nn.silu(xt @ ws1) * (xt @ ws3)) @ ws2
    return (routed + shared).reshape(Bn, S, D)

def setup_inputs(seed: int = 0) -> dict:
    key = jax.random.key(seed)
    ks = jax.random.split(key, 40)
    L, D, E, F = DEPTH, D_MODEL, N_EXPERTS, D_EXPERT
    nrm = lambda k, shape, s: jax.random.normal(k, shape, jnp.float32) * s
    gain = lambda k, shape: 1.0 + 0.01 * jax.random.normal(k, shape, jnp.float32)
    return {
        'x': nrm(ks[0], (BATCH, SEQ, D), 1.0),
        'c': nrm(ks[1], (BATCH, D), 1.0),
        'w_ada': nrm(ks[2], (L, D, 6 * D), 0.5 * D ** -0.5),
        'b_ada': nrm(ks[3], (L, 6 * D), 0.01),
        'norm_pre_mix': gain(ks[4], (L, D)),
        'norm_post_mix': gain(ks[5], (L, D)),
        'norm_pre_ffn': gain(ks[6], (L, D)),
        'norm_post_ffn': gain(ks[7], (L, D)),
        'w_in': nrm(ks[8], (L, D, IN_COLS), D ** -0.5),
        'w_out': nrm(ks[9], (L, MIX_WIDTH, D), MIX_WIDTH ** -0.5),
        'rel_bias_table': nrm(ks[10], (N_BUCKETS, A_HEADS), 0.5),
        'diff_lambda': nrm(ks[11], (L, 4, A_QK_DIM), 0.1),
        'diff_subln': gain(ks[12], (L, 2 * A_QK_DIM)),
        'rwkv_mu': jax.random.uniform(ks[13], (L, B_COLS), jnp.float32),
        'rwkv_w0': jax.random.uniform(ks[14], (L, B_WIDTH), jnp.float32, -6.0, 0.0),
        'rwkv_w2': nrm(ks[15], (L, B_DECAY_LORA, B_WIDTH), 0.1 * B_DECAY_LORA ** -0.5),
        'rwkv_a0': nrm(ks[16], (L, B_WIDTH), 0.1),
        'rwkv_a2': nrm(ks[17], (L, B_AAA_LORA, B_WIDTH), 0.1 * B_AAA_LORA ** -0.5),
        'rwkv_g2': nrm(ks[18], (L, B_GATE_LORA, B_WIDTH), B_GATE_LORA ** -0.5),
        'rwkv_k_k': 0.85 + nrm(ks[19], (L, B_WIDTH), 0.01),
        'rwkv_k_a': gain(ks[20], (L, B_WIDTH)),
        'rwkv_r_k': nrm(ks[21], (L, B_HEADS, B_HEAD_DIM), 0.1),
        'rwkv_lnx_g': gain(ks[22], (L, B_WIDTH)),
        'rwkv_lnx_b': nrm(ks[23], (L, B_WIDTH), 0.01),
        'gmlp_ln_g': gain(ks[24], (L, C_WIDTH)),
        'gmlp_ln_b': nrm(ks[25], (L, C_WIDTH), 0.01),
        'gmlp_w_s': nrm(ks[26], (L, C_GROUPS, CHUNK, CHUNK), 0.5 * CHUNK ** -0.5),
        'gmlp_b_s': gain(ks[27], (L, C_GROUPS, CHUNK)),
        'router_w': nrm(ks[28], (L, D, E), D ** -0.5),
        'router_bias': nrm(ks[29], (L, E), 0.01),
        'exp_w1': nrm(ks[30], (L, E, D, F), D ** -0.5),
        'exp_w3': nrm(ks[31], (L, E, D, F), D ** -0.5),
        'exp_w2': nrm(ks[32], (L, E, F, D), F ** -0.5),
        'shared_w1': nrm(ks[33], (L, D, D_SHARED), D ** -0.5),
        'shared_w3': nrm(ks[34], (L, D, D_SHARED), D ** -0.5),
        'shared_w2': nrm(ks[35], (L, D_SHARED, D), D_SHARED ** -0.5),
    }

def reference(x, c, w_ada, b_ada, norm_pre_mix, norm_post_mix, norm_pre_ffn, norm_post_ffn,
              w_in, w_out, rel_bias_table, diff_lambda, diff_subln,
              rwkv_mu, rwkv_w0, rwkv_w2, rwkv_a0, rwkv_a2, rwkv_g2, rwkv_k_k, rwkv_k_a, rwkv_r_k,
              rwkv_lnx_g, rwkv_lnx_b, gmlp_ln_g, gmlp_ln_b, gmlp_w_s, gmlp_b_s,
              router_w, router_bias, exp_w1, exp_w3, exp_w2, shared_w1, shared_w3, shared_w2):
    cond = jax.nn.silu(c)
    for l in range(DEPTH):
        mod = cond @ w_ada[l] + b_ada[l]
        sh1, sc1, g1, sh2, sc2, g2 = jnp.split(mod[:, None, :], 6, axis=-1)
        h = rmsnorm(x, norm_pre_mix[l]) * (1 + sc1) + sh1
        proj = h @ w_in[l]
        pa = proj[..., :A_COLS]
        pb = proj[..., A_COLS:A_COLS + B_COLS]
        pc = proj[..., A_COLS + B_COLS:]
        lambda_init = 0.8 - 0.6 * math.exp(-0.3 * l)
        ya = diff_attention(pa, rel_bias_table, diff_lambda[l], diff_subln[l], lambda_init)
        yb = rwkv7_time_mix(pb, rwkv_mu[l], rwkv_w0[l], rwkv_w2[l], rwkv_a0[l], rwkv_a2[l], rwkv_g2[l],
                            rwkv_k_k[l], rwkv_k_a[l], rwkv_r_k[l], rwkv_lnx_g[l], rwkv_lnx_b[l])
        yc = chunk_gmlp(pc, gmlp_ln_g[l], gmlp_ln_b[l], gmlp_w_s[l], gmlp_b_s[l])
        y = jnp.concatenate([ya, yb, yc], axis=-1) @ w_out[l]
        x = x + g1 * rmsnorm(y, norm_post_mix[l])
        h = rmsnorm(x, norm_pre_ffn[l]) * (1 + sc2) + sh2
        y = moe_ffn(h, router_w[l], router_bias[l], exp_w1[l], exp_w3[l], exp_w2[l],
                    shared_w1[l], shared_w3[l], shared_w2[l])
        x = x + g2 * rmsnorm(y, norm_post_ffn[l])
    return x


_drawn_inputs = setup_inputs


def setup_inputs(seed=0):
    import zlib

    import numpy as np

    out = dict(_drawn_inputs(seed))
    spreads = {}
    factors = {'norm_pre_mix': 4.001,
     'norm_post_mix': 4.406,
     'norm_post_ffn': 56.034,
     'diff_subln': 20.478,
     'rwkv_w2': 8.0,
     'rwkv_a0': 3.249,
     'rwkv_a2': 3.4,
     'rwkv_k_k': 32.714,
     'rwkv_k_a': 6.724,
     'rwkv_lnx_g': 26.738,
     'rwkv_lnx_b': 31.635,
     'gmlp_ln_g': 30.077,
     'gmlp_ln_b': 36.682,
     'gmlp_b_s': 6.881}
    for name, (base, spread) in spreads.items():
        noise = np.random.default_rng([zlib.crc32(name.encode()), seed]).standard_normal(out[name].shape)
        drawn = base * np.exp(spread * noise) if base else spread * noise
        out[name] = __import__('jax').numpy.asarray(drawn.astype(out[name].dtype))
    for name, factor in factors.items():
        out[name] = (out[name] * factor).astype(out[name].dtype)
    return out
```

```python
import concourse.bass as bass
from concourse import mybir
from contextlib import ExitStack
import math
import numpy as np

F32 = mybir.dt.float32
ALU = mybir.AluOpType
ACT = mybir.ActivationFunctionType
AX = mybir.AxisListType

P = 128
D = 1024
S = 1024
NT = S // P
KC = D // P
BANK = 512
AH, AQK = 4, 64
AW = AH * 2 * AQK
BH, BD = 4, 64
BW = BH * BD
CG, CD = 4, 64
CW = CG * CD
A_COLS, B_COLS = 3 * AW, 3 * BW + 64 + 64 + 128
RMS_EPS = 1e-6
LN_EPS = 1e-5
EXP_AND_LN = 6
GELU_1 = 2.0 * math.sqrt(2.0 / math.pi)
GELU_3 = GELU_1 * 0.044715


class Steps:

    def __init__(self, eng, sem):
        self.eng, self.sem, self.n = eng, sem, 0

    def then(self, ins):
        self.n += 1
        ins.then_inc(self.sem, 1)
        self.eng.wait_ge(self.sem, self.n)

    def restart(self):
        self.eng.sem_inc(self.sem, 1)
        self.eng.sem_clear(self.sem)
        self.n = 0


def make_rows(nc, io, dr):
    NCH = 6 * D // BANK
    with ExitStack() as ctx:
        sb = lambda n, s: ctx.enter_context(nc.sbuf_tensor(n, s, F32))
        sem = lambda n: ctx.enter_context(nc.semaphore(n))
        c_col = sb("c_col", [P, KC])
        e_col = sb("e_col", [P, KC])
        cond = sb("cond", [P, KC, P])
        w = [sb(f"w_ada{j}", [P, KC, BANK]) for j in range(2)]
        mod = sb("mod", [P, 6 * D])
        gains = sb("gains", [P, 4, D])
        ps = [ctx.enter_context(nc.psum_tensor(f"ps_mod{j}", [P, BANK], F32)) for j in range(2)]
        c_in, gains_in, cond_ready = sem("c_in"), sem("gains_in"), sem("cond_ready")
        w_in = [sem(f"w_ada_in{j}") for j in range(2)]
        mod_mm = [sem(f"mod_mm{j}") for j in range(2)]
        mod_read = [sem(f"mod_read{j}") for j in range(2)]
        c_low = sem("c_low")
        exp_done, dve_step, rows_ready, rows_out = sem("exp_done"), sem("dve_step"), sem("rows_ready"), sem("rows_out")
        w_view = io["w_ada"][0].rearrange("(k p) n -> p k n", p=P)
        block = ctx.enter_context(nc.Block())

        @block.sync
        def _(sp):
            sp.dma_start(c_col[:], io["c"].rearrange("a (k p) -> p (a k)", p=P), allow_slow_non_contiguous=True).then_inc(c_in, 16)
            sp.dma_start(mod[:], io["b_ada"][0:1, :].partition_broadcast(P)).then_inc(gains_in, 16)
            for n, name in enumerate(("norm_pre_mix", "norm_post_mix", "norm_pre_ffn", "norm_post_ffn")):
                sp.dma_start(gains[:, n, :], io[name][0:1, :].partition_broadcast(P)).then_inc(gains_in, 16)
            with sp.Fori(0, NCH // 2) as i:
                for j in range(2):
                    sp.wait_ge(mod_mm[j], i + 1)
                    sp.dma_start(w[j][:], w_view[:, :, bass.ds((i * 2 + j) * BANK, BANK)]).then_inc(w_in[j], 16)
            sp.wait_ge(rows_ready, 1)
            sp.dma_start(dr["rows"], mod[0:1, :]).then_inc(rows_out, 16)
            sp.wait_ge(rows_out, 16)

        @block.scalar
        def _(act):
            act.wait_ge(c_low, 1)
            act.activation(e_col[:], e_col[:], ACT.Exp, scale=-1.0).then_inc(exp_done, 1)

        @block.tensor
        def _(pe):
            pe.sem_inc(mod_mm[0], 1)
            pe.sem_inc(mod_mm[1], 1)
            pe.wait_ge(cond_ready, 1)
            with pe.Fori(0, NCH // 2) as i:
                for j in range(2):
                    pe.wait_ge(w_in[j], i * 16 + 16)
                    pe.wait_ge(mod_read[j], i + 1)
                    for k in range(KC):
                        mm = pe.matmul(ps[j][:], cond[:, k, :], w[j][:, k, :], start=(k == 0), stop=(k == KC - 1))
                    mm.then_inc(mod_mm[j], 1)

        @block.vector
        def _(dve):
            step = Steps(dve, dve_step)
            dve.sem_inc(mod_read[0], 1)
            dve.sem_inc(mod_read[1], 1)
            dve.wait_ge(c_in, 16)
            dve.tensor_scalar(e_col[:], c_col[:], -80.0, None, ALU.max).then_inc(c_low, 1)
            dve.wait_ge(exp_done, 1)
            step.then(dve.tensor_scalar(e_col[:], e_col[:], 1.0, None, ALU.add))
            step.then(dve.reciprocal(e_col[:], e_col[:]))
            step.then(dve.tensor_tensor(c_col[:], c_col[:], e_col[:], ALU.mult))
            dve.tensor_copy(cond[:], c_col[:].unsqueeze(2).to_broadcast([P, KC, P])).then_inc(cond_ready, 1)
            dve.wait_ge(gains_in, 16 * 5)
            with dve.Fori(0, NCH // 2) as i:
                for j in range(2):
                    dve.wait_ge(mod_mm[j], i + 2)
                    m = mod[:, bass.ds((i * 2 + j) * BANK, BANK)]
                    dve.tensor_tensor(m, ps[j][:], m, ALU.add).then_inc(mod_read[j], 1)
            for j in range(2):
                dve.wait_ge(mod_read[j], NCH // 2 + 1)
            row = lambda n: mod[:, n * D:(n + 1) * D]
            for half in range(2):
                step.then(dve.scalar_tensor_tensor(row(3 * half + 1), row(3 * half + 1), 1.0, gains[:, 2 * half, :], ALU.add, ALU.mult))
                step.then(dve.tensor_tensor(row(3 * half + 2), row(3 * half + 2), gains[:, 2 * half + 1, :], ALU.mult))
            dve.sem_inc(rows_ready, 1)


def project(nc, io, dr, keep):
    GROUPS = 6
    with ExitStack() as ctx:
        sb = lambda n, s: ctx.enter_context(nc.sbuf_tensor(n, s, F32))
        sem = lambda n: ctx.enter_context(nc.semaphore(n))
        pt = lambda n: ctx.enter_context(nc.psum_tensor(n, [P, BANK], F32))
        w = sb("w_in", [P, KC, 3072])
        shift, scale = sb("shift1", [P, D]), sb("scale1", [P, D])
        ln_g, ln_b, b_s = sb("ln_g", [P, CW]), sb("ln_b", [P, CW]), sb("b_s", [P, CG])
        w_s, w_sT = sb("w_s", [P, CG, P]), sb("w_sT", [P, CG, P])
        x = sb("x_tile", [P, D])
        h = sb("h_tile", [P, D])
        hT = [sb(f"hT{j}", [P, KC, P]) for j in range(2)]
        pb = sb("pb_tile", [P, 2 * BANK])
        z, zt = sb("z", [P, 2 * CW]), sb("zt", [P, 2 * CW])
        st = sb("stats", [P, 8])
        yc = sb("yc", [P, CW])
        ident, upper = keep["ident"], keep["upper"]
        ps_t = [pt(f"ps_t{n}") for n in range(2)]
        ps_p = [pt(f"ps_p{n}") for n in range(4)]
        ps_s = pt("ps_s")
        w_loaded, consts_in, x_in, ss_ready = sem("w_loaded"), sem("consts_in"), sem("x_in"), sem("ss_ready")
        act_step, dve_step = sem("act_step"), sem("dve_step")
        rstd_ready, h_ready, tr_done, hT_ready = sem("rstd_ready"), sem("h_ready"), sem("tr_done"), sem("hT_ready")
        proj_mm, proj_read, pb_out, x_read = sem("proj_mm"), sem("proj_read"), sem("pb_out"), sem("x_read")
        arg_ready, e_ready, var_in, v_rstd = sem("arg_ready"), sem("e_ready"), sem("var_in"), sem("v_rstd")
        v_ready, sv_mm, yc_ready, yc_out, wsT_done, wsT_mm = sem("v_ready"), sem("sv_mm"), sem("yc_ready"), sem("yc_out"), sem("wsT_done"), sem("wsT_mm")
        z_read, pb_free, yc_free = sem("z_read"), sem("pb_free"), sem("yc_free")
        x_view = io["x"][0]
        block = ctx.enter_context(nc.Block())

        @block.sync
        def _(sp):
            sp.dma_start(shift[:], dr["rows"][:, 0:D].partition_broadcast(P)).then_inc(consts_in, 16)
            sp.dma_start(scale[:], dr["rows"][:, D:2 * D].partition_broadcast(P)).then_inc(consts_in, 16)
            sp.dma_start(w_s[:], io["gmlp_w_s"][0].rearrange("g t s -> t g s")).then_inc(consts_in, 16)
            sp.dma_start(ln_g[:], io["gmlp_ln_g"][0:1, :].partition_broadcast(P)).then_inc(consts_in, 16)
            sp.dma_start(ln_b[:], io["gmlp_ln_b"][0:1, :].partition_broadcast(P)).then_inc(consts_in, 16)
            sp.dma_start(b_s[:], io["gmlp_b_s"][0].rearrange("g t -> t g"), allow_slow_non_contiguous=True).then_inc(consts_in, 16)
            wv = io["w_in"][0].rearrange("(k p) n -> p k n", p=P)
            for k in range(KC):
                sp.dma_start(w[:, k, :], wv[:, k, :]).then_inc(w_loaded, 16)
            with sp.Fori(0, NT) as t:
                sp.wait_ge(x_read, t + 1)
                sp.dma_start(x[:], x_view[bass.ds(t * P, P), :]).then_inc(x_in, 16)
            sp.wait_ge(x_in, 16 * NT)

        @block.gpsimd
        def _(pool):
            pool.sem_inc(pb_free, 1)
            pool.sem_inc(yc_free, 1)
            with pool.Fori(0, NT) as t:
                pool.wait_ge(proj_read, t * GROUPS + 4 + 6)
                pool.dma_start(dr["pb"][bass.ds(t * P + 1, P), :], pb[:]).then_inc(pb_out, 16)
                pool.wait_ge(pb_out, t * 16 + 16)
                pool.sem_inc(pb_free, 1)
                pool.wait_ge(yc_ready, t + 1)
                pool.dma_start(dr["ymix"][bass.ds(t * P, P), AW + BW:D], yc[:]).then_inc(yc_out, 16)
                pool.wait_ge(yc_out, t * 16 + 16)
                pool.sem_inc(yc_free, 1)

        @block.scalar
        def _(act):
            load_exp_and_ln(nc, act)
            step = Steps(act, act_step)
            act.sem_inc(proj_read, 4)
            with act.Fori(0, NT // 2) as i:
                for j in range(2):
                    t = i * 2 + j
                    act.wait_ge(x_in, t * 16 + 16)
                    act.wait_ge(h_ready, t + 1)
                    act.wait_ge(tr_done, t + 1)
                    step.then(act.activation(h[:], x[:], ACT.Square, accum_out=st[:, 0:1]))
                    step.then(act.activation(st[:, 1:2], st[:, 0:1], ACT.Ln, scale=1.0 / D, bias=keep["eps"][:, 0:1]))
                    act.activation(st[:, 2:3], st[:, 1:2], ACT.Exp, scale=-0.5).then_inc(rstd_ready, 1)
                    for g in range(GROUPS):
                        act.wait_ge(proj_mm, i * (2 * GROUPS) + j * GROUPS + g + 1)
                        src = ps_p[(j * GROUPS + g) % 4]
                        if g == 0:
                            act.wait_ge(z_read, t + 1)
                            act.copy(z[:], src[:]).then_inc(proj_read, 1)
                        elif g < 3:
                            dst = (keep["qT"], keep["kT"])[g - 1]
                            act.copy(dst[:, :, bass.ds(t * P, P)], src[:].rearrange("p (h n) -> p h n", h=AH)).then_inc(proj_read, 1)
                        elif g == 3:
                            act.copy(keep["v"][:, bass.ds(t, 1), :], src[:].unsqueeze(1)).then_inc(proj_read, 1)
                        else:
                            act.wait_ge(pb_free, t + 1)
                            act.copy(pb[:, (g - 4) * BANK:(g - 3) * BANK], src[:]).then_inc(proj_read, 1)
                        if g == 1:
                            act.wait_ge(arg_ready, t + 1)
                            act.activation(zt[:], zt[:], ACT.Exp, scale=-1.0).then_inc(e_ready, 1)
                        if g == 2:
                            act.wait_ge(var_in, t + 1)
                            step.then(act.activation(zt[:, 0:CW], z[:, CW:2 * CW], ACT.Square, accum_out=st[:, 5:6]))
                            step.then(act.activation(st[:, 6:7], st[:, 5:6], ACT.Ln, scale=1.0 / CW, bias=keep["eps"][:, 1:2]))
                            act.activation(st[:, 7:8], st[:, 6:7], ACT.Exp, scale=-0.5).then_inc(v_rstd, 1)
                step.restart()

        @block.vector
        def _(dve):
            step = Steps(dve, dve_step)
            for s in (h_ready, x_read, z_read):
                dve.sem_inc(s, 1)
            dve.sem_inc(hT_ready, 2)
            dve.wait_ge(consts_in, 16 * 6)
            dve.wait_ge(wsT_mm, 1)
            dve.tensor_tensor(w_sT[:], ps_t[0][:].rearrange("p (g n) -> p g n", g=CG),
                              upper[:].unsqueeze(1).to_broadcast([P, CG, P]), ALU.mult).then_inc(wsT_done, 1)
            with dve.Fori(0, NT // 2) as i:
                for j in range(2):
                    t = i * 2 + j
                    dve.wait_ge(rstd_ready, t + 1)
                    dve.scalar_tensor_tensor(h[:], x[:], st[:, 2:3], scale[:], ALU.mult, ALU.mult).then_inc(x_read, 1)
                    dve.wait_ge(x_read, t + 2)
                    dve.tensor_tensor(h[:], h[:], shift[:], ALU.add).then_inc(h_ready, 1)
                    for half in range(2):
                        dve.wait_ge(tr_done, t + 2)
                        dve.tensor_copy(hT[j][:, 4 * half:4 * half + 4, :], ps_t[half][:].rearrange("p (k n) -> p k n", k=4)).then_inc(hT_ready, 1)
                    dve.wait_ge(proj_read, i * (2 * GROUPS) + j * GROUPS + 1 + 4)
                    step.then(dve.tensor_tensor(zt[:], z[:], z[:], ALU.mult))
                    step.then(dve.tensor_scalar(zt[:], zt[:], GELU_3, GELU_1, ALU.mult, ALU.add))
                    step.then(dve.tensor_tensor(zt[:], zt[:], z[:], ALU.mult))
                    dve.tensor_scalar(zt[:], zt[:], -80.0, None, ALU.max).then_inc(arg_ready, 1)
                    dve.wait_ge(e_ready, t + 1)
                    step.then(dve.tensor_scalar(zt[:], zt[:], 1.0, None, ALU.add))
                    step.then(dve.reciprocal(zt[:], zt[:]))
                    step.then(dve.tensor_tensor(z[:], z[:], zt[:], ALU.mult))
                    v = z[:, CW:2 * CW]
                    step.then(dve.tensor_reduce(st[:, 3:4], v, AX.X, ALU.add))
                    step.then(dve.tensor_scalar(st[:, 4:5], st[:, 3:4], -1.0 / CW, None, ALU.mult))
                    dve.tensor_scalar(v, v, st[:, 4:5], None, ALU.add).then_inc(var_in, 1)
                    dve.wait_ge(v_rstd, t + 1)
                    step.then(dve.scalar_tensor_tensor(v, v, st[:, 7:8], ln_g[:], ALU.mult, ALU.mult))
                    dve.tensor_tensor(v, v, ln_b[:], ALU.add).then_inc(v_ready, 1)
                    dve.wait_ge(sv_mm, t + 1)
                    dve.wait_ge(yc_free, t + 1)
                    for g in range(CG):
                        c = slice(g * CD, (g + 1) * CD)
                        step.then(dve.scalar_tensor_tensor(yc[:, c], ps_s[:, c], b_s[:, g:g + 1], z[:, c], ALU.add, ALU.mult))
                    dve.sem_inc(z_read, 1)
                    dve.sem_inc(yc_ready, 1)
                step.restart()

        @block.tensor
        def _(pe):
            for s in (tr_done,):
                pe.sem_inc(s, 1)
            pe.wait_ge(consts_in, 16 * 6)
            for g in range(CG):
                mm = pe.transpose(ps_t[0][:, g * P:(g + 1) * P], w_s[:, g, :], ident[:])
            mm.then_inc(wsT_mm, 1)
            pe.wait_ge(wsT_done, 1)
            pe.wait_ge(w_loaded, 16 * KC)
            cols = [A_COLS + B_COLS, 0, AW, 2 * AW, A_COLS, A_COLS + BANK]
            with pe.Fori(0, NT // 2) as i:
                for j in range(2):
                    t = i * 2 + j
                    pe.wait_ge(h_ready, t + 2)
                    if True:
                        pe.wait_ge(hT_ready, t * 2 + 2)
                    for k in range(KC):
                        tr = pe.transpose(ps_t[k // 4][:, (k % 4) * P:(k % 4 + 1) * P], h[:, k * P:(k + 1) * P], ident[:])
                    tr.then_inc(tr_done, 1)
                    pe.wait_ge(hT_ready, t * 2 + 4)
                    for g in range(GROUPS):
                        out = ps_p[(j * GROUPS + g) % 4]
                        pe.wait_ge(proj_read, i * (2 * GROUPS) + j * GROUPS + g + 1)
                        if g in (1, 2):
                            for c in range(AH):
                                for k in range(KC):
                                    mm = pe.matmul(out[:, c * P:(c + 1) * P], w[:, k, cols[g] + c * P:cols[g] + (c + 1) * P], hT[j][:, k, :],
                                                   start=(k == 0), stop=(k == KC - 1))
                        else:
                            for k in range(KC):
                                mm = pe.matmul(out[:], hT[j][:, k, :], w[:, k, cols[g]:cols[g] + BANK], start=(k == 0), stop=(k == KC - 1))
                        mm.then_inc(proj_mm, 1)
                    pe.wait_ge(v_ready, t + 1)
                    pe.wait_ge(z_read, t + 1)
                    for g in range(CG):
                        mm = pe.matmul(ps_s[:, g * CD:(g + 1) * CD], w_sT[:, g, :], z[:, CW + g * CD:CW + (g + 1) * CD], start=True, stop=True)
                    mm.then_inc(sv_mm, 1)


LAMBDA_INIT = 0.8 - 0.6 * math.exp(-0.3 * 0)
N_BUCKETS, MAX_DISTANCE = 32, 128
NEG = -1e30


def load_exp_and_ln(nc, act):
    act.add_instruction(mybir.InstLoadActFuncSet(act_func_set_id=EXP_AND_LN, name=nc.get_next_instruction_name(),
                                                 engine=mybir.EngineType.Activation))


class Stages:

    def __init__(self, sem, names):
        self.sem, self.names, self.n = sem, names, len(names)
        self.built = 0

    def start(self, eng):
        eng.sem_inc(self.sem, self.n)

    def done(self, ins, name):
        assert self.names[self.built % self.n] == name, (name, self.names[self.built % self.n])
        self.built += 1
        return ins.then_inc(self.sem, 1)

    def wait(self, eng, turn, name):
        eng.wait_ge(self.sem, turn * self.n + self.n + self.names.index(name) + 1)

    def wait_before(self, eng, turn, name):
        eng.wait_ge(self.sem, turn * self.n + self.names.index(name) + 1)


def attend(nc, io, dr, keep):
    with ExitStack() as ctx:
        sb = lambda n, s: ctx.enter_context(nc.sbuf_tensor(n, s, F32))
        sem = lambda n: ctx.enter_context(nc.semaphore(n))
        pt = lambda n, b=1: ctx.enter_context(nc.psum_tensor(n, [P, b * BANK], F32))
        ident = keep["ident"]
        table, oh = sb("table", [N_BUCKETS + 1, AH]), sb("onehot", [N_BUCKETS + 1, 3 * P])
        rv = sb("bias_rows", [P, AH, 3 * P])
        table_b = sb("table_b", [N_BUCKETS + 1, AH, P])
        bias = sb("bias", [P, AH, 2 * P])
        lp, lam = sb("lambda_par", [P, 4, AQK]), sb("lambda", [P, 4])
        gain = sb("subln", [P, 2 * AQK])
        q, k, v = sb("q_head", [P, S]), sb("k_head", [P, S]), sb("v_head", [P, NT, P])
        p = [[sb(f"p{b}{m}", [P, S]) for m in range(2)] for b in range(2)]
        attn = [sb(f"attn{b}", [P, S]) for b in range(2)]
        aT = [sb(f"attnT{b}", [P, NT, P]) for b in range(2)]
        o = [sb(f"o{b}", [P, P]) for b in range(2)]
        junk = sb("squares", [P, P])
        st = [sb(f"soft_stats{b}", [P, 12]) for b in range(3)]
        ps_s = [pt(f"ps_scores{m}", 2) for m in range(2)]
        ps_t = [pt(f"ps_attnT{b}") for b in range(2)]
        ps_o = [pt(f"ps_o{b}") for b in range(2)]
        consts_in, table_done, rv_mm, rv_ready, rv_out, bias_in = (sem(n) for n in (
            "att_consts_in", "table_done", "rv_mm", "rv_ready", "rv_out", "bias_in"))
        lam_dot, lam_exp, gain_done, dve_step, act_step, o_out = (sem(n) for n in (
            "lam_dot", "lam_exp", "gain_done", "att_dve_step", "att_act_step", "o_out"))
        heads_in = sem("head_copied")
        s_mm = sem("scores_mm")
        s_max = sem("scores_max")
        s_exp = sem("scores_exp")
        a_ready = sem("attn_ready")
        t_mm = sem("attnT_mm")
        t_read = sem("attnT_copied")
        o_mm = sem("o_mm")
        o_rstd = sem("o_rstd")
        o_free = sem("o_free")
        o_ready = sem("o_ready")
        halves = lambda n: [(a, min(a + 4, n + 1)) for a in range(0, n + 1, 4)]
        T_HEAD = sum(len(halves(n)) for n in range(NT))
        t_before = lambda n: sum(len(halves(m)) for m in range(n))
        block = ctx.enter_context(nc.Block())

        @block.sync
        def _(sp):
            sp.dma_start(table[0:N_BUCKETS, :], io["rel_bias_table"]).then_inc(consts_in, 16)
            sp.dma_start(oh[:], io["c_onehot"]).then_inc(consts_in, 16)
            sp.dma_start(lp[:], io["diff_lambda"].rearrange("l a b -> l (a b)").partition_broadcast(P)).then_inc(consts_in, 16)
            sp.dma_start(gain[:], io["diff_subln"][0:1, :].partition_broadcast(P)).then_inc(consts_in, 16)
            sp.wait_ge(rv_ready, 1)
            sp.dma_start(dr["bias_by_dist"].rearrange("h p n -> p h n"), rv[:]).then_inc(rv_out, 16)
            sp.wait_ge(rv_out, 16)
            t = dr["bias_by_dist"]
            for h in range(AH):
                src = bass.AP(t.tensor, h * P * 3 * P + P - 1, [[3 * P - 1, P], [1, 2 * P]])
                sp.dma_start(bias[:, h, :], src).then_inc(bias_in, 16)
            sp.sem_inc(o_free, 2)
            with sp.Fori(0, AH) as h:
                for n in range(NT):
                    sp.wait_ge(o_ready, h * NT + n + 1)
                    sp.dma_start(dr["ymix"][n * P:(n + 1) * P, bass.ds(h * P, P)], o[n % 2][:]).then_inc(o_out, 16)
                    sp.wait_ge(o_out, (h * NT + n) * 16 + 16)
                    sp.sem_inc(o_free, 1)

        @block.scalar
        def _(act):
            load_exp_and_ln(nc, act)
            step = Steps(act, act_step)
            act.sem_inc(t_read, 2)
            act.sem_inc(s_exp, 2)
            act.wait_ge(lam_dot, 1)
            act.activation(lam[:, 2:4], lam[:, 0:2], ACT.Exp).then_inc(lam_exp, 1)
            with act.Fori(0, AH) as h:
                act.wait_ge(o_mm, h * NT + 1)
                act.mul(q[:], keep["qT"][:, bass.ds(h, 1), :].squeeze(1), AQK ** -0.5).then_inc(heads_in, 1)
                act.copy(k[:], keep["kT"][:, bass.ds(h, 1), :].squeeze(1)).then_inc(heads_in, 1)
                act.copy(v[:], keep["v"][:, :, bass.ds(h * P, P)]).then_inc(heads_in, 1)
                for it in range(NT + 2):
                    if it < NT:
                        n, b, L = it, it % 2, (it + 1) * P
                        if n >= 2:
                            act.wait_ge(a_ready, h * NT + n - 1)
                        for m in range(2):
                            act.wait_ge(s_max, h * (2 * NT) + 2 * n + m + 1)
                            act.activation(p[b][m][:, 0:L], ps_s[m][:, 0:L], ACT.Exp, bias=st[n % 3][:, m:m + 1],
                                           accum_out=st[n % 3][:, 2 + m:3 + m]).then_inc(s_exp, 1)
                    if 1 <= it <= NT:
                        n = it - 1
                        if n >= 2:
                            act.wait_ge(o_mm, h * NT + n - 1 + 1)
                        for x, (a, z) in enumerate(halves(n)):
                            c = t_before(n) + x
                            act.wait_ge(t_mm, h * T_HEAD + c + 1)
                            act.copy(aT[n % 2][:, a:z, :], ps_t[c % 2][:, 0:(z - a) * P].rearrange("p (a n) -> p a n", n=P)).then_inc(t_read, 1)
                    if it >= 2:
                        n = it - 2
                        s = st[n % 3]
                        act.wait_ge(o_mm, h * NT + n + 1 + 1)
                        step.then(act.activation(junk[:], ps_o[n % 2][:, 0:P], ACT.Square, accum_out=s[:, 8:9]))
                        step.then(act.activation(s[:, 9:10], s[:, 8:9], ACT.Ln, scale=1.0 / P, bias=keep["eps"][:, 0:1]))
                        act.activation(s[:, 10:11], s[:, 9:10], ACT.Exp, scale=-0.5).then_inc(o_rstd, 1)
                step.restart()

        @block.vector
        def _(dve):
            step = Steps(dve, dve_step)
            dve.memset(table[N_BUCKETS:N_BUCKETS + 1, :], NEG).then_inc(table_done, 1)
            dve.wait_ge(consts_in, 64)
            dve.wait_ge(table_done, 1)
            dve.tensor_copy(table_b[:], table[:].unsqueeze(2).to_broadcast([N_BUCKETS + 1, AH, P])).then_inc(table_done, 1)
            step.then(dve.tensor_tensor(lp[:, 0, :], lp[:, 0, :], lp[:, 1, :], ALU.mult))
            step.then(dve.tensor_tensor(lp[:, 2, :], lp[:, 2, :], lp[:, 3, :], ALU.mult))
            step.then(dve.tensor_reduce(lam[:, 0:1], lp[:, 0, :], AX.X, ALU.add))
            dve.tensor_reduce(lam[:, 1:2], lp[:, 2, :], AX.X, ALU.add).then_inc(lam_dot, 1)
            dve.wait_ge(lam_exp, 1)
            step.then(dve.tensor_tensor(lam[:, 0:1], lam[:, 3:4], lam[:, 2:3], ALU.subtract))
            step.then(dve.tensor_scalar(lam[:, 0:1], lam[:, 0:1], -LAMBDA_INIT, None, ALU.add))
            step.then(dve.tensor_scalar(gain[:], gain[:], 1.0 - LAMBDA_INIT, None, ALU.mult))
            dve.wait_ge(rv_mm, 1)
            rv_ps = [ps_s[0][:, 0:BANK], ps_s[0][:, BANK:], ps_s[1][:, 0:BANK], ps_s[1][:, BANK:]]
            for h in range(AH):
                q = dve.tensor_copy(rv[:, h, :], rv_ps[h][:, 0:3 * P])
            step.then(q)
            for h in range(AH):
                q = dve.tensor_scalar(rv[:, h, 1:], rv[:, h, 1:], rv[:, h, 0:1], None, ALU.subtract)
            step.then(q)
            dve.memset(rv[:, :, 0:1], 0.0).then_inc(rv_ready, 1)
            dve.wait_ge(bias_in, 16 * AH)
            step.restart()
            with dve.Fori(0, AH) as h:
                for it in range(NT + 2):
                    if it < NT:
                        n, s, L = it, st[it % 3], (it + 1) * P
                        w = min(L, 2 * P)
                        if n >= 3:
                            dve.wait_ge(o_ready, h * NT + n - 2)
                        for m in range(2):
                            dve.wait_ge(s_mm, h * (2 * NT) + 2 * n + m + 1)
                            near = ps_s[m][:, L - w:L]
                            step.then(dve.tensor_tensor(near, near, bias[:, bass.ds(h, 1), 2 * P - w:2 * P].squeeze(1), ALU.add))
                            dve.tensor_reduce(s[:, m:m + 1], ps_s[m][:, 0:L], AX.X, ALU.max, negate=True).then_inc(s_max, 1)
                    if 1 <= it <= NT:
                        n, b, s, L = it - 1, (it - 1) % 2, st[(it - 1) % 3], it * P
                        dve.wait_ge(s_exp, h * (2 * NT) + 2 * n + 2 + 2)
                        if n >= 2:
                            dve.wait_ge(t_mm, h * T_HEAD + t_before(n - 1))
                        step.then(dve.reciprocal(s[:, 4:6], s[:, 2:4]))
                        step.then(dve.tensor_tensor(s[:, 6:7], s[:, 5:6], lam[:, 0:1], ALU.mult))
                        step.then(dve.tensor_scalar(attn[b][:, 0:L], p[b][0][:, 0:L], s[:, 4:5], None, ALU.mult))
                        dve.scalar_tensor_tensor(attn[b][:, 0:L], p[b][1][:, 0:L], s[:, 6:7], attn[b][:, 0:L], ALU.mult, ALU.add).then_inc(a_ready, 1)
                    if it >= 2:
                        n = it - 2
                        dve.wait_ge(o_rstd, h * NT + n + 1)
                        dve.wait_ge(o_free, h * NT + n + 1)
                        dve.scalar_tensor_tensor(o[n % 2][:], ps_o[n % 2][:, 0:P], st[n % 3][:, 10:11], gain[:], ALU.mult, ALU.mult).then_inc(o_ready, 1)
                step.restart()

        @block.tensor
        def _(pe):
            pe.sem_inc(o_mm, 1)
            pe.wait_ge(consts_in, 64)
            pe.wait_ge(table_done, 2)
            for h in range(AH):
                mm = pe.matmul(ps_s[h // 2][:, (h % 2) * BANK:(h % 2) * BANK + 3 * P], table_b[:, h, :], oh[:], start=True, stop=True)
            mm.then_inc(rv_mm, 1)
            pe.wait_ge(rv_ready, 1)
            with pe.Fori(0, AH) as h:
                pe.wait_ge(heads_in, h * 3 + 3)
                for it in range(NT + 1):
                    if it < NT:
                        n, L = it, (it + 1) * P
                        for m in range(2):
                            pe.wait_ge(s_exp, h * (2 * NT) + 2 * n + m - 2 + 1 + 2)
                            r = slice(m * AQK, (m + 1) * AQK)
                            for a in range(0, L, BANK):
                                z = min(a + BANK, L)
                                mm = pe.matmul(ps_s[m][:, a:z], q[r, n * P:(n + 1) * P], k[r, a:z], start=True, stop=True)
                            mm.then_inc(s_mm, 1)
                    if it >= 1:
                        n = it - 1
                        pe.wait_ge(a_ready, h * NT + n + 1)
                        for x, (a, z) in enumerate(halves(n)):
                            c = t_before(n) + x
                            pe.wait_ge(t_read, h * T_HEAD + c + 1)
                            for kt in range(a, z):
                                tr = pe.transpose(ps_t[c % 2][:, (kt - a) * P:(kt - a + 1) * P], attn[n % 2][:, kt * P:(kt + 1) * P], ident[:])
                            tr.then_inc(t_mm, 1)
                        if n >= 2:
                            pe.wait_ge(o_ready, h * NT + n - 1)
                        for x, (a, z) in enumerate(halves(n)):
                            pe.wait_ge(t_read, h * T_HEAD + t_before(n) + x + 1 + 2)
                            for kt in range(a, z):
                                mm = pe.matmul(ps_o[n % 2][:, 0:P], aT[n % 2][:, kt, :], v[:, kt, :], start=(kt == 0), stop=(kt == n))
                        mm.then_inc(o_mm, 1)


def rwkv(nc, io, dr, keep):
    HALF = math.exp(-0.5)
    with ExitStack() as ctx:
        sb = lambda n, s: ctx.enter_context(nc.sbuf_tensor(n, s, F32))
        sem = lambda n: ctx.enter_context(nc.semaphore(n))
        bank = [ctx.enter_context(nc.psum_tensor(f"bank{n}", [P, BANK], F32)) for n in range(8)]
        ident = keep["ident"]
        H4 = [P, BH, P]
        mu = sb("mu", [P, B_COLS])
        wa0 = sb("w0_a0", [P, 2 * BW])
        k_k, k_a, r_k, lnx_g, lnx_b = (sb(n, [P, BW]) for n in ("k_k", "k_a", "r_k", "lnx_g", "lnx_b"))
        wa2, g2 = sb("w2_a2", [P, BW]), sb("g2", [P, BW])
        mask4 = sb("mask4", [P, 4, P])
        masks = sb("masks", [P, 9, P])
        cum_m, halves_m = sb("cum_m", [P, P]), sb("halves_m", [P, 2])
        cur, prev, p = sb("pb_cur", [P, B_COLS]), sb("pb_prev", [P, B_COLS]), sb("p_mixed", [P, B_COLS])
        lr, lrT = sb("low_rank", [P, 2 * P]), sb("low_rankT", [P, 2 * P])
        wa, g, lw, cx = sb("w_a", [P, 2 * BW]), sb("gate", [P, BW]), sb("log_decay", [P, BW]), sb("cum_before", [P, BW])
        kk, k2, tmp = sb("kk", [P, BW]), sb("k2", [P, BW]), sb("tmp", [P, BW])
        s4 = sb("per_head", [P, 8, BH])
        dec = sb("decays", [P, 3, BW])
        fs = sb("state_factors", [P, 4])
        ops = sb("operands", [P, 4, BW])
        arT, bkT = sb("arT", [P, 2, 2, P]), sb("bkT", [P, 2, 2, P])
        gm = sb("grams", [P, BH, 4, P])
        A = sb("A_ab", H4)
        Dm, DT, T, TT, Z, ZT = (sb(n, H4) for n in ("pow", "powT", "T", "TT", "Z", "ZT"))
        O, OT = [sb(f"off{n}", H4) for n in range(3)], [sb(f"offT{n}", H4) for n in range(2)]
        Xs, Us, taT = sb("X", [P, BW]), sb("U", [P, BW]), sb("taT", [P, 2, P])
        St, Sc = sb("state", [P, 2, BD]), sb("state_mid", [P, 2, BD])
        ys, yq, yo = sb("y", [P, BW]), sb("y_sq", [P, BW]), sb("y_out", [P, BW])
        zero = sb("zero_row", [1, B_COLS])
        consts_in, zero_done, zero_out, load_in, pool_done, y_out, y_free = (sem(n) for n in (
            "rwkv_consts_in", "zero_done", "zero_out", "pb_in", "offs_done", "y_out", "y_free"))
        dve_step, act_step = sem("rwkv_dve_step"), sem("rwkv_act_step")
        PE = Stages(sem("pe_done"), ["lr_T", "lora", "cum", "operands_T", "grams", "X", "sq0", "sq1", "sq2", "sq3",
                                     "z0", "m0", "z1", "m1", "z2", "m2", "ta", "U", "Y", "state"])
        V = Stages(sem("dve_done"), ["mixed", "lr_args", "lr", "wa", "logw", "kk_ss", "cx", "operands", "masked", "D0",
                                     "v0", "v1", "v2", "v3", "vz0", "vm0", "vz1", "vm1", "vz2", "vm2", "Sc", "U", "state", "var", "y"])
        C = Stages(sem("act_done"), ["lr_exp", "lrT", "g", "wa_exp", "kk_rstd", "decays", "opsT", "X", "c0", "c1", "c2",
                                     "cz0", "cz1", "ta", "y", "rstd"])
        h3 = lambda x: x.rearrange("p (h d) -> p h d", h=BH)
        hc = lambda h: slice(h * BD, (h + 1) * BD)
        half = lambda h: slice(64 * (h % 2), 64 * (h % 2) + 64)
        bc = lambda col: col.unsqueeze(2).to_broadcast([P, BH, BD])
        mb = lambda n: masks[:, n, :].unsqueeze(1).to_broadcast(H4)
        ib = ident[:].unsqueeze(1).to_broadcast(H4)
        b4 = lambda n: bank[n][:].rearrange("p (h n) -> p h n", h=BH)
        by_parity = lambda x, e: x[:].rearrange("p (a e d) -> p e a d", e=2, d=BD)[:, e]
        bank_pair = lambda n: bank[n][:, 0:2 * BD].rearrange("p (a d) -> p a d", d=BD)
        r_, k_, v_ = p[:, 0:BW], p[:, BW:2 * BW], p[:, 2 * BW:3 * BW]
        pr = lambda n, a: io[n][0:1, :].partition_broadcast(P)
        block = ctx.enter_context(nc.Block())

        @block.sync
        def _(sp):
            for dst, src in ((mu[:], pr("rwkv_mu", 0)), (wa0[:, 0:BW], pr("rwkv_w0", 0)), (wa0[:, BW:], pr("rwkv_a0", 0)),
                             (k_k[:], pr("rwkv_k_k", 0)), (k_a[:], pr("rwkv_k_a", 0)),
                             (r_k[:], io["rwkv_r_k"].rearrange("l a b -> l (a b)").partition_broadcast(P)),
                             (lnx_g[:], pr("rwkv_lnx_g", 0)), (lnx_b[:], pr("rwkv_lnx_b", 0)),
                             (wa2[0:64, :], io["rwkv_w2"][0]), (wa2[64:128, :], io["rwkv_a2"][0]), (g2[:], io["rwkv_g2"][0]),
                             (mask4[:], io["c_mask4"]), (masks[:], io["c_masks"]), (cum_m[:], io["c_cum"]), (halves_m[:], io["c_halves"])):
                sp.dma_start(dst, src).then_inc(consts_in, 16)
            sp.wait_ge(zero_done, 1)
            sp.dma_start(dr["pb"][0:1, :], zero[:]).then_inc(zero_out, 16)
            sp.wait_ge(zero_out, 16)
            with sp.Fori(0, NT) as t:
                V.wait_before(sp, t, "mixed")
                sp.dma_start(cur[:], dr["pb"][bass.ds(t * P + 1, P), :]).then_inc(load_in, 16)
                sp.dma_start(prev[:], dr["pb"][bass.ds(t * P, P), :]).then_inc(load_in, 16)
            sp.wait_ge(load_in, 32 * NT)

        @block.gpsimd
        def _(pool):
            pool.sem_inc(y_free, 1)
            pool.wait_ge(consts_in, 16 * 15)
            with pool.Fori(0, NT) as t:
                V.wait(pool, t, "masked")
                PE.wait_before(pool, t, "m2")
                for n in range(3):
                    pool.tensor_tensor(O[n][:], A[:], mb(3 + 2 * n), ALU.mult).then_inc(pool_done, 1)
                    if n < 2:
                        pool.tensor_tensor(OT[n][:], gm[:, :, 0, :], mb(4 + 2 * n), ALU.mult).then_inc(pool_done, 1)
                V.wait(pool, t, "y")
                pool.dma_start(dr["ymix"][bass.ds(t * P, P), AW:AW + BW], yo[:]).then_inc(y_out, 16)
                pool.wait_ge(y_out, t * 16 + 16)
                pool.sem_inc(y_free, 1)

        @block.scalar
        def _(act):
            load_exp_and_ln(nc, act)
            step = Steps(act, act_step)
            C.start(act)
            with act.Fori(0, NT) as t:
                V.wait(act, t, "lr_args")
                C.done(act.activation(lr[:], lr[:], ACT.Exp, scale=-1.0), "lr_exp")
                PE.wait(act, t, "lr_T")
                C.done(act.copy(lrT[:], bank[0][:, 0:2 * P]), "lrT")
                PE.wait(act, t, "lora")
                V.wait_before(act, t, "y")
                C.done(act.copy(g[:], bank[3][:, 0:BW]), "g")
                V.wait(act, t, "wa")
                C.done(act.activation(wa[:], wa[:], ACT.Exp, scale=-1.0), "wa_exp")
                V.wait(act, t, "kk_ss")
                step.then(act.activation(s4[:, 1, :], s4[:, 0, :], ACT.Ln))
                C.done(act.activation(s4[:, 2, :], s4[:, 1, :], ACT.Exp, scale=-0.5), "kk_rstd")
                V.wait(act, t, "cx")
                PE.wait(act, t, "cum")
                act.activation(dec[:, 0, :], bank[1][:, 0:BW], ACT.Exp)
                act.activation(dec[:, 1, :], bank[1][:, 0:BW], ACT.Exp, scale=-1.0)
                act.activation(dec[:, 2, :], cx[:], ACT.Exp)
                C.done(act.activation(fs[:], bank[2][:, 0:4], ACT.Exp), "decays")
                PE.wait(act, t, "operands_T")
                act.copy(arT[:], bank[4][:].rearrange("p (a b n) -> p a b n", a=2, b=2))
                C.done(act.copy(bkT[:], bank[5][:].rearrange("p (a b n) -> p a b n", a=2, b=2)), "opsT")
                PE.wait(act, t, "X")
                C.done(act.copy(Xs[:], bank[4][:, 0:BW]), "X")
                for n in range(3):
                    PE.wait(act, t, f"sq{n}")
                    C.done(act.copy(Dm[:], b4(0)), f"c{n}")
                for n in range(2):
                    PE.wait(act, t, f"z{n}")
                    C.done(act.copy(Z[:], b4(0)), f"cz{n}")
                PE.wait(act, t, "ta")
                C.done(act.copy(taT[:], bank[4][:, 0:2 * P].rearrange("p (a n) -> p a n", a=2)), "ta")
                PE.wait(act, t, "Y")
                step.then(act.copy(by_parity(ys, 0), bank_pair(7)))
                C.done(act.copy(by_parity(ys, 1), bank_pair(1)), "y")
                V.wait(act, t, "var")
                step.then(act.activation(s4[:, 6, :], s4[:, 5, :], ACT.Ln, scale=1.0 / BD, bias=keep["eps"][:, 2:3]))
                C.done(act.activation(s4[:, 7, :], s4[:, 6, :], ACT.Exp, scale=-0.5), "rstd")
                step.restart()

        @block.vector
        def _(dve):
            step = Steps(dve, dve_step)
            tt = dve.tensor_tensor
            V.start(dve)
            dve.memset(zero[:], 0.0).then_inc(zero_done, 1)
            step.then(dve.memset(St[:], 0.0))
            dve.wait_ge(consts_in, 16 * 15)
            step.restart()
            with dve.Fori(0, NT) as t:
                dve.wait_ge(load_in, t * 32 + 32)
                step.then(tt(prev[:], prev[:], cur[:], ALU.subtract))
                step.then(tt(prev[:], prev[:], mu[:], ALU.mult))
                PE.wait_before(dve, t, "state")
                V.done(tt(p[:], prev[:], cur[:], ALU.add), "mixed")
                V.wait(dve, t, "mixed")
                PE.wait_before(dve, t, "lr_T")
                step.then(dve.tensor_scalar(lr[:, 0:64], p[:, 3 * BW:3 * BW + 64], 2.0, -80.0, ALU.mult, ALU.max))
                step.then(dve.tensor_scalar(lr[:, 64:128], p[:, 3 * BW + 64:3 * BW + 128], 0.0, None, ALU.mult))
                V.done(dve.tensor_scalar(lr[:, 128:256], p[:, 3 * BW + 128:], -80.0, None, ALU.max), "lr_args")
                C.wait(dve, t, "lr_exp")
                step.then(dve.tensor_scalar(lr[:], lr[:], 1.0, None, ALU.add))
                step.then(dve.reciprocal(lr[:], lr[:]))
                step.then(dve.tensor_scalar(lr[:, 0:64], lr[:, 0:64], 2.0, -1.0, ALU.mult, ALU.add))
                V.done(dve.tensor_copy(lr[:, 64:128], p[:, 3 * BW + 64:3 * BW + 128]), "lr")
                PE.wait(dve, t, "lora")
                step.then(tt(wa[:, 0:BW], bank[1][:, 0:BW], wa0[:, 0:BW], ALU.add))
                step.then(tt(wa[:, BW:], bank[2][:, 0:BW], wa0[:, BW:], ALU.add))
                V.done(dve.tensor_scalar(wa[:], wa[:], -80.0, None, ALU.max), "wa")
                C.wait(dve, t, "wa_exp")
                step.then(dve.tensor_scalar(wa[:], wa[:], 1.0, None, ALU.add))
                step.then(dve.reciprocal(wa[:], wa[:]))
                a_ = wa[:, BW:]
                V.done(dve.tensor_scalar(lw[:], wa[:, 0:BW], -HALF, None, ALU.mult), "logw")
                step.then(tt(kk[:], k_, k_k[:], ALU.mult))
                step.then(tt(tmp[:], kk[:], kk[:], ALU.mult))
                step.then(dve.tensor_reduce(s4[:, 3, :], h3(tmp[:]), AX.X, ALU.add))
                V.done(dve.tensor_scalar(s4[:, 0, :], s4[:, 3, :], 1e-24, None, ALU.max), "kk_ss")
                step.then(dve.scalar_tensor_tensor(k2[:], a_, -1.0, k_a[:], ALU.add, ALU.mult))
                step.then(dve.scalar_tensor_tensor(k2[:], k2[:], 1.0, k_, ALU.add, ALU.mult))
                step.then(tt(tmp[:], r_, k2[:], ALU.mult))
                step.then(tt(tmp[:], tmp[:], r_k[:], ALU.mult))
                step.then(dve.tensor_reduce(s4[:, 4, :], h3(tmp[:]), AX.X, ALU.add))
                PE.wait(dve, t, "cum")
                V.done(tt(cx[:], bank[1][:, 0:BW], lw[:], ALU.subtract), "cx")
                C.wait(dve, t, "kk_rstd")
                step.then(tt(h3(kk[:]), h3(kk[:]), bc(s4[:, 2, :]), ALU.mult))
                C.wait(dve, t, "decays")
                step.then(dve.scalar_tensor_tensor(ops[:, 0, :], kk[:], -1.0, dec[:, 2, :], ALU.mult, ALU.mult))
                step.then(tt(ops[:, 1, :], r_, dec[:, 0, :], ALU.mult))
                step.then(tt(tmp[:], kk[:], a_, ALU.mult))
                step.then(tt(ops[:, 2, :], tmp[:], dec[:, 1, :], ALU.mult))
                V.done(tt(ops[:, 3, :], k2[:], dec[:, 1, :], ALU.mult), "operands")
                PE.wait(dve, t, "grams")
                dve.wait_ge(pool_done, t * 5 + 5)
                for h in range(BH):
                    step.then(tt(gm[:, h, :, :], b4(h), mask4[:], ALU.mult))
                ho = lambda x, e: x.rearrange("p (a e) n -> p e a n", e=2)[:, e]
                ml = masks[:, 0, :].unsqueeze(1).to_broadcast([P, 2, P])
                for e in range(2):
                    q = tt(ho(A[:], e), bank[6 + e][:, 0:2 * P].rearrange("p (a n) -> p a n", a=2), ml, ALU.mult)
                    if e == 0:
                        step.then(q)
                V.done(q, "masked")
                V.wait(dve, t, "masked")
                step.then(tt(Dm[:], A[:], mb(1), ALU.mult))
                step.then(tt(DT[:], gm[:, :, 0, :], mb(2), ALU.mult))
                step.then(tt(T[:], Dm[:], ib, ALU.add))
                V.done(tt(TT[:], DT[:], ib, ALU.add), "D0")
                for n in range(4):
                    PE.wait(dve, t, f"sq{n}")
                    if n > 0:
                        step.then(tt(T[:], T[:], b4(1), ALU.add))
                        q = tt(TT[:], TT[:], b4(3), ALU.add)
                    if n < 3:
                        if n > 0:
                            step.then(q)
                        q = dve.tensor_copy(DT[:], b4(2))
                    V.done(q, f"v{n}")
                for n in range(3):
                    PE.wait(dve, t, f"z{n}")
                    V.done(dve.tensor_copy(ZT[:], b4(2)), f"vz{n}")
                    PE.wait(dve, t, f"m{n}")
                    if n < 2:
                        step.then(tt(T[:], T[:], b4(1), ALU.add))
                    V.done(tt(TT[:], TT[:], b4(3), ALU.add), f"vm{n}")
                f = lambda n: fs[:].rearrange("p (a b) -> p b a", b=2)[:, n].unsqueeze(2).to_broadcast([P, 2, BD])
                V.done(tt(Sc[:], St[:], f(0), ALU.mult), "Sc")
                PE.wait(dve, t, "U")
                step.then(dve.tensor_copy(by_parity(Us, 0), bank_pair(6)))
                V.done(dve.tensor_copy(by_parity(Us, 1), bank_pair(0)), "U")
                PE.wait(dve, t, "state")
                step.then(tt(Sc[:], Sc[:], bank[5][:, 0:2 * BD].rearrange("p (a d) -> p a d", a=2), ALU.add))
                V.done(tt(St[:], Sc[:], f(1), ALU.mult), "state")
                C.wait(dve, t, "y")
                step.then(dve.tensor_reduce(s4[:, 3, :], h3(ys[:]), AX.X, ALU.add))
                step.then(dve.tensor_scalar(s4[:, 3, :], s4[:, 3, :], -1.0 / BD, None, ALU.mult))
                step.then(tt(h3(ys[:]), h3(ys[:]), bc(s4[:, 3, :]), ALU.add))
                step.then(tt(yq[:], ys[:], ys[:], ALU.mult))
                V.done(dve.tensor_reduce(s4[:, 5, :], h3(yq[:]), AX.X, ALU.add), "var")
                step.then(tt(h3(tmp[:]), h3(v_), bc(s4[:, 4, :]), ALU.mult))
                C.wait(dve, t, "rstd")
                step.then(tt(h3(ys[:]), h3(ys[:]), bc(s4[:, 7, :]), ALU.mult))
                step.then(tt(ys[:], ys[:], lnx_g[:], ALU.mult))
                step.then(tt(ys[:], ys[:], lnx_b[:], ALU.add))
                step.then(tt(ys[:], ys[:], tmp[:], ALU.add))
                dve.wait_ge(y_free, t + 1)
                V.done(tt(yo[:], ys[:], g[:], ALU.mult), "y")
                V.wait(dve, t, "y")
                step.restart()

        @block.tensor
        def _(pe):
            PE.start(pe)
            pe.sem_inc(pool_done, 5)
            pe.wait_ge(consts_in, 16 * 15)
            mm = pe.matmul
            with pe.Fori(0, NT) as t:
                V.wait(pe, t, "lr")
                for n in range(2):
                    q = pe.transpose(bank[0][:, n * P:(n + 1) * P], lr[:, n * P:(n + 1) * P], ident[:])
                PE.done(q, "lr_T")
                C.wait(pe, t, "lrT")
                mm(bank[1][:, 0:BW], lrT[0:64, 0:P], wa2[0:64, :], start=True, stop=True)
                mm(bank[2][:, 0:BW], lrT[64:128, 0:P], wa2[64:128, :], start=True, stop=True)
                PE.done(mm(bank[3][:, 0:BW], lrT[:, P:2 * P], g2[:], start=True, stop=True), "lora")
                V.wait(pe, t, "logw")
                mm(bank[1][:, 0:BW], cum_m[:], lw[:], start=True, stop=True)
                for a in range(2):
                    q = mm(bank[2][:, 2 * a:2 * a + 2], lw[:, a * P:(a + 1) * P], halves_m[:], start=True, stop=True)
                PE.done(q, "cum")
                V.wait(pe, t, "operands")
                for a in range(2):
                    for x in range(2):
                        pe.transpose(bank[4][:, (2 * a + x) * P:(2 * a + x + 1) * P], ops[:, x, a * P:(a + 1) * P], ident[:])
                        q = pe.transpose(bank[5][:, (2 * a + x) * P:(2 * a + x + 1) * P], ops[:, 2 + x, a * P:(a + 1) * P], ident[:])
                PE.done(q, "operands_T")
                C.wait(pe, t, "opsT")
                for h in (0, 2, 1, 3):
                    r, a = half(h), h // 2
                    mm(bank[h][:, 0:2 * P], bkT[r, a, 0, :], arT[r, a, :, :], start=True, stop=True)
                    mm(bank[h][:, 2 * P:4 * P], bkT[r, a, 1, :], arT[r, a, :, :], start=True, stop=True)
                    q = mm(bank[6 + h % 2][:, a * P:(a + 1) * P], arT[r, a, 0, :], bkT[r, a, 0, :], start=True, stop=True)
                PE.done(q, "grams")
                V.wait(pe, t, "D0")
                for h in range(BH):
                    q = mm(bank[4][:, hc(h)], gm[:, h, 2, :], v_[:, hc(h)], start=True, stop=True)
                PE.done(q, "X")
                for n in range(4):
                    if n > 0:
                        V.wait(pe, t, f"v{n - 1}")
                        C.wait(pe, t, f"c{n - 1}")
                    for h in range(BH):
                        c = slice(h * P, (h + 1) * P)
                        if n < 3:
                            q = mm(bank[0][:, c], DT[:, h, :], Dm[:, h, :], start=True, stop=True)
                            q = mm(bank[2][:, c], Dm[:, h, :], DT[:, h, :], start=True, stop=True)
                        if n > 0:
                            q = mm(bank[1][:, c], DT[:, h, :], T[:, h, :], start=True, stop=True)
                            q = mm(bank[3][:, c], Dm[:, h, :], TT[:, h, :], start=True, stop=True)
                    PE.done(q, f"sq{n}")
                for n in range(3):
                    if n == 0:
                        pe.wait_ge(pool_done, t * 5 + 10)
                        V.wait(pe, t, "v3")
                    else:
                        V.wait(pe, t, f"vm{n - 1}")
                    for h in range(BH):
                        c = slice(h * P, (h + 1) * P)
                        if n < 2:
                            mm(bank[0][:, c], OT[n][:, h, :], T[:, h, :], start=True, stop=True)
                        q = mm(bank[2][:, c], O[n][:, h, :], TT[:, h, :], start=True, stop=True)
                    PE.done(q, f"z{n}")
                    V.wait(pe, t, f"vz{n}")
                    if n < 2:
                        C.wait(pe, t, f"cz{n}")
                    for h in range(BH):
                        c = slice(h * P, (h + 1) * P)
                        if n < 2:
                            mm(bank[1][:, c], TT[:, h, :], Z[:, h, :], start=True, stop=True)
                        q = mm(bank[3][:, c], T[:, h, :], ZT[:, h, :], start=True, stop=True)
                    PE.done(q, f"m{n}")
                V.wait(pe, t, "vm2")
                C.wait(pe, t, "X")
                for h in range(BH):
                    q = mm(bank[4][half(h), (h // 2) * P:(h // 2 + 1) * P], ops[:, 0, hc(h)], TT[:, h, :], start=True, stop=True)
                PE.done(q, "ta")
                C.wait(pe, t, "ta")
                V.wait(pe, t, "Sc")
                for h in range(BH):
                    o = bank[(6, 0)[h % 2]][:, hc(h // 2)]
                    mm(o, TT[:, h, :], Xs[:, hc(h)], start=True, stop=False)
                    q = mm(o, taT[half(h), h // 2, :], Sc[half(h), h // 2, :], start=False, stop=True)
                PE.done(q, "U")
                V.wait(pe, t, "U")
                for h in range(BH):
                    o = bank[(7, 1)[h % 2]][:, hc(h // 2)]
                    mm(o, gm[:, h, 3, :], v_[:, hc(h)], start=True, stop=False)
                    mm(o, gm[:, h, 1, :], Us[:, hc(h)], start=False, stop=False)
                    q = mm(o, arT[half(h), h // 2, 1, :], Sc[half(h), h // 2, :], start=False, stop=True)
                PE.done(q, "Y")
                for h in range(BH):
                    o = bank[5][half(h), (h // 2) * BD:(h // 2 + 1) * BD]
                    mm(o, ops[:, 3, hc(h)], v_[:, hc(h)], start=True, stop=False)
                    q = mm(o, ops[:, 2, hc(h)], Us[:, hc(h)], start=False, stop=True)
                PE.done(q, "state")


E, F, TOP_K, NG, TOPK_GROUPS = 64, 256, 8, 8, 4
EG = E // NG
FC = F // P
ROUTED_SCALE = 2.5
BLOCKS = E + (S * TOP_K - E) // P
NB = BLOCKS + 6
DROP = -3.0e38


def norm_route(nc, io, dr, keep):
    with ExitStack() as ctx:
        sb = lambda n, s: ctx.enter_context(nc.sbuf_tensor(n, s, F32))
        sem = lambda n: ctx.enter_context(nc.semaphore(n))
        bank = [ctx.enter_context(nc.psum_tensor(f"rbank{n}", [P, BANK], F32)) for n in range(8)]
        ident = keep["ident"]
        w_out = sb("w_out", [P, KC, D])
        w_r = sb("router_w", [P, KC, E])
        ws13, ws2 = sb("shared_w13", [P, 2, KC, F]), sb("shared_w2", [P, FC, D])
        post, scale, shift = sb("post_scale", [P, D]), sb("scale2", [P, D]), sb("shift2", [P, D])
        e_bias = sb("router_bias", [P, E])
        ones, strict, before = sb("ones", [P, P]), sb("strict", [P, P]), sb("group_before", [P, NG, NG])
        ym, x, x2, h2 = sb("ymix_tile", [P, D]), sb("x_in", [P, D]), sb("x2_tile", [P, D]), sb("h2_tile", [P, D])
        yT, h2T = sb("ymixT", [P, KC, P]), sb("h2T", [P, KC, P])
        sq = sb("sq", [P, D])
        st = sb("norm_stats", [P, 8])
        sc, bi, cand, left = sb("scores", [P, E]), sb("biased", [P, E]), sb("candidates", [P, E]), sb("left", [P, E])
        sel, rw = sb("selected", [P, E]), sb("route_w", [P, E])
        g8 = sb("group_top", [P, NG, 8])
        gs, gr, gq, gk = sb("group_score", [P, NG]), sb("group_rank", [P, NG]), sb("group_cmp", [P, NG, NG]), sb("group_eq", [P, NG, NG])
        top, ws = sb("top8", [P, 8]), sb("weight_sum", [P, 4])
        sg, acts, aT, ysh = sb("sh_sig", [P, F]), sb("sh_act", [P, F]), sb("sh_actT", [P, FC, P]), sb("y_shared", [P, D])
        posm, W, seen = keep["posm"], keep["W"], keep["seen"]
        consts_in, load_in, zero_done, outs, out_free = (sem(n) for n in ("r_consts_in", "ymix_in", "r_zero_done", "r_outs", "r_out_free"))
        dve_step, act_step = sem("r_dve_step"), sem("r_act_step")
        PE = Stages(sem("r_pe_done"), ["yT", "proj", "h2T", "route", "up", "pos", "aT", "down"])
        V = Stages(sem("r_dve_done"), ["ss", "xn", "x2", "h2", "logit", "sh_arg", "sh_act", "sel", "aT", "pos"])
        C = Stages(sem("r_act_done"), ["yT", "sq", "rstd", "rstd2", "h2T", "score_exp", "sh_exp", "down"])
        k4 = lambda x: x.rearrange("p (k n) -> p k n", k=4)
        row = lambda n: dr["rows"][:, n * D:(n + 1) * D].partition_broadcast(P)
        kp = lambda x: x.rearrange("(k p) n -> p k n", p=P)
        CONSTS = 12
        block = ctx.enter_context(nc.Block())

        @block.sync
        def _(sp):
            for dst, src in ((w_out[:], kp(io["w_out"][0])), (w_r[:], kp(io["router_w"][0])),
                             (ws13[:, 0], kp(io["shared_w1"][0])), (ws13[:, 1], kp(io["shared_w3"][0])), (ws2[:], kp(io["shared_w2"][0])),
                             (post[:], row(2)), (scale[:], row(4)), (shift[:], row(3)),
                             (e_bias[:], io["router_bias"][0:1, :].partition_broadcast(P)),
                             (ones[:], io["c_ones"]), (strict[:], io["c_strict"]), (before[:], io["c_before"])):
                sp.dma_start(dst, src).then_inc(consts_in, 16)
            sp.wait_ge(zero_done, 1)
            sp.dma_start(dr["h2"][S:S + P, :], sq[:]).then_inc(outs, 16)
            sp.dma_start(dr["acc"][S:S + P, :], sq[:]).then_inc(outs, 16)
            sp.wait_ge(outs, 32)
            sp.sem_inc(out_free, 3)
            with sp.Fori(0, NT) as t:
                rows = bass.ds(t * P, P)
                PE.wait_before(sp, t, "yT")
                sp.dma_start(ym[:], dr["ymix"][rows, :]).then_inc(load_in, 16)
                V.wait_before(sp, t, "x2")
                sp.dma_start(x[:], io["x"][0][rows, :]).then_inc(load_in, 16)
                V.wait(sp, t, "x2")
                sp.dma_start(dr["x2"][rows, :], x2[:]).then_inc(outs, 16)
                V.wait(sp, t, "h2")
                sp.dma_start(dr["h2"][rows, :], h2[:]).then_inc(outs, 16)
                sp.wait_ge(outs, t * 48 + 64)
                sp.sem_inc(out_free, 2)
                C.wait(sp, t, "down")
                sp.dma_start(dr["acc"][rows, :], ysh[:]).then_inc(outs, 16)
                sp.wait_ge(outs, t * 48 + 80)
                sp.sem_inc(out_free, 1)

        @block.scalar
        def _(act):
            load_exp_and_ln(nc, act)
            step = Steps(act, act_step)
            C.start(act)
            act.wait_ge(out_free, 3)
            with act.Fori(0, NT) as t:
                PE.wait(act, t, "yT")
                act.copy(yT[:, 0:4, :], k4(bank[0][:]))
                C.done(act.copy(yT[:, 4:8, :], k4(bank[1][:])), "yT")
                PE.wait(act, t, "proj")
                act.activation(sq[:, 0:BANK], bank[2][:], ACT.Square, accum_out=st[:, 0:1])
                C.done(act.activation(sq[:, BANK:], bank[3][:], ACT.Square, accum_out=st[:, 1:2]), "sq")
                V.wait(act, t, "ss")
                step.then(act.activation(st[:, 3:4], st[:, 2:3], ACT.Ln, scale=1.0 / D, bias=keep["eps"][:, 0:1]))
                C.done(act.activation(st[:, 4:5], st[:, 3:4], ACT.Exp, scale=-0.5), "rstd")
                V.wait(act, t, "x2")
                step.then(act.activation(sq[:], x2[:], ACT.Square, accum_out=st[:, 5:6]))
                step.then(act.activation(st[:, 6:7], st[:, 5:6], ACT.Ln, scale=1.0 / D, bias=keep["eps"][:, 0:1]))
                C.done(act.activation(st[:, 7:8], st[:, 6:7], ACT.Exp, scale=-0.5), "rstd2")
                PE.wait(act, t, "h2T")
                act.copy(h2T[:, 0:4, :], k4(bank[0][:]))
                C.done(act.copy(h2T[:, 4:8, :], k4(bank[1][:])), "h2T")
                V.wait(act, t, "logit")
                C.done(act.activation(sc[:], sc[:], ACT.Exp, scale=-1.0), "score_exp")
                V.wait(act, t, "sh_arg")
                C.done(act.activation(sg[:], sg[:], ACT.Exp, scale=-1.0), "sh_exp")
                PE.wait(act, t, "down")
                act.wait_ge(out_free, t * 3 + 3)
                act.copy(ysh[:, 0:BANK], bank[2][:])
                C.done(act.copy(ysh[:, BANK:], bank[3][:]), "down")
                step.restart()

        @block.vector
        def _(dve):
            step = Steps(dve, dve_step)
            tt, ts, stt = dve.tensor_tensor, dve.tensor_scalar, dve.scalar_tensor_tensor
            V.start(dve)
            dve.memset(sq[:], 0.0).then_inc(zero_done, 1)
            step.then(dve.memset(seen[:], 0.0))
            dve.wait_ge(consts_in, 16 * CONSTS)
            step.restart()
            with dve.Fori(0, NT) as t:
                C.wait(dve, t, "sq")
                V.done(tt(st[:, 2:3], st[:, 0:1], st[:, 1:2], ALU.add), "ss")
                C.wait(dve, t, "rstd")
                dve.wait_ge(out_free, t * 3 + 3)
                for n in range(2):
                    c = slice(n * BANK, (n + 1) * BANK)
                    q = stt(x2[:, c], bank[2 + n][:], st[:, 4:5], post[:, c], ALU.mult, ALU.mult)
                V.done(q, "xn")
                V.wait(dve, t, "xn")
                dve.wait_ge(load_in, t * 32 + 32)
                V.done(tt(x2[:], x2[:], x[:], ALU.add), "x2")
                C.wait(dve, t, "rstd2")
                step.then(stt(h2[:], x2[:], st[:, 7:8], scale[:], ALU.mult, ALU.mult))
                V.done(tt(h2[:], h2[:], shift[:], ALU.add), "h2")
                PE.wait(dve, t, "route")
                V.done(ts(sc[:], bank[4][:, 0:E], -80.0, None, ALU.max), "logit")
                PE.wait(dve, t, "up")
                V.done(ts(sg[:], bank[5][:, 0:F], -80.0, None, ALU.max), "sh_arg")
                C.wait(dve, t, "score_exp")
                step.then(ts(sc[:], sc[:], 1.0, None, ALU.add))
                step.then(dve.reciprocal(sc[:], sc[:]))
                C.wait(dve, t, "sh_exp")
                step.then(ts(sg[:], sg[:], 1.0, None, ALU.add))
                step.then(dve.reciprocal(sg[:], sg[:]))
                step.then(tt(sg[:], sg[:], bank[5][:, 0:F], ALU.mult))
                PE.wait_before(dve, t, "aT")
                V.done(tt(acts[:], sg[:], bank[5][:, F:2 * F], ALU.mult), "sh_act")
                step.then(tt(bi[:], sc[:], e_bias[:], ALU.add))
                for n in range(NG):
                    q = dve.max(g8[:, n, :], bi[:, n * EG:(n + 1) * EG])
                step.then(q)
                step.then(tt(gs[:], g8[:, :, 0], g8[:, :, 1], ALU.add))
                mine, other = gs[:].unsqueeze(2).to_broadcast([P, NG, NG]), gs[:].unsqueeze(1).to_broadcast([P, NG, NG])
                step.then(tt(gk[:], other, mine, ALU.is_equal))
                step.then(tt(gk[:], gk[:], before[:], ALU.mult))
                step.then(tt(gq[:], other, mine, ALU.is_gt))
                step.then(tt(gq[:], gq[:], gk[:], ALU.add))
                step.then(dve.tensor_reduce(gr[:], gq[:], AX.X, ALU.add))
                step.then(ts(gr[:], gr[:], TOPK_GROUPS - 0.5, None, ALU.is_lt))
                step.then(ts(gs[:], gr[:], -NEG, NEG, ALU.mult, ALU.add))
                g3 = lambda x: x.rearrange("p (g e) -> p g e", g=NG)
                gb = lambda x: x.unsqueeze(2).to_broadcast([P, NG, EG])
                step.then(tt(g3(cand[:]), g3(bi[:]), gb(gr[:]), ALU.mult))
                step.then(tt(g3(cand[:]), g3(cand[:]), gb(gs[:]), ALU.add))
                step.then(dve.max(top[:], cand[:]))
                step.then(dve.match_replace(left[:], top[:], cand[:], DROP))
                PE.wait_before(dve, t, "pos")
                V.done(ts(sel[:], left[:], DROP, None, ALU.is_equal), "sel")
                V.wait(dve, t, "sel")
                step.then(tt(rw[:], sc[:], sel[:], ALU.mult))
                step.then(dve.tensor_reduce(ws[:, 0:1], rw[:], AX.X, ALU.add))
                step.then(ts(ws[:, 1:2], ws[:, 0:1], 1e-20, None, ALU.add))
                step.then(dve.reciprocal(ws[:, 2:3], ws[:, 1:2]))
                step.then(ts(W[:, bass.ds(t, 1), :].squeeze(1), rw[:], ws[:, 2:3], ROUTED_SCALE, ALU.mult, ALU.mult))
                PE.wait(dve, t, "aT")
                V.done(dve.tensor_copy(aT[:], bank[6][:, 0:F].rearrange("p (k n) -> p k n", k=FC)), "aT")
                PE.wait(dve, t, "pos")
                step.then(tt(seen[:], seen[:], sel[:], ALU.add))
                step.then(stt(left[:], bank[7][:, 0:E], 1.0, sel[:], ALU.add, ALU.mult))
                V.done(ts(posm[:, bass.ds(t, 1), :].squeeze(1), left[:], -1.0, None, ALU.add), "pos")
                V.wait(dve, t, "pos")
                step.restart()

        @block.tensor
        def _(pe):
            PE.start(pe)
            mm = pe.matmul
            pe.wait_ge(consts_in, 16 * CONSTS)
            with pe.Fori(0, NT) as t:
                pe.wait_ge(load_in, t * 32 + 32)
                for k in range(KC):
                    q = pe.transpose(bank[k // 4][:, (k % 4) * P:(k % 4 + 1) * P], ym[:, k * P:(k + 1) * P], ident[:])
                PE.done(q, "yT")
                C.wait(pe, t, "yT")
                C.wait_before(pe, t, "down")
                for n in range(2):
                    for k in range(KC):
                        q = mm(bank[2 + n][:], yT[:, k, :], w_out[:, k, n * BANK:(n + 1) * BANK], start=(k == 0), stop=(k == KC - 1))
                PE.done(q, "proj")
                V.wait(pe, t, "h2")
                for k in range(KC):
                    q = pe.transpose(bank[k // 4][:, (k % 4) * P:(k % 4 + 1) * P], h2[:, k * P:(k + 1) * P], ident[:])
                PE.done(q, "h2T")
                C.wait(pe, t, "h2T")
                for k in range(KC):
                    q = mm(bank[4][:, 0:E], h2T[:, k, :], w_r[:, k, :], start=(k == 0), stop=(k == KC - 1))
                PE.done(q, "route")
                for k in range(KC):
                    q = mm(bank[5][:].rearrange("p (a n) -> p a n", a=2), h2T[:, k, :], ws13[:, :, k, :], start=(k == 0), stop=(k == KC - 1))
                PE.done(q, "up")
                V.wait(pe, t, "sel")
                mm(bank[7][:, 0:E], ones[:], seen[:], start=True, stop=False)
                PE.done(mm(bank[7][:, 0:E], strict[:], sel[:], start=False, stop=True), "pos")
                V.wait(pe, t, "sh_act")
                for k in range(FC):
                    q = pe.transpose(bank[6][:, k * P:(k + 1) * P], acts[:, k * P:(k + 1) * P], ident[:])
                PE.done(q, "aT")
                V.wait(pe, t, "aT")
                for n in range(2):
                    for k in range(FC):
                        q = mm(bank[2 + n][:], aT[:, k, :], ws2[:, k, n * BANK:(n + 1) * BANK], start=(k == 0), stop=(k == FC - 1))
                PE.done(q, "down")


def schedule(nc, io, dr, keep):
    with ExitStack() as ctx:
        sb = lambda n, s: ctx.enter_context(nc.sbuf_tensor(n, s, F32))
        sem = lambda n: ctx.enter_context(nc.semaphore(n))
        ps_a, ps_b = (ctx.enter_context(nc.psum_tensor(n, [P, BANK], F32)) for n in ("sched_a", "sched_b"))
        ones, upper, thr, iota_b, step3 = sb("s_ones", [P, P]), sb("s_upper", [P, P]), sb("thresholds", [E, 8]), sb("iota_b", [P, NB]), sb("step3", [E, P])
        cnt, more, nblk, end, ind, nbc = sb("counts", [E, 1]), sb("more", [E, 8]), sb("n_blocks", [E, 1]), sb("end", [E, 1]), sb("ended", [E, NB]), sb("nbc", [E, P])
        over, first = sb("over", [P, NB]), sb("first", [P, NB])
        tab, base = keep["tab"], keep["base"]
        consts_in, dve_done, pe_done = sem("s_consts_in"), sem("s_dve_done"), sem("s_pe_done")
        block = ctx.enter_context(nc.Block())

        @block.sync
        def _(sp):
            for dst, src in ((ones[:], io["c_ones"]), (upper[:], io["c_upper"]), (thr[:], io["c_thresholds"]),
                             (iota_b[:], io["c_iota_b"].partition_broadcast(P)), (step3[:], io["c_step3"])):
                sp.dma_start(dst, src).then_inc(consts_in, 16)
            sp.wait_ge(consts_in, 80)

        @block.vector
        def _(dve):
            step = Steps(dve, dve_done)
            dve.wait_ge(consts_in, 80)
            dve.wait_ge(pe_done, 1)
            step.then(dve.tensor_copy(cnt[:], ps_a[0:E, 0:1]))
            step.then(dve.tensor_scalar(more[:], thr[:], cnt[:], None, ALU.is_lt))
            step.then(dve.tensor_reduce(nblk[:], more[:], AX.X, ALU.add))
            step.then(dve.tensor_copy(nbc[:], nblk[:].to_broadcast([E, P])))
            dve.wait_ge(pe_done, 2)
            step.then(dve.tensor_copy(end[:], ps_b[0:E, 0:1]))
            step.then(dve.tensor_scalar(ind[:], iota_b[0:E, :], end[:], None, ALU.is_ge))
            dve.wait_ge(pe_done, 3)
            e_raw, start, w3 = (ps_a[:, n * NB:(n + 1) * NB] for n in range(3))
            step.then(dve.tensor_scalar(over[:], e_raw, E - 0.5, 4096.0, ALU.is_gt, ALU.mult))
            step.then(dve.tensor_tensor(first[:], iota_b[:], start, ALU.subtract))
            step.then(dve.scalar_tensor_tensor(base[:], first[:], float(P), over[:], ALU.mult, ALU.add))
            step.then(dve.tensor_scalar(tab[0:1, 0, :], e_raw[0:1, :], E - 1.0, None, ALU.min))
            step.then(dve.tensor_copy(tab[0:1, 1, :], w3[0:1, :]))
            step.then(dve.tensor_copy(tab[0:1, 2, 0:E], ps_b[0:1, E:2 * E]))

        @block.tensor
        def _(pe):
            mm = pe.matmul
            pe.wait_ge(consts_in, 80)
            mm(ps_a[0:E, 0:1], keep["seen"][:], ones[:, 0:1], start=True, stop=True).then_inc(pe_done, 1)
            pe.wait_ge(dve_done, 4)
            mm(ps_b[0:E, 0:1], upper[0:E, 0:E], nblk[:], start=True, stop=True).then_inc(pe_done, 1)
            pe.wait_ge(dve_done, 6)
            mm(ps_b[:, E:2 * E], nbc[:], upper[0:E, 0:E], start=True, stop=True)
            mm(ps_a[:, 0:NB], ones[0:E, :], ind[:], start=True, stop=True)
            mm(ps_a[:, NB:2 * NB], nbc[:], ind[:], start=True, stop=True)
            mm(ps_a[:, 2 * NB:3 * NB], step3[:], ind[:], start=True, stop=True).then_inc(pe_done, 1)


def experts(nc, io, dr, keep):
    I32 = mybir.dt.int32
    with ExitStack() as ctx:
        sb = lambda n, s, dt=F32: ctx.enter_context(nc.sbuf_tensor(n, s, dt))
        sem = lambda n: ctx.enter_context(nc.semaphore(n))
        pt = lambda n: ctx.enter_context(nc.psum_tensor(n, [P, BANK], F32))
        ident, posm, W, tab, base = keep["ident"], keep["posm"], keep["W"], keep["tab"], keep["base"]
        w13, w2 = sb("w13", [P, 3, 2, KC, F]), sb("w2", [P, 3, FC, D])
        iota, vals, empty = sb("iota_p", [P, P]), sb("id_and_weight", [P, NT, 2]), sb("empty_row", [P, 1])
        pcol, onehot = sb("place", [P, NT]), sb("onehot_p", [P, NT, P])
        nid, isn = sb("list_id", [P, 4]), sb("is_empty", [P, 2])
        wslot = [sb(f"slot_w{j}", [P, 1]) for j in range(4)]
        idx = [sb(f"idx{j}", [P, 1], I32) for j in range(4)]
        sidx = [sb(f"scatter_idx{j}", [P, 1], I32) for j in range(2)]
        xg = [sb(f"gathered{j}", [P, D]) for j in range(2)]
        y = [sb(f"y_rows{j}", [P, D]) for j in range(2)]
        xT, sg, acts, aT = sb("xT", [P, KC, P]), sb("silu_g", [P, F]), sb("act", [P, F]), sb("actT", [P, FC, P])
        ps_x, ps_y = [pt(f"ps_x{n}") for n in range(2)], [pt(f"ps_y{n}") for n in range(2)]
        ps_h, ps_a, ps_l = pt("ps_h"), pt("ps_a"), pt("ps_l")
        held = sem("held")
        consts_in, w_ready, dve_step = sem("e_consts_in"), sem("w_ready"), sem("e_dve_step")
        piece_in = [sem(f"piece_in{n}") for n in range(3)]
        xg_in = [sem(f"xg_in{n}") for n in range(2)]
        onehot_ready, list_mm, idx_ready, x_mm, x_copied, up_mm, silu_done, act_ready, at_mm, aT_ready, dn_mm, y_ready, y_out, y_free = (
            sem(n) for n in ("onehot_ready", "list_mm", "idx_ready", "x_mm", "x_copied", "up_mm", "silu_done", "act_ready",
                             "at_mm", "aT_ready", "dn_mm", "y_ready", "e_y_out", "e_y_free"))
        views = [io[n][0].rearrange("e (p k) f -> e p k f", p=P) for n in ("exp_w1", "exp_w3")]
        view2 = io["exp_w2"][0].rearrange("e (p k) d -> e p k d", p=P)
        TURNS = (BLOCKS + 3) // 4
        block = ctx.enter_context(nc.Block())

        def n_blocks(eng):
            return eng.value_load(tab[0:1, 2, E - 1:E], min_val=E, max_val=BLOCKS)

        @block.sync
        def _(sp):
            for dst, src in ((iota[:], io["c_iota_p"].partition_broadcast(P)), (vals[:, :, 0:1], io["c_ids"]), (empty[:], io["c_empty"])):
                sp.dma_start(dst, src, allow_slow_non_contiguous=True).then_inc(consts_in, 16)

            def load(e, s, turn, after=None):
                for n in range(6):
                    if s or n >= 3 or after is not None:
                        sp.wait_ge(piece_in[n % 3], turn * 96 + (s * 6 + n) // 3 * 16)
                    if n == 3 and (s or after is not None):
                        sp.sem_inc(w_ready, 1)
                    if n == 0 and after is not None:
                        sp.wait_ge(dn_mm, sp.value_load(tab[0:1, 2, bass.ds(after, 1)], min_val=1, max_val=BLOCKS) + 1)
                    which, half = n // 2, n % 2
                    if which < 2:
                        k = slice(half * KC // 2, (half + 1) * KC // 2)
                        sp.dma_start(w13[:, s, which, k], views[which][bass.ds(e, 1)].squeeze(0)[:, k, :]).then_inc(piece_in[n % 3], 16)
                    else:
                        sp.dma_start(w2[:, s, half], view2[bass.ds(e, 1)].squeeze(0)[:, half, :]).then_inc(piece_in[n % 3], 16)

            for s in range(3):
                load(s, s, 0)
            with sp.Fori(1, E // 3) as i:
                for s in range(3):
                    load(i * 3 + s, s, i, i * 3 + s - 3)
            load(E - 1, 0, E // 3, E - 4)
            for n in range(3):
                sp.wait_ge(piece_in[n], E * 32)
            sp.sem_inc(w_ready, 1)

        @block.gpsimd
        def _(pool):
            nb = n_blocks(pool)
            pool.sem_inc(y_free, 2)

            def gather(n, j):
                par = j % 2
                pool.wait_ge(idx_ready, n + 1)
                pool.sem_inc(held, 1)
                pool.indirect_dma_start(xg[par][:], None, dr["h2"], bass.IndirectOffsetOnAxis(ap=idx[j][:], axis=0)).then_inc(xg_in[par], 16)

            for n in range(3):
                if n == 2:
                    pool.wait_ge(x_mm, 1)
                gather(n, n)
            with pool.Fori(0, TURNS) as i:
                with pool.If(nb > i * 4):
                    for j in range(4):
                        b = i * 4 + j
                        pool.wait_ge(x_mm, b + 2)
                        gather(b + 3, (j + 3) % 4)
                        pool.wait_ge(y_ready, b + 2)
                        pool.sem_inc(held, 1)
                        pool.indirect_dma_start(dr["acc"], bass.IndirectOffsetOnAxis(ap=sidx[j % 2][:], axis=0), y[j % 2][:], None,
                                                compute_op=ALU.add).then_inc(y_out, 16)
                        pool.wait_ge(y_out, b * 16 + 16)
                        pool.sem_inc(y_free, 1)

        @block.scalar
        def _(act):
            nb = n_blocks(act)
            act.sem_inc(y_ready, 1)

            def x_copy(n):
                act.wait_ge(x_mm, n + 1)
                act.copy(xT[:, 0:4, :], ps_x[0][:].rearrange("p (k n) -> p k n", k=4))
                act.copy(xT[:, 4:8, :], ps_x[1][:].rearrange("p (k n) -> p k n", k=4)).then_inc(x_copied, 1)

            def silu(n):
                act.wait_ge(up_mm, n + 1)
                act.activation(sg[:], ps_h[:, 0:F], ACT.Silu).then_inc(silu_done, 1)

            x_copy(0)
            silu(0)
            with act.Fori(0, TURNS) as i:
                with act.If(nb > i * 4):
                    for j in range(4):
                        b = i * 4 + j
                        x_copy(b + 1)
                        act.wait_ge(act_ready, b + 1)
                        silu(b + 1)
                        act.wait_ge(y_free, b + 1)
                        act.wait_ge(dn_mm, b + 2)
                        act.copy(y[j % 2][:, 0:BANK], ps_y[0][:])
                        act.copy(y[j % 2][:, BANK:], ps_y[1][:]).then_inc(y_ready, 1)

        @block.vector
        def _(dve):
            step = Steps(dve, dve_step)
            nb = n_blocks(dve)
            dve.wait_ge(consts_in, 48)

            def make_onehot(n, e):
                step.then(dve.tensor_scalar(pcol[:], posm[:, :, bass.ds(e, 1)].squeeze(2), base[:, bass.ds(n, 1)], None, ALU.subtract))
                step.then(dve.tensor_copy(vals[:, :, 1:2], W[:, :, bass.ds(e, 1)]))
                for k in range(NT):
                    q = dve.tensor_scalar(onehot[:, k, :], iota[:], pcol[:, k:k + 1], None, ALU.is_equal)
                q.then_inc(onehot_ready, 1)

            def expert_of(n):
                return dve.value_load(tab[0:1, 0, bass.ds(n, 1)], min_val=0, max_val=E - 1)

            def make_index(n, par):
                dve.wait_ge(list_mm, n + 1)
                step.then(dve.tensor_copy(nid[:, 0:2], ps_l[:, 0:2]))
                step.then(dve.tensor_scalar(isn[:, 0:1], nid[:, 0:1], 0.0, None, ALU.is_equal))
                step.then(dve.tensor_copy(wslot[par][:], nid[:, 1:2]))
                step.then(dve.tensor_tensor(isn[:, 1:2], isn[:, 0:1], empty[:], ALU.mult))
                dve.scalar_tensor_tensor(idx[par][:], nid[:, 0:1], -1.0, isn[:, 1:2], ALU.add, ALU.add).then_inc(idx_ready, 1)

            def activate(n, par):
                dve.wait_ge(silu_done, n + 1)
                dve.scalar_tensor_tensor(acts[:], sg[:], wslot[par][:], ps_h[:, F:2 * F], ALU.mult, ALU.mult).then_inc(act_ready, 1)

            for n in range(3):
                make_onehot(n, expert_of(n))
                make_index(n, n)
            make_onehot(3, expert_of(3))
            activate(0, 0)
            step.restart()
            with dve.Fori(0, TURNS) as i:
                with dve.If(nb > i * 4):
                    for j in range(4):
                        b = i * 4 + j
                        dve.wait_ge(at_mm, b + 1)
                        dve.wait_ge(dn_mm, b + 1)
                        dve.tensor_copy(aT[:], ps_a[:, 0:F].rearrange("p (k n) -> p k n", k=FC)).then_inc(aT_ready, 1)
                        dve.wait_ge(y_free, b + 1)
                        dve.wait_ge(idx_ready, b + 1)
                        step.then(dve.tensor_copy(sidx[j % 2][:], idx[j][:]))
                        dve.wait_ge(x_mm, b + 1)
                        make_index(b + 3, (j + 3) % 4)
                        make_onehot(b + 4, expert_of(b + 4))
                        activate(b + 1, (j + 1) % 4)
                    step.restart()

        @block.tensor
        def _(pe):
            nb = n_blocks(pe)
            pe.sem_inc(dn_mm, 1)

            def list_of(n):
                pe.wait_ge(onehot_ready, n + 1)
                for k in range(NT):
                    q = pe.matmul(ps_l[:, 0:2], onehot[:, k, :], vals[:, k, :], start=(k == 0), stop=(k == NT - 1))
                q.then_inc(list_mm, 1)

            def x_transpose(n, par, turn):
                pe.wait_ge(xg_in[par], turn * 16 + 16)
                for k in range(KC):
                    q = pe.transpose(ps_x[k // 4][:, (k % 4) * P:(k % 4 + 1) * P], xg[par][:].rearrange("p (c k) -> p k c", k=KC)[:, k, :], ident[:])
                q.then_inc(x_mm, 1)

            def entry(which, n, hi):
                return pe.value_load(tab[0:1, which, bass.ds(n, 1)], min_val=0, max_val=hi)

            def up(n):
                e, w = entry(0, n, E - 1), entry(1, n, 2)
                pe.wait_ge(w_ready, e + 1)
                pe.wait_ge(x_copied, n + 1)
                for k in range(KC):
                    q = pe.matmul(ps_h[:].rearrange("p (a n) -> p a n", a=2), xT[:, k, :], w13[:, bass.ds(w, 1), :, k, :].squeeze(1),
                                  start=(k == 0), stop=(k == KC - 1))
                q.then_inc(up_mm, 1)

            for n in range(3):
                if n:
                    pe.wait_ge(idx_ready, n)
                list_of(n)
            x_transpose(0, 0, 0)
            up(0)
            with pe.Fori(0, TURNS) as i:
                with pe.If(nb > i * 4):
                    for j in range(4):
                        b = i * 4 + j
                        x_transpose(b + 1, (j + 1) % 2, i * 2 + (j + 1) // 2)
                        pe.wait_ge(act_ready, b + 1)
                        for k in range(FC):
                            q = pe.transpose(ps_a[:, k * P:(k + 1) * P], acts[:].rearrange("p (c k) -> p k c", k=FC)[:, k, :], ident[:])
                        q.then_inc(at_mm, 1)
                        pe.wait_ge(idx_ready, b + 3)
                        list_of(b + 3)
                        up(b + 1)
                        w = entry(1, b, 2)
                        pe.wait_ge(aT_ready, b + 1)
                        pe.wait_ge(y_ready, b + 1)
                        for n in range(2):
                            for k in range(FC):
                                q = pe.matmul(ps_y[n][:], aT[:, k, :], w2[:, bass.ds(w, 1), k, n * BANK:(n + 1) * BANK].squeeze(1),
                                              start=(k == 0), stop=(k == FC - 1))
                        q.then_inc(dn_mm, 1)


def finish(nc, io, dr, keep, out):
    with ExitStack() as ctx:
        sb = lambda n, s: ctx.enter_context(nc.sbuf_tensor(n, s, F32))
        sem = lambda n: ctx.enter_context(nc.semaphore(n))
        post = sb("post2", [P, D])
        a, x2, junk = ([sb(f"{n}{j}", [P, D]) for j in range(2)] for n in ("acc_tile", "x2_in", "sq2"))
        st = [sb(f"f_stats{j}", [P, 3]) for j in range(2)]
        post_in, dve_step = sem("post_in"), sem("f_dve_step")
        tile_in = [sem(f"tile_in{j}") for j in range(2)]
        rstd, sums, ready, outs, act_step = sem("f_rstd"), sem("f_sums"), sem("f_ready"), sem("f_outs"), sem("f_act_step")
        block = ctx.enter_context(nc.Block())

        @block.sync
        def _(sp):
            sp.dma_start(post[:], dr["rows"][:, 5 * D:6 * D].partition_broadcast(P)).then_inc(post_in, 16)
            with sp.Fori(0, NT // 2) as i:
                for j in range(2):
                    rows = bass.ds((i * 2 + j) * P, P)
                    sp.wait_ge(ready, i * 2 + j + 1)
                    sp.dma_start(a[j][:], dr["acc"][rows, :]).then_inc(tile_in[j], 16)
                    sp.dma_start(x2[j][:], dr["x2"][rows, :]).then_inc(tile_in[j], 16)

        @block.scalar
        def _(act):
            load_exp_and_ln(nc, act)
            step = Steps(act, act_step)
            with act.Fori(0, NT // 2) as i:
                for j in range(2):
                    act.wait_ge(tile_in[j], i * 32 + 32)
                    step.then(act.activation(junk[j][:], a[j][:], ACT.Square, accum_out=st[j][:, 0:1]))
                    step.then(act.activation(st[j][:, 1:2], st[j][:, 0:1], ACT.Ln, scale=1.0 / D, bias=keep["eps"][:, 0:1]))
                    act.activation(st[j][:, 2:3], st[j][:, 1:2], ACT.Exp, scale=-0.5).then_inc(rstd, 1)
                step.restart()

        @block.vector
        def _(dve):
            step = Steps(dve, dve_step)
            dve.wait_ge(post_in, 16)
            with dve.Fori(0, NT // 2) as i:
                for j in range(2):
                    dve.wait_ge(rstd, i * 2 + j + 1)
                    step.then(dve.scalar_tensor_tensor(a[j][:], a[j][:], st[j][:, 2:3], post[:], ALU.mult, ALU.mult))
                    step.then(dve.tensor_tensor(x2[j][:], x2[j][:], a[j][:], ALU.add))
                    dve.sem_inc(sums, 1)
                step.restart()

        @block.gpsimd
        def _(pool):
            pool.sem_inc(ready, 2)
            with pool.Fori(0, NT // 2) as i:
                for j in range(2):
                    t = i * 2 + j
                    pool.wait_ge(sums, t + 1)
                    pool.dma_start(out[0][bass.ds(t * P, P), :], x2[j][:]).then_inc(outs, 16)
                    pool.wait_ge(outs, t * 16 + 16)
                    pool.sem_inc(ready, 1)


def t5_buckets(n):
    exact = N_BUCKETS // 2
    nf = np.maximum(n, 1).astype(np.float32)
    large = exact + (np.log(nf / exact) / math.log(MAX_DISTANCE / exact) * (N_BUCKETS - exact)).astype(np.int32)
    return np.where(n < exact, n, np.minimum(large, N_BUCKETS - 1))


def constants():
    s, t = np.arange(P)[:, None], np.arange(P)[None, :]
    f = lambda x: np.ascontiguousarray(x, dtype=np.float32)
    dist = 2 * P - 1 - np.arange(3 * P)
    onehot = np.zeros((N_BUCKETS + 1, 3 * P), np.float32)
    onehot[np.where(dist >= 0, t5_buckets(np.maximum(dist, 0)), N_BUCKETS), np.arange(3 * P)] = 1
    lower, upper = s > t, s < t
    blocks = [s // b == t // b for b in (16, 32, 64, 128)]
    masks = [lower, lower & blocks[0], upper & blocks[0]]
    for n in range(3):
        masks += [lower & blocks[n + 1] & ~blocks[n], upper & blocks[n + 1] & ~blocks[n]]
    mid = P // 2 - 1
    return {
        "c_ident": f(s == t),
        "c_upper": f(s <= t),
        "c_onehot": onehot,
        "c_mask4": f(np.stack([upper, s <= t, upper, s <= t], 1)),
        "c_masks": f(np.stack(masks, 1)),
        "c_cum": f((s <= t).astype(int) - (s <= mid).astype(int)),
        "c_ones": f(np.ones((P, P))),
        "c_strict": f(upper),
        "c_before": f(np.broadcast_to(np.tril(np.ones((NG, NG)), -1), (P, NG, NG))),
        "c_thresholds": f(np.broadcast_to([-1] + [P * n for n in range(1, S // P)], (E, 8))),
        "c_iota_b": f(np.arange(NB)[None, :]),
        "c_step3": f(np.broadcast_to([[(e + 1) % 3 - e % 3] for e in range(E)], (E, P))),
        "c_iota_p": f(np.arange(P)[None, :]),
        "c_ids": f((np.arange(NT)[None, :] * P + np.arange(P)[:, None] + 1)[:, :, None]),
        "c_empty": f(S + 1 + np.arange(P)[:, None]),
        "c_halves": f(np.concatenate([s <= mid, s > mid], 1)),
    }


def build(nc, io, out, dr):
    with ExitStack() as ctx:
        sb = lambda n, s: ctx.enter_context(nc.sbuf_tensor(n, s, F32))
        keep = {"ident": sb("ident", [P, P]), "upper": sb("upper", [P, P]), "eps": sb("eps", [P, 4])}
        consts_in = ctx.enter_context(nc.semaphore("masks_in"))
        eps_done = ctx.enter_context(nc.semaphore("eps_done"))
        with nc.Block() as block:
            @block.sync
            def _(sp):
                sp.dma_start(keep["ident"][:], io["c_ident"]).then_inc(consts_in, 16)
                sp.dma_start(keep["upper"][:], io["c_upper"]).then_inc(consts_in, 16)
                sp.wait_ge(consts_in, 32)

            @block.vector
            def _(dve):
                dve.memset(keep["eps"][:, 0:1], RMS_EPS)
                dve.memset(keep["eps"][:, 1:2], LN_EPS)
                dve.memset(keep["eps"][:, 2:3], 64e-5).then_inc(eps_done, 1)
                dve.wait_ge(eps_done, 1)
        make_rows(nc, io, dr)
        with ExitStack() as qkv:
            for n, s in (("qT", [P, AH, S]), ("kT", [P, AH, S]), ("v", [P, NT, AW])):
                keep[n] = qkv.enter_context(nc.sbuf_tensor(n, s, F32))
            project(nc, io, dr, keep)
            attend(nc, io, dr, keep)
        rwkv(nc, io, dr, keep)
        for n, s in (("posm", [P, NT, E]), ("W", [P, NT, E]), ("seen", [P, E]), ("base", [P, NB])):
            keep[n] = sb(n, s)
        keep["tab"] = ctx.enter_context(nc.sbuf_tensor("tab", [1, 3, NB], mybir.dt.int32))
        norm_route(nc, io, dr, keep)
        schedule(nc, io, dr, keep)
        experts(nc, io, dr, keep)
        finish(nc, io, dr, keep, out)


DUMP = ["rows", "pb", "ymix", "x2", "h2", "acc", "out_x"]
_INS = ['x', 'c', 'w_ada', 'b_ada', 'norm_pre_mix', 'norm_post_mix', 'norm_pre_ffn', 'norm_post_ffn',
        'w_in', 'w_out', 'rel_bias_table', 'diff_lambda', 'diff_subln', 'rwkv_mu', 'rwkv_w0', 'rwkv_w2', 'rwkv_a0', 'rwkv_a2',
        'rwkv_g2', 'rwkv_k_k', 'rwkv_k_a', 'rwkv_r_k', 'rwkv_lnx_g', 'rwkv_lnx_b', 'gmlp_ln_g', 'gmlp_ln_b', 'gmlp_w_s', 'gmlp_b_s',
        'router_w', 'router_bias', 'exp_w1', 'exp_w3', 'exp_w2', 'shared_w1', 'shared_w3', 'shared_w2']


def kernel(**inputs):
    import concourse.bacc as bacc
    from concourse.bass_utils import run_bass_kernel_spmd

    nc = bacc.Bacc("TRN2", target_bir_lowering=False, num_devices=1)
    arrays, io = {}, {}
    for name, a in [(n, np.ascontiguousarray(inputs[n])) for n in _INS] + list(constants().items()):
        arrays[f"in_{name}"] = a
        io[name] = nc.dram_tensor(f"in_{name}", a.shape, mybir.dt.from_np(a.dtype), kind="ExternalInput").ap()
    out = nc.dram_tensor("out_x", (1, S, D), F32, kind="ExternalOutput").ap()
    dr = {
        "rows": nc.dram_tensor("rows", (1, 6 * D), F32).ap(),
        "pb": nc.dram_tensor("pb", (S + 1, B_COLS), F32).ap(),
        "bias_by_dist": nc.dram_tensor("bias_by_dist", (AH, P, 3 * P), F32).ap(),
        "x2": nc.dram_tensor("x2", (S, D), F32).ap(),
        "h2": nc.dram_tensor("h2", (S + P, D), F32).ap(),
        "acc": nc.dram_tensor("acc", (S + P, D), F32).ap(),
        "ymix": nc.dram_tensor("ymix", (S, D), F32).ap(),
    }
    build(nc, io, out, dr)
    r = run_bass_kernel_spmd(nc, [arrays], core_ids=[0])
    return r.results[0]["out_x"]
```

```python
import concourse.bass as bass
from concourse import mybir
from contextlib import ExitStack
import math
import numpy as np

F32 = mybir.dt.float32
ALU = mybir.AluOpType
ACT = mybir.ActivationFunctionType
AX = mybir.AxisListType

P = 128
D = 1024
S = 1024
NT = S // P
KC = D // P
BANK = 512
AH, AQK = 4, 64
AW = AH * 2 * AQK
BH, BD = 4, 64
BW = BH * BD
CG, CD = 4, 64
CW = CG * CD
A_COLS, B_COLS = 3 * AW, 3 * BW + 64 + 64 + 128
RMS_EPS = 1e-6
LN_EPS = 1e-5
EXP_AND_LN = 6
GELU_1 = 2.0 * math.sqrt(2.0 / math.pi)
GELU_3 = GELU_1 * 0.044715


class Steps:

    def __init__(self, eng, sem):
        self.eng, self.sem, self.n = eng, sem, 0

    def then(self, ins):
        self.n += 1
        ins.then_inc(self.sem, 1)
        self.eng.wait_ge(self.sem, self.n)

    def restart(self):
        self.eng.sem_inc(self.sem, 1)
        self.eng.sem_clear(self.sem)
        self.n = 0


def make_rows(nc, io, dr):
    NCH = 6 * D // BANK
    with ExitStack() as ctx:
        sb = lambda n, s: ctx.enter_context(nc.sbuf_tensor(n, s, F32))
        sem = lambda n: ctx.enter_context(nc.semaphore(n))
        c_col = sb("c_col", [P, KC])
        e_col = sb("e_col", [P, KC])
        cond = sb("cond", [P, KC, P])
        w = [sb(f"w_ada{j}", [P, KC, BANK]) for j in range(2)]
        mod = sb("mod", [P, 6 * D])
        gains = sb("gains", [P, 4, D])
        ps = [ctx.enter_context(nc.psum_tensor(f"ps_mod{j}", [P, BANK], F32)) for j in range(2)]
        c_in, gains_in, cond_ready = sem("c_in"), sem("gains_in"), sem("cond_ready")
        w_in = [sem(f"w_ada_in{j}") for j in range(2)]
        mod_mm = [sem(f"mod_mm{j}") for j in range(2)]
        mod_read = [sem(f"mod_read{j}") for j in range(2)]
        c_low = sem("c_low")
        exp_done, dve_step, rows_ready, rows_out = sem("exp_done"), sem("dve_step"), sem("rows_ready"), sem("rows_out")
        w_view = io["w_ada"][0].rearrange("(k p) n -> p k n", p=P)
        block = ctx.enter_context(nc.Block())

        @block.sync
        def _(sp):
            sp.dma_start(c_col[:], io["c"].rearrange("a (k p) -> p (a k)", p=P), allow_slow_non_contiguous=True).then_inc(c_in, 16)
            sp.dma_start(mod[:], io["b_ada"][0:1, :].partition_broadcast(P)).then_inc(gains_in, 16)
            for n, name in enumerate(("norm_pre_mix", "norm_post_mix", "norm_pre_ffn", "norm_post_ffn")):
                sp.dma_start(gains[:, n, :], io[name][0:1, :].partition_broadcast(P)).then_inc(gains_in, 16)
            with sp.Fori(0, NCH // 2) as i:
                for j in range(2):
                    sp.wait_ge(mod_mm[j], i + 1)
                    sp.dma_start(w[j][:], w_view[:, :, bass.ds((i * 2 + j) * BANK, BANK)]).then_inc(w_in[j], 16)
            sp.wait_ge(rows_ready, 1)
            sp.dma_start(dr["rows"], mod[0:1, :]).then_inc(rows_out, 16)
            sp.wait_ge(rows_out, 16)

        @block.scalar
        def _(act):
            act.wait_ge(c_low, 1)
            act.activation(e_col[:], e_col[:], ACT.Exp, scale=-1.0).then_inc(exp_done, 1)

        @block.tensor
        def _(pe):
            pe.sem_inc(mod_mm[0], 1)
            pe.sem_inc(mod_mm[1], 1)
            pe.wait_ge(cond_ready, 1)
            with pe.Fori(0, NCH // 2) as i:
                for j in range(2):
                    pe.wait_ge(w_in[j], i * 16 + 16)
                    pe.wait_ge(mod_read[j], i + 1)
                    for k in range(KC):
                        mm = pe.matmul(ps[j][:], cond[:, k, :], w[j][:, k, :], start=(k == 0), stop=(k == KC - 1))
                    mm.then_inc(mod_mm[j], 1)

        @block.vector
        def _(dve):
            step = Steps(dve, dve_step)
            dve.sem_inc(mod_read[0], 1)
            dve.sem_inc(mod_read[1], 1)
            dve.wait_ge(c_in, 16)
            dve.tensor_scalar(e_col[:], c_col[:], -80.0, None, ALU.max).then_inc(c_low, 1)
            dve.wait_ge(exp_done, 1)
            step.then(dve.tensor_scalar(e_col[:], e_col[:], 1.0, None, ALU.add))
            step.then(dve.reciprocal(e_col[:], e_col[:]))
            step.then(dve.tensor_tensor(c_col[:], c_col[:], e_col[:], ALU.mult))
            dve.tensor_copy(cond[:], c_col[:].unsqueeze(2).to_broadcast([P, KC, P])).then_inc(cond_ready, 1)
            dve.wait_ge(gains_in, 16 * 5)
            with dve.Fori(0, NCH // 2) as i:
                for j in range(2):
                    dve.wait_ge(mod_mm[j], i + 2)
                    m = mod[:, bass.ds((i * 2 + j) * BANK, BANK)]
                    dve.tensor_tensor(m, ps[j][:], m, ALU.add).then_inc(mod_read[j], 1)
            for j in range(2):
                dve.wait_ge(mod_read[j], NCH // 2 + 1)
            row = lambda n: mod[:, n * D:(n + 1) * D]
            for half in range(2):
                step.then(dve.scalar_tensor_tensor(row(3 * half + 1), row(3 * half + 1), 1.0, gains[:, 2 * half, :], ALU.add, ALU.mult))
                step.then(dve.tensor_tensor(row(3 * half + 2), row(3 * half + 2), gains[:, 2 * half + 1, :], ALU.mult))
            dve.sem_inc(rows_ready, 1)


def project(nc, io, dr, keep):
    GROUPS = 6
    with ExitStack() as ctx:
        sb = lambda n, s: ctx.enter_context(nc.sbuf_tensor(n, s, F32))
        sem = lambda n: ctx.enter_context(nc.semaphore(n))
        pt = lambda n: ctx.enter_context(nc.psum_tensor(n, [P, BANK], F32))
        w = sb("w_in", [P, KC, 3072])
        shift, scale = sb("shift1", [P, D]), sb("scale1", [P, D])
        ln_g, ln_b, b_s = sb("ln_g", [P, CW]), sb("ln_b", [P, CW]), sb("b_s", [P, CG])
        w_s, w_sT = sb("w_s", [P, CG, P]), sb("w_sT", [P, CG, P])
        x = sb("x_tile", [P, D])
        h = sb("h_tile", [P, D])
        hT = [sb(f"hT{j}", [P, KC, P]) for j in range(2)]
        pb = sb("pb_tile", [P, 2 * BANK])
        z, zt = sb("z", [P, 2 * CW]), sb("zt", [P, 2 * CW])
        st = sb("stats", [P, 8])
        yc = sb("yc", [P, CW])
        ident, upper = keep["ident"], keep["upper"]
        ps_t = [pt(f"ps_t{n}") for n in range(2)]
        ps_p = [pt(f"ps_p{n}") for n in range(4)]
        ps_s = pt("ps_s")
        w_loaded, consts_in, x_in, ss_ready = sem("w_loaded"), sem("consts_in"), sem("x_in"), sem("ss_ready")
        act_step, dve_step = sem("act_step"), sem("dve_step")
        rstd_ready, h_ready, tr_done, hT_ready = sem("rstd_ready"), sem("h_ready"), sem("tr_done"), sem("hT_ready")
        proj_mm, proj_read, pb_out, x_read = sem("proj_mm"), sem("proj_read"), sem("pb_out"), sem("x_read")
        arg_ready, e_ready, var_in, v_rstd = sem("arg_ready"), sem("e_ready"), sem("var_in"), sem("v_rstd")
        v_ready, sv_mm, yc_ready, yc_out, wsT_done, wsT_mm = sem("v_ready"), sem("sv_mm"), sem("yc_ready"), sem("yc_out"), sem("wsT_done"), sem("wsT_mm")
        z_read, pb_free, yc_free = sem("z_read"), sem("pb_free"), sem("yc_free")
        x_view = io["x"][0]
        block = ctx.enter_context(nc.Block())

        @block.sync
        def _(sp):
            sp.dma_start(shift[:], dr["rows"][:, 0:D].partition_broadcast(P)).then_inc(consts_in, 16)
            sp.dma_start(scale[:], dr["rows"][:, D:2 * D].partition_broadcast(P)).then_inc(consts_in, 16)
            sp.dma_start(w_s[:], io["gmlp_w_s"][0].rearrange("g t s -> t g s")).then_inc(consts_in, 16)
            sp.dma_start(ln_g[:], io["gmlp_ln_g"][0:1, :].partition_broadcast(P)).then_inc(consts_in, 16)
            sp.dma_start(ln_b[:], io["gmlp_ln_b"][0:1, :].partition_broadcast(P)).then_inc(consts_in, 16)
            sp.dma_start(b_s[:], io["gmlp_b_s"][0].rearrange("g t -> t g"), allow_slow_non_contiguous=True).then_inc(consts_in, 16)
            wv = io["w_in"][0].rearrange("(k p) n -> p k n", p=P)
            for k in range(KC):
                sp.dma_start(w[:, k, :], wv[:, k, :]).then_inc(w_loaded, 16)
            with sp.Fori(0, NT) as t:
                sp.wait_ge(x_read, t + 1)
                sp.dma_start(x[:], x_view[bass.ds(t * P, P), :]).then_inc(x_in, 16)
            sp.wait_ge(x_in, 16 * NT)

        @block.gpsimd
        def _(pool):
            pool.sem_inc(pb_free, 1)
            pool.sem_inc(yc_free, 1)
            with pool.Fori(0, NT) as t:
                pool.wait_ge(proj_read, t * GROUPS + 4 + 6)
                pool.dma_start(dr["pb"][bass.ds(t * P + 1, P), :], pb[:]).then_inc(pb_out, 16)
                pool.wait_ge(pb_out, t * 16 + 16)
                pool.sem_inc(pb_free, 1)
                pool.wait_ge(yc_ready, t + 1)
                pool.dma_start(dr["ymix"][bass.ds(t * P, P), AW + BW:D], yc[:]).then_inc(yc_out, 16)
                pool.wait_ge(yc_out, t * 16 + 16)
                pool.sem_inc(yc_free, 1)

        @block.scalar
        def _(act):
            load_exp_and_ln(nc, act)
            step = Steps(act, act_step)
            act.sem_inc(proj_read, 4)
            with act.Fori(0, NT // 2) as i:
                for j in range(2):
                    t = i * 2 + j
                    act.wait_ge(x_in, t * 16 + 16)
                    act.wait_ge(h_ready, t + 1)
                    act.wait_ge(tr_done, t + 1)
                    step.then(act.activation(h[:], x[:], ACT.Square, accum_out=st[:, 0:1]))
                    step.then(act.activation(st[:, 1:2], st[:, 0:1], ACT.Ln, scale=1.0 / D, bias=keep["eps"][:, 0:1]))
                    act.activation(st[:, 2:3], st[:, 1:2], ACT.Exp, scale=-0.5).then_inc(rstd_ready, 1)
                    for g in range(GROUPS):
                        act.wait_ge(proj_mm, i * (2 * GROUPS) + j * GROUPS + g + 1)
                        src = ps_p[(j * GROUPS + g) % 4]
                        if g == 0:
                            act.wait_ge(z_read, t + 1)
                            act.copy(z[:], src[:]).then_inc(proj_read, 1)
                        elif g < 3:
                            dst = (keep["qT"], keep["kT"])[g - 1]
                            act.copy(dst[:, :, bass.ds(t * P, P)], src[:].rearrange("p (h n) -> p h n", h=AH)).then_inc(proj_read, 1)
                        elif g == 3:
                            act.copy(keep["v"][:, bass.ds(t, 1), :], src[:].unsqueeze(1)).then_inc(proj_read, 1)
                        else:
                            act.wait_ge(pb_free, t + 1)
                            act.copy(pb[:, (g - 4) * BANK:(g - 3) * BANK], src[:]).then_inc(proj_read, 1)
                        if g == 1:
                            act.wait_ge(arg_ready, t + 1)
                            act.activation(zt[:], zt[:], ACT.Exp, scale=-1.0).then_inc(e_ready, 1)
                        if g == 2:
                            act.wait_ge(var_in, t + 1)
                            step.then(act.activation(zt[:, 0:CW], z[:, CW:2 * CW], ACT.Square, accum_out=st[:, 5:6]))
                            step.then(act.activation(st[:, 6:7], st[:, 5:6], ACT.Ln, scale=1.0 / CW, bias=keep["eps"][:, 1:2]))
                            act.activation(st[:, 7:8], st[:, 6:7], ACT.Exp, scale=-0.5).then_inc(v_rstd, 1)
                step.restart()

        @block.vector
        def _(dve):
            step = Steps(dve, dve_step)
            for s in (h_ready, x_read, z_read):
                dve.sem_inc(s, 1)
            dve.sem_inc(hT_ready, 2)
            dve.wait_ge(consts_in, 16 * 6)
            dve.wait_ge(wsT_mm, 1)
            dve.tensor_tensor(w_sT[:], ps_t[0][:].rearrange("p (g n) -> p g n", g=CG),
                              upper[:].unsqueeze(1).to_broadcast([P, CG, P]), ALU.mult).then_inc(wsT_done, 1)
            with dve.Fori(0, NT // 2) as i:
                for j in range(2):
                    t = i * 2 + j
                    dve.wait_ge(rstd_ready, t + 1)
                    dve.scalar_tensor_tensor(h[:], x[:], st[:, 2:3], scale[:], ALU.mult, ALU.mult).then_inc(x_read, 1)
                    dve.wait_ge(x_read, t + 2)
                    dve.tensor_tensor(h[:], h[:], shift[:], ALU.add).then_inc(h_ready, 1)
                    for half in range(2):
                        dve.wait_ge(tr_done, t + 2)
                        dve.tensor_copy(hT[j][:, 4 * half:4 * half + 4, :], ps_t[half][:].rearrange("p (k n) -> p k n", k=4)).then_inc(hT_ready, 1)
                    dve.wait_ge(proj_read, i * (2 * GROUPS) + j * GROUPS + 1 + 4)
                    step.then(dve.tensor_tensor(zt[:], z[:], z[:], ALU.mult))
                    step.then(dve.tensor_scalar(zt[:], zt[:], GELU_3, GELU_1, ALU.mult, ALU.add))
                    step.then(dve.tensor_tensor(zt[:], zt[:], z[:], ALU.mult))
                    dve.tensor_scalar(zt[:], zt[:], -80.0, None, ALU.max).then_inc(arg_ready, 1)
                    dve.wait_ge(e_ready, t + 1)
                    step.then(dve.tensor_scalar(zt[:], zt[:], 1.0, None, ALU.add))
                    step.then(dve.reciprocal(zt[:], zt[:]))
                    step.then(dve.tensor_tensor(z[:], z[:], zt[:], ALU.mult))
                    v = z[:, CW:2 * CW]
                    step.then(dve.tensor_reduce(st[:, 3:4], v, AX.X, ALU.add))
                    step.then(dve.tensor_scalar(st[:, 4:5], st[:, 3:4], -1.0 / CW, None, ALU.mult))
                    dve.tensor_scalar(v, v, st[:, 4:5], None, ALU.add).then_inc(var_in, 1)
                    dve.wait_ge(v_rstd, t + 1)
                    step.then(dve.scalar_tensor_tensor(v, v, st[:, 7:8], ln_g[:], ALU.mult, ALU.mult))
                    dve.tensor_tensor(v, v, ln_b[:], ALU.add).then_inc(v_ready, 1)
                    dve.wait_ge(sv_mm, t + 1)
                    dve.wait_ge(yc_free, t + 1)
                    for g in range(CG):
                        c = slice(g * CD, (g + 1) * CD)
                        step.then(dve.scalar_tensor_tensor(yc[:, c], ps_s[:, c], b_s[:, g:g + 1], z[:, c], ALU.add, ALU.mult))
                    dve.sem_inc(z_read, 1)
                    dve.sem_inc(yc_ready, 1)
                step.restart()

        @block.tensor
        def _(pe):
            for s in (tr_done,):
                pe.sem_inc(s, 1)
            pe.wait_ge(consts_in, 16 * 6)
            for g in range(CG):
                mm = pe.transpose(ps_t[0][:, g * P:(g + 1) * P], w_s[:, g, :], ident[:])
            mm.then_inc(wsT_mm, 1)
            pe.wait_ge(wsT_done, 1)
            pe.wait_ge(w_loaded, 16 * KC)
            cols = [A_COLS + B_COLS, 0, AW, 2 * AW, A_COLS, A_COLS + BANK]
            with pe.Fori(0, NT // 2) as i:
                for j in range(2):
                    t = i * 2 + j
                    pe.wait_ge(h_ready, t + 2)
                    if True:
                        pe.wait_ge(hT_ready, t * 2 + 2)
                    for k in range(KC):
                        tr = pe.transpose(ps_t[k // 4][:, (k % 4) * P:(k % 4 + 1) * P], h[:, k * P:(k + 1) * P], ident[:])
                    tr.then_inc(tr_done, 1)
                    pe.wait_ge(hT_ready, t * 2 + 4)
                    for g in range(GROUPS):
                        out = ps_p[(j * GROUPS + g) % 4]
                        pe.wait_ge(proj_read, i * (2 * GROUPS) + j * GROUPS + g + 1)
                        if g in (1, 2):
                            for c in range(AH):
                                for k in range(KC):
                                    mm = pe.matmul(out[:, c * P:(c + 1) * P], w[:, k, cols[g] + c * P:cols[g] + (c + 1) * P], hT[j][:, k, :],
                                                   start=(k == 0), stop=(k == KC - 1))
                        else:
                            for k in range(KC):
                                mm = pe.matmul(out[:], hT[j][:, k, :], w[:, k, cols[g]:cols[g] + BANK], start=(k == 0), stop=(k == KC - 1))
                        mm.then_inc(proj_mm, 1)
                    pe.wait_ge(v_ready, t + 1)
                    pe.wait_ge(z_read, t + 1)
                    for g in range(CG):
                        mm = pe.matmul(ps_s[:, g * CD:(g + 1) * CD], w_sT[:, g, :], z[:, CW + g * CD:CW + (g + 1) * CD], start=True, stop=True)
                    mm.then_inc(sv_mm, 1)


LAMBDA_INIT = 0.8 - 0.6 * math.exp(-0.3 * 0)
N_BUCKETS, MAX_DISTANCE = 32, 128
NEG = -1e30


def load_exp_and_ln(nc, act):
    act.add_instruction(mybir.InstLoadActFuncSet(act_func_set_id=EXP_AND_LN, name=nc.get_next_instruction_name(),
                                                 engine=mybir.EngineType.Activation))


class Stages:

    def __init__(self, sem, names):
        self.sem, self.names, self.n = sem, names, len(names)
        self.built = 0

    def start(self, eng):
        eng.sem_inc(self.sem, self.n)

    def done(self, ins, name):
        assert self.names[self.built % self.n] == name, (name, self.names[self.built % self.n])
        self.built += 1
        return ins.then_inc(self.sem, 1)

    def wait(self, eng, turn, name):
        eng.wait_ge(self.sem, turn * self.n + self.n + self.names.index(name) + 1)

    def wait_before(self, eng, turn, name):
        eng.wait_ge(self.sem, turn * self.n + self.names.index(name) + 1)


def attend(nc, io, dr, keep):
    with ExitStack() as ctx:
        sb = lambda n, s: ctx.enter_context(nc.sbuf_tensor(n, s, F32))
        sem = lambda n: ctx.enter_context(nc.semaphore(n))
        pt = lambda n, b=1: ctx.enter_context(nc.psum_tensor(n, [P, b * BANK], F32))
        ident = keep["ident"]
        table, oh = sb("table", [N_BUCKETS + 1, AH]), sb("onehot", [N_BUCKETS + 1, 3 * P])
        rv = sb("bias_rows", [P, AH, 3 * P])
        table_b = sb("table_b", [N_BUCKETS + 1, AH, P])
        bias = sb("bias", [P, AH, 2 * P])
        lp, lam = sb("lambda_par", [P, 4, AQK]), sb("lambda", [P, 4])
        gain = sb("subln", [P, 2 * AQK])
        q, k, v = sb("q_head", [P, S]), sb("k_head", [P, S]), sb("v_head", [P, NT, P])
        p = [[sb(f"p{b}{m}", [P, S]) for m in range(2)] for b in range(2)]
        attn = [sb(f"attn{b}", [P, S]) for b in range(2)]
        aT = [sb(f"attnT{b}", [P, NT, P]) for b in range(2)]
        o = [sb(f"o{b}", [P, P]) for b in range(2)]
        junk = sb("squares", [P, P])
        st = [sb(f"soft_stats{b}", [P, 12]) for b in range(3)]
        ps_s = [pt(f"ps_scores{m}", 2) for m in range(2)]
        ps_t = [pt(f"ps_attnT{b}") for b in range(2)]
        ps_o = [pt(f"ps_o{b}") for b in range(2)]
        consts_in, table_done, rv_mm, rv_ready, rv_out, bias_in = (sem(n) for n in (
            "att_consts_in", "table_done", "rv_mm", "rv_ready", "rv_out", "bias_in"))
        lam_dot, lam_exp, gain_done, dve_step, act_step, o_out = (sem(n) for n in (
            "lam_dot", "lam_exp", "gain_done", "att_dve_step", "att_act_step", "o_out"))
        heads_in = sem("head_copied")
        s_mm = sem("scores_mm")
        s_max = sem("scores_max")
        s_exp = sem("scores_exp")
        a_ready = sem("attn_ready")
        t_mm = sem("attnT_mm")
        t_read = sem("attnT_copied")
        o_mm = sem("o_mm")
        o_rstd = sem("o_rstd")
        o_free = sem("o_free")
        o_ready = sem("o_ready")
        halves = lambda n: [(a, min(a + 4, n + 1)) for a in range(0, n + 1, 4)]
        T_HEAD = sum(len(halves(n)) for n in range(NT))
        t_before = lambda n: sum(len(halves(m)) for m in range(n))
        block = ctx.enter_context(nc.Block())

        @block.sync
        def _(sp):
            sp.dma_start(table[0:N_BUCKETS, :], io["rel_bias_table"]).then_inc(consts_in, 16)
            sp.dma_start(oh[:], io["c_onehot"]).then_inc(consts_in, 16)
            sp.dma_start(lp[:], io["diff_lambda"].rearrange("l a b -> l (a b)").partition_broadcast(P)).then_inc(consts_in, 16)
            sp.dma_start(gain[:], io["diff_subln"][0:1, :].partition_broadcast(P)).then_inc(consts_in, 16)
            sp.wait_ge(rv_ready, 1)
            sp.dma_start(dr["bias_by_dist"].rearrange("h p n -> p h n"), rv[:]).then_inc(rv_out, 16)
            sp.wait_ge(rv_out, 16)
            t = dr["bias_by_dist"]
            for h in range(AH):
                src = bass.AP(t.tensor, h * P * 3 * P + P - 1, [[3 * P - 1, P], [1, 2 * P]])
                sp.dma_start(bias[:, h, :], src).then_inc(bias_in, 16)
            sp.sem_inc(o_free, 2)
            with sp.Fori(0, AH) as h:
                for n in range(NT):
                    sp.wait_ge(o_ready, h * NT + n + 1)
                    sp.dma_start(dr["ymix"][n * P:(n + 1) * P, bass.ds(h * P, P)], o[n % 2][:]).then_inc(o_out, 16)
                    sp.wait_ge(o_out, (h * NT + n) * 16 + 16)
                    sp.sem_inc(o_free, 1)

        @block.scalar
        def _(act):
            load_exp_and_ln(nc, act)
            step = Steps(act, act_step)
            act.sem_inc(t_read, 2)
            act.sem_inc(s_exp, 2)
            act.wait_ge(lam_dot, 1)
            act.activation(lam[:, 2:4], lam[:, 0:2], ACT.Exp).then_inc(lam_exp, 1)
            with act.Fori(0, AH) as h:
                act.wait_ge(o_mm, h * NT + 1)
                act.mul(q[:], keep["qT"][:, bass.ds(h, 1), :].squeeze(1), AQK ** -0.5).then_inc(heads_in, 1)
                act.copy(k[:], keep["kT"][:, bass.ds(h, 1), :].squeeze(1)).then_inc(heads_in, 1)
                act.copy(v[:], keep["v"][:, :, bass.ds(h * P, P)]).then_inc(heads_in, 1)
                for it in range(NT + 2):
                    if it < NT:
                        n, b, L = it, it % 2, (it + 1) * P
                        if n >= 2:
                            act.wait_ge(a_ready, h * NT + n - 1)
                        for m in range(2):
                            act.wait_ge(s_max, h * (2 * NT) + 2 * n + m + 1)
                            act.activation(p[b][m][:, 0:L], ps_s[m][:, 0:L], ACT.Exp, bias=st[n % 3][:, m:m + 1],
                                           accum_out=st[n % 3][:, 2 + m:3 + m]).then_inc(s_exp, 1)
                    if 1 <= it <= NT:
                        n = it - 1
                        if n >= 2:
                            act.wait_ge(o_mm, h * NT + n - 1 + 1)
                        for x, (a, z) in enumerate(halves(n)):
                            c = t_before(n) + x
                            act.wait_ge(t_mm, h * T_HEAD + c + 1)
                            act.copy(aT[n % 2][:, a:z, :], ps_t[c % 2][:, 0:(z - a) * P].rearrange("p (a n) -> p a n", n=P)).then_inc(t_read, 1)
                    if it >= 2:
                        n = it - 2
                        s = st[n % 3]
                        act.wait_ge(o_mm, h * NT + n + 1 + 1)
                        step.then(act.activation(junk[:], ps_o[n % 2][:, 0:P], ACT.Square, accum_out=s[:, 8:9]))
                        step.then(act.activation(s[:, 9:10], s[:, 8:9], ACT.Ln, scale=1.0 / P, bias=keep["eps"][:, 0:1]))
                        act.activation(s[:, 10:11], s[:, 9:10], ACT.Exp, scale=-0.5).then_inc(o_rstd, 1)
                step.restart()

        @block.vector
        def _(dve):
            step = Steps(dve, dve_step)
            dve.memset(table[N_BUCKETS:N_BUCKETS + 1, :], NEG).then_inc(table_done, 1)
            dve.wait_ge(consts_in, 64)
            dve.wait_ge(table_done, 1)
            dve.tensor_copy(table_b[:], table[:].unsqueeze(2).to_broadcast([N_BUCKETS + 1, AH, P])).then_inc(table_done, 1)
            step.then(dve.tensor_tensor(lp[:, 0, :], lp[:, 0, :], lp[:, 1, :], ALU.mult))
            step.then(dve.tensor_tensor(lp[:, 2, :], lp[:, 2, :], lp[:, 3, :], ALU.mult))
            step.then(dve.tensor_reduce(lam[:, 0:1], lp[:, 0, :], AX.X, ALU.add))
            dve.tensor_reduce(lam[:, 1:2], lp[:, 2, :], AX.X, ALU.add).then_inc(lam_dot, 1)
            dve.wait_ge(lam_exp, 1)
            step.then(dve.tensor_tensor(lam[:, 0:1], lam[:, 3:4], lam[:, 2:3], ALU.subtract))
            step.then(dve.tensor_scalar(lam[:, 0:1], lam[:, 0:1], -LAMBDA_INIT, None, ALU.add))
            step.then(dve.tensor_scalar(gain[:], gain[:], 1.0 - LAMBDA_INIT, None, ALU.mult))
            dve.wait_ge(rv_mm, 1)
            rv_ps = [ps_s[0][:, 0:BANK], ps_s[0][:, BANK:], ps_s[1][:, 0:BANK], ps_s[1][:, BANK:]]
            for h in range(AH):
                q = dve.tensor_copy(rv[:, h, :], rv_ps[h][:, 0:3 * P])
            step.then(q)
            for h in range(AH):
                q = dve.tensor_scalar(rv[:, h, 1:], rv[:, h, 1:], rv[:, h, 0:1], None, ALU.subtract)
            step.then(q)
            dve.memset(rv[:, :, 0:1], 0.0).then_inc(rv_ready, 1)
            dve.wait_ge(bias_in, 16 * AH)
            step.restart()
            with dve.Fori(0, AH) as h:
                for it in range(NT + 2):
                    if it < NT:
                        n, s, L = it, st[it % 3], (it + 1) * P
                        w = min(L, 2 * P)
                        if n >= 3:
                            dve.wait_ge(o_ready, h * NT + n - 2)
                        for m in range(2):
                            dve.wait_ge(s_mm, h * (2 * NT) + 2 * n + m + 1)
                            near = ps_s[m][:, L - w:L]
                            step.then(dve.tensor_tensor(near, near, bias[:, bass.ds(h, 1), 2 * P - w:2 * P].squeeze(1), ALU.add))
                            dve.tensor_reduce(s[:, m:m + 1], ps_s[m][:, 0:L], AX.X, ALU.max, negate=True).then_inc(s_max, 1)
                    if 1 <= it <= NT:
                        n, b, s, L = it - 1, (it - 1) % 2, st[(it - 1) % 3], it * P
                        dve.wait_ge(s_exp, h * (2 * NT) + 2 * n + 2 + 2)
                        if n >= 2:
                            dve.wait_ge(t_mm, h * T_HEAD + t_before(n - 1))
                        step.then(dve.reciprocal(s[:, 4:6], s[:, 2:4]))
                        step.then(dve.tensor_tensor(s[:, 6:7], s[:, 5:6], lam[:, 0:1], ALU.mult))
                        step.then(dve.tensor_scalar(attn[b][:, 0:L], p[b][0][:, 0:L], s[:, 4:5], None, ALU.mult))
                        dve.scalar_tensor_tensor(attn[b][:, 0:L], p[b][1][:, 0:L], s[:, 6:7], attn[b][:, 0:L], ALU.mult, ALU.add).then_inc(a_ready, 1)
                    if it >= 2:
                        n = it - 2
                        dve.wait_ge(o_rstd, h * NT + n + 1)
                        dve.wait_ge(o_free, h * NT + n + 1)
                        dve.scalar_tensor_tensor(o[n % 2][:], ps_o[n % 2][:, 0:P], st[n % 3][:, 10:11], gain[:], ALU.mult, ALU.mult).then_inc(o_ready, 1)
                step.restart()

        @block.tensor
        def _(pe):
            pe.sem_inc(o_mm, 1)
            pe.wait_ge(consts_in, 64)
            pe.wait_ge(table_done, 2)
            for h in range(AH):
                mm = pe.matmul(ps_s[h // 2][:, (h % 2) * BANK:(h % 2) * BANK + 3 * P], table_b[:, h, :], oh[:], start=True, stop=True)
            mm.then_inc(rv_mm, 1)
            pe.wait_ge(rv_ready, 1)
            with pe.Fori(0, AH) as h:
                pe.wait_ge(heads_in, h * 3 + 3)
                for it in range(NT + 1):
                    if it < NT:
                        n, L = it, (it + 1) * P
                        for m in range(2):
                            pe.wait_ge(s_exp, h * (2 * NT) + 2 * n + m - 2 + 1 + 2)
                            r = slice(m * AQK, (m + 1) * AQK)
                            for a in range(0, L, BANK):
                                z = min(a + BANK, L)
                                mm = pe.matmul(ps_s[m][:, a:z], q[r, n * P:(n + 1) * P], k[r, a:z], start=True, stop=True)
                            mm.then_inc(s_mm, 1)
                    if it >= 1:
                        n = it - 1
                        pe.wait_ge(a_ready, h * NT + n + 1)
                        for x, (a, z) in enumerate(halves(n)):
                            c = t_before(n) + x
                            pe.wait_ge(t_read, h * T_HEAD + c + 1)
                            for kt in range(a, z):
                                tr = pe.transpose(ps_t[c % 2][:, (kt - a) * P:(kt - a + 1) * P], attn[n % 2][:, kt * P:(kt + 1) * P], ident[:])
                            tr.then_inc(t_mm, 1)
                        if n >= 2:
                            pe.wait_ge(o_ready, h * NT + n - 1)
                        for x, (a, z) in enumerate(halves(n)):
                            pe.wait_ge(t_read, h * T_HEAD + t_before(n) + x + 1 + 2)
                            for kt in range(a, z):
                                mm = pe.matmul(ps_o[n % 2][:, 0:P], aT[n % 2][:, kt, :], v[:, kt, :], start=(kt == 0), stop=(kt == n))
                        mm.then_inc(o_mm, 1)


class Lane:

    def __init__(self, sb, bank, j):
        f = lambda n, *s: sb(f"{n}{j}", [P, *s])
        self.bank = bank[4 * j:4 * j + 4]
        self.cur, self.prev, self.p = f("pb_cur", B_COLS), f("pb_prev", B_COLS), f("p_mixed", B_COLS)
        self.lr, self.lrT = f("low_rank", 2 * P), f("low_rankT", 2 * P)
        self.wa, self.g, self.lw, self.cx = f("w_a", 2 * BW), f("gate", BW), f("log_decay", BW), f("cum_before", BW)
        self.kk, self.k2, self.tmp = f("kk", BW), f("k2", BW), f("tmp", BW)
        self.s4 = f("per_head", 8, BH)
        self.dec = f("decays", 3, BW)
        self.fs = f("state_factors", 4)
        self.ops = f("operands", 4, BW)
        self.arT, self.bkT = f("arT", 2, 2, P), f("bkT", 2, 2, P)
        self.gm = f("grams", BH, 4, P)
        self.A = f("A_ab", BH, P)
        self.Dm, self.DT, self.T, self.TT, self.Z, self.ZT = (f(n, BH, P) for n in ("pow", "powT", "T", "TT", "Z", "ZT"))
        self.O, self.OT = [f(f"off{n}_", BH, P) for n in range(3)], [f(f"offT{n}_", BH, P) for n in range(2)]
        self.Xs, self.Us, self.taT = f("X", BW), f("U", BW), f("taT", 2, P)
        self.Sc = f("state_mid", 2, BD)
        self.ys, self.yq, self.yo = f("y", BW), f("y_sq", BW), f("y_out", BW)

    def b4(self, n):
        return self.bank[n][:].rearrange("p (h n) -> p h n", h=BH)

    def bank_pair(self, n):
        return self.bank[n][:, 0:2 * BD].rearrange("p (a d) -> p a d", d=BD)


def in_lanes(*groups):
    return [f"{n}.{j}" for group in groups for j in range(2) for n in group.split()]


def rwkv(nc, io, dr, keep):
    HALF = math.exp(-0.5)
    TURNS = NT // 2
    with ExitStack() as ctx:
        sb = lambda n, s: ctx.enter_context(nc.sbuf_tensor(n, s, F32))
        sem = lambda n: ctx.enter_context(nc.semaphore(n))
        bank = [ctx.enter_context(nc.psum_tensor(f"bank{n}", [P, BANK], F32)) for n in range(8)]
        ident = keep["ident"]
        H4 = [P, BH, P]
        mu = sb("mu", [P, B_COLS])
        wa0 = sb("w0_a0", [P, 2 * BW])
        k_k, k_a, r_k, lnx_g, lnx_b = (sb(n, [P, BW]) for n in ("k_k", "k_a", "r_k", "lnx_g", "lnx_b"))
        wa2, g2 = sb("w2_a2", [P, BW]), sb("g2", [P, BW])
        mask4 = sb("mask4", [P, 4, P])
        masks = sb("masks", [P, 9, P])
        cum_m, halves_m = sb("cum_m", [P, P]), sb("halves_m", [P, 2])
        lane = [Lane(sb, bank, j) for j in range(2)]
        St = sb("state", [P, 2, BD])
        zero = sb("zero_row", [1, B_COLS])
        consts_in, zero_done, zero_out, pool_done, dve_step, act_step = (sem(n) for n in (
            "rwkv_consts_in", "zero_done", "zero_out", "offs_done", "rwkv_dve_step", "rwkv_act_step"))
        load_in, y_out, y_free = ([sem(f"{n}{j}") for j in range(2)] for n in ("pb_in", "y_out", "y_free"))
        PE = Stages(sem("pe_done"), in_lanes("lr_T", "lora", "cum", "operands_T", "grams", "A", "X", "sq0", "sq1", "sq2", "sq3",
                                             "z0", "m0", "z1", "m1", "z2", "m2", "ta", "U Y state"))
        V = Stages(sem("dve_done"), in_lanes("mixed lr_args", "lr", "wa", "logw kk_ss", "cx", "operands", "masked", "D0",
                                             "v0", "v1", "v2", "v3", "vz0", "vm0", "vz1", "vm1", "vz2", "vm2", "Sc U state", "var", "y"))
        C = Stages(sem("act_done"), in_lanes("lr_exp", "lrT", "g", "wa_exp", "kk_rstd", "decays", "opsT", "X", "c0", "c1", "c2",
                                             "cz0", "cz1", "ta", "y", "rstd"))
        h3 = lambda x: x.rearrange("p (h d) -> p h d", h=BH)
        hc = lambda h: slice(h * BD, (h + 1) * BD)
        half = lambda h: slice(64 * (h % 2), 64 * (h % 2) + 64)
        bc = lambda col: col.unsqueeze(2).to_broadcast([P, BH, BD])
        mb = lambda n: masks[:, n, :].unsqueeze(1).to_broadcast(H4)
        ib = ident[:].unsqueeze(1).to_broadcast(H4)
        by_parity = lambda x, e: x[:].rearrange("p (a e d) -> p e a d", e=2, d=BD)[:, e]
        pr = lambda n: io[n][0:1, :].partition_broadcast(P)
        block = ctx.enter_context(nc.Block())

        @block.sync
        def _(sp):
            for dst, src in ((mu[:], pr("rwkv_mu")), (wa0[:, 0:BW], pr("rwkv_w0")), (wa0[:, BW:], pr("rwkv_a0")),
                             (k_k[:], pr("rwkv_k_k")), (k_a[:], pr("rwkv_k_a")),
                             (r_k[:], io["rwkv_r_k"].rearrange("l a b -> l (a b)").partition_broadcast(P)),
                             (lnx_g[:], pr("rwkv_lnx_g")), (lnx_b[:], pr("rwkv_lnx_b")),
                             (wa2[0:64, :], io["rwkv_w2"][0]), (wa2[64:128, :], io["rwkv_a2"][0]), (g2[:], io["rwkv_g2"][0]),
                             (mask4[:], io["c_mask4"]), (masks[:], io["c_masks"]), (cum_m[:], io["c_cum"]), (halves_m[:], io["c_halves"])):
                sp.dma_start(dst, src).then_inc(consts_in, 16)
            sp.wait_ge(zero_done, 1)
            sp.dma_start(dr["pb"][0:1, :], zero[:]).then_inc(zero_out, 16)
            sp.wait_ge(zero_out, 16)
            with sp.Fori(0, TURNS) as i:
                for j in range(2):
                    V.wait_before(sp, i, f"mixed.{j}")
                    sp.dma_start(lane[j].cur[:], dr["pb"][bass.ds((i * 2 + j) * P + 1, P), :]).then_inc(load_in[j], 16)
                    sp.dma_start(lane[j].prev[:], dr["pb"][bass.ds((i * 2 + j) * P, P), :]).then_inc(load_in[j], 16)
            for j in range(2):
                sp.wait_ge(load_in[j], 32 * TURNS)

        @block.gpsimd
        def _(pool):
            for j in range(2):
                pool.sem_inc(y_free[j], 1)
            pool.wait_ge(consts_in, 16 * 15)
            with pool.Fori(0, TURNS) as i:
                for j in range(2):
                    w = lane[j]
                    V.wait(pool, i, f"D0.{j}")
                    PE.wait_before(pool, i, f"m2.{j}")
                    for n in range(3):
                        pool.tensor_tensor(w.O[n][:], w.A[:], mb(3 + 2 * n), ALU.mult).then_inc(pool_done, 1)
                        if n < 2:
                            pool.tensor_tensor(w.OT[n][:], w.gm[:, :, 0, :], mb(4 + 2 * n), ALU.mult).then_inc(pool_done, 1)
                for j in range(2):
                    V.wait(pool, i, f"y.{j}")
                    pool.dma_start(dr["ymix"][bass.ds((i * 2 + j) * P, P), AW:AW + BW], lane[j].yo[:]).then_inc(y_out[j], 16)
                for j in range(2):
                    pool.wait_ge(y_out[j], i * 16 + 16)
                    pool.sem_inc(y_free[j], 1)

        @block.scalar
        def _(act):
            load_exp_and_ln(nc, act)
            step = Steps(act, act_step)
            C.start(act)
            with act.Fori(0, TURNS) as i:
                for j in range(2):
                    w = lane[j]
                    V.wait(act, i, f"lr_args.{j}")
                    C.done(act.activation(w.lr[:], w.lr[:], ACT.Exp, scale=-1.0), f"lr_exp.{j}")
                for j in range(2):
                    w = lane[j]
                    PE.wait(act, i, f"lr_T.{j}")
                    C.done(act.copy(w.lrT[:], w.bank[0][:, 0:2 * P]), f"lrT.{j}")
                for j in range(2):
                    w = lane[j]
                    PE.wait(act, i, f"lora.{j}")
                    V.wait_before(act, i, f"y.{j}")
                    C.done(act.copy(w.g[:], w.bank[3][:, 0:BW]), f"g.{j}")
                for j in range(2):
                    w = lane[j]
                    V.wait(act, i, f"wa.{j}")
                    C.done(act.activation(w.wa[:], w.wa[:], ACT.Exp, scale=-1.0), f"wa_exp.{j}")
                for j in range(2):
                    w = lane[j]
                    V.wait(act, i, f"kk_ss.{j}")
                    step.then(act.activation(w.s4[:, 1, :], w.s4[:, 0, :], ACT.Ln))
                    C.done(act.activation(w.s4[:, 2, :], w.s4[:, 1, :], ACT.Exp, scale=-0.5), f"kk_rstd.{j}")
                for j in range(2):
                    w = lane[j]
                    V.wait(act, i, f"cx.{j}")
                    PE.wait(act, i, f"cum.{j}")
                    act.activation(w.dec[:, 0, :], w.bank[1][:, 0:BW], ACT.Exp)
                    act.activation(w.dec[:, 1, :], w.bank[1][:, 0:BW], ACT.Exp, scale=-1.0)
                    act.activation(w.dec[:, 2, :], w.cx[:], ACT.Exp)
                    C.done(act.activation(w.fs[:], w.bank[2][:, 0:4], ACT.Exp), f"decays.{j}")
                for j in range(2):
                    w = lane[j]
                    PE.wait(act, i, f"operands_T.{j}")
                    act.copy(w.arT[:], w.bank[0][:].rearrange("p (a b n) -> p a b n", a=2, b=2))
                    C.done(act.copy(w.bkT[:], w.bank[3][:].rearrange("p (a b n) -> p a b n", a=2, b=2)), f"opsT.{j}")
                for j in range(2):
                    w = lane[j]
                    PE.wait(act, i, f"X.{j}")
                    C.done(act.copy(w.Xs[:], w.bank[3][:, 0:BW]), f"X.{j}")
                for n in range(3):
                    for j in range(2):
                        w = lane[j]
                        PE.wait(act, i, f"sq{n}.{j}")
                        C.done(act.copy(w.Dm[:], w.b4(0)), f"c{n}.{j}")
                for n in range(2):
                    for j in range(2):
                        w = lane[j]
                        PE.wait(act, i, f"z{n}.{j}")
                        C.done(act.copy(w.Z[:], w.b4(0)), f"cz{n}.{j}")
                for j in range(2):
                    w = lane[j]
                    PE.wait(act, i, f"ta.{j}")
                    C.done(act.copy(w.taT[:], w.bank[0][:, 0:2 * P].rearrange("p (a n) -> p a n", a=2)), f"ta.{j}")
                for j in range(2):
                    w = lane[j]
                    PE.wait(act, i, f"Y.{j}")
                    step.then(act.copy(by_parity(w.ys, 0), w.bank_pair(3)))
                    C.done(act.copy(by_parity(w.ys, 1), w.bank_pair(0)), f"y.{j}")
                for j in range(2):
                    w = lane[j]
                    V.wait(act, i, f"var.{j}")
                    step.then(act.activation(w.s4[:, 6, :], w.s4[:, 5, :], ACT.Ln, scale=1.0 / BD, bias=keep["eps"][:, 2:3]))
                    C.done(act.activation(w.s4[:, 7, :], w.s4[:, 6, :], ACT.Exp, scale=-0.5), f"rstd.{j}")
                step.restart()

        @block.vector
        def _(dve):
            step = Steps(dve, dve_step)
            tt = dve.tensor_tensor
            V.start(dve)
            dve.memset(zero[:], 0.0).then_inc(zero_done, 1)
            step.then(dve.memset(St[:], 0.0))
            dve.wait_ge(consts_in, 16 * 15)
            step.restart()
            with dve.Fori(0, TURNS) as i:
                for j in range(2):
                    w = lane[j]
                    dve.wait_ge(load_in[j], i * 32 + 32)
                    step.then(tt(w.prev[:], w.prev[:], w.cur[:], ALU.subtract))
                    step.then(tt(w.prev[:], w.prev[:], mu[:], ALU.mult))
                    PE.wait_before(dve, i, f"state.{j}")
                    V.done(tt(w.p[:], w.prev[:], w.cur[:], ALU.add), f"mixed.{j}")
                    V.wait(dve, i, f"mixed.{j}")
                    PE.wait_before(dve, i, f"lr_T.{j}")
                    step.then(dve.tensor_scalar(w.lr[:, 0:64], w.p[:, 3 * BW:3 * BW + 64], 2.0, -80.0, ALU.mult, ALU.max))
                    step.then(dve.tensor_scalar(w.lr[:, 64:128], w.p[:, 3 * BW + 64:3 * BW + 128], 0.0, None, ALU.mult))
                    V.done(dve.tensor_scalar(w.lr[:, 128:256], w.p[:, 3 * BW + 128:], -80.0, None, ALU.max), f"lr_args.{j}")
                for j in range(2):
                    w = lane[j]
                    C.wait(dve, i, f"lr_exp.{j}")
                    step.then(dve.tensor_scalar(w.lr[:], w.lr[:], 1.0, None, ALU.add))
                    step.then(dve.reciprocal(w.lr[:], w.lr[:]))
                    step.then(dve.tensor_scalar(w.lr[:, 0:64], w.lr[:, 0:64], 2.0, -1.0, ALU.mult, ALU.add))
                    V.done(dve.tensor_copy(w.lr[:, 64:128], w.p[:, 3 * BW + 64:3 * BW + 128]), f"lr.{j}")
                for j in range(2):
                    w = lane[j]
                    PE.wait(dve, i, f"lora.{j}")
                    step.then(tt(w.wa[:, 0:BW], w.bank[1][:, 0:BW], wa0[:, 0:BW], ALU.add))
                    step.then(tt(w.wa[:, BW:], w.bank[2][:, 0:BW], wa0[:, BW:], ALU.add))
                    V.done(dve.tensor_scalar(w.wa[:], w.wa[:], -80.0, None, ALU.max), f"wa.{j}")
                for j in range(2):
                    w = lane[j]
                    C.wait(dve, i, f"wa_exp.{j}")
                    step.then(dve.tensor_scalar(w.wa[:], w.wa[:], 1.0, None, ALU.add))
                    step.then(dve.reciprocal(w.wa[:], w.wa[:]))
                    V.done(dve.tensor_scalar(w.lw[:], w.wa[:, 0:BW], -HALF, None, ALU.mult), f"logw.{j}")
                    step.then(tt(w.kk[:], w.p[:, BW:2 * BW], k_k[:], ALU.mult))
                    step.then(tt(w.tmp[:], w.kk[:], w.kk[:], ALU.mult))
                    step.then(dve.tensor_reduce(w.s4[:, 3, :], h3(w.tmp[:]), AX.X, ALU.add))
                    V.done(dve.tensor_scalar(w.s4[:, 0, :], w.s4[:, 3, :], 1e-24, None, ALU.max), f"kk_ss.{j}")
                for j in range(2):
                    w = lane[j]
                    PE.wait(dve, i, f"cum.{j}")
                    V.done(tt(w.cx[:], w.bank[1][:, 0:BW], w.lw[:], ALU.subtract), f"cx.{j}")
                for j in range(2):
                    w = lane[j]
                    a_, r_, k_ = w.wa[:, BW:], w.p[:, 0:BW], w.p[:, BW:2 * BW]
                    step.then(dve.scalar_tensor_tensor(w.k2[:], a_, -1.0, k_a[:], ALU.add, ALU.mult))
                    step.then(dve.scalar_tensor_tensor(w.k2[:], w.k2[:], 1.0, k_, ALU.add, ALU.mult))
                    C.wait(dve, i, f"kk_rstd.{j}")
                    step.then(tt(h3(w.kk[:]), h3(w.kk[:]), bc(w.s4[:, 2, :]), ALU.mult))
                    C.wait(dve, i, f"decays.{j}")
                    step.then(dve.scalar_tensor_tensor(w.ops[:, 0, :], w.kk[:], -1.0, w.dec[:, 2, :], ALU.mult, ALU.mult))
                    step.then(tt(w.ops[:, 1, :], r_, w.dec[:, 0, :], ALU.mult))
                    step.then(tt(w.tmp[:], w.kk[:], a_, ALU.mult))
                    step.then(tt(w.ops[:, 2, :], w.tmp[:], w.dec[:, 1, :], ALU.mult))
                    V.done(tt(w.ops[:, 3, :], w.k2[:], w.dec[:, 1, :], ALU.mult), f"operands.{j}")
                for j in range(2):
                    w = lane[j]
                    PE.wait(dve, i, f"grams.{j}")
                    dve.wait_ge(pool_done, i * 10 + 5 * j + 5)
                    for h in range(BH):
                        q = tt(w.gm[:, h, :, :], w.b4(h), mask4[:], ALU.mult)
                        if h < BH - 1:
                            step.then(q)
                    V.done(q, f"masked.{j}")
                for j in range(2):
                    w = lane[j]
                    V.wait(dve, i, f"masked.{j}")
                    step.then(tt(w.DT[:], w.gm[:, :, 0, :], mb(2), ALU.mult))
                    step.then(tt(w.TT[:], w.DT[:], ib, ALU.add))
                    PE.wait(dve, i, f"A.{j}")
                    ho = lambda x, e: x.rearrange("p (a e) n -> p e a n", e=2)[:, e]
                    ml = masks[:, 0, :].unsqueeze(1).to_broadcast([P, 2, P])
                    for e in range(2):
                        step.then(tt(ho(w.A[:], e), w.bank[e][:, 0:2 * P].rearrange("p (a n) -> p a n", a=2), ml, ALU.mult))
                    step.then(tt(w.Dm[:], w.A[:], mb(1), ALU.mult))
                    V.done(tt(w.T[:], w.Dm[:], ib, ALU.add), f"D0.{j}")
                for n in range(4):
                    for j in range(2):
                        w = lane[j]
                        PE.wait(dve, i, f"sq{n}.{j}")
                        if n > 0:
                            step.then(tt(w.T[:], w.T[:], w.b4(1), ALU.add))
                            q = tt(w.TT[:], w.TT[:], w.b4(3), ALU.add)
                        if n < 3:
                            if n > 0:
                                step.then(q)
                            q = dve.tensor_copy(w.DT[:], w.b4(2))
                        V.done(q, f"v{n}.{j}")
                    if n == 0:
                        for j in range(2):
                            w = lane[j]
                            step.then(tt(w.tmp[:], w.p[:, 0:BW], w.k2[:], ALU.mult))
                            step.then(tt(w.tmp[:], w.tmp[:], r_k[:], ALU.mult))
                            step.then(dve.tensor_reduce(w.s4[:, 4, :], h3(w.tmp[:]), AX.X, ALU.add))
                for n in range(3):
                    for j in range(2):
                        w = lane[j]
                        PE.wait(dve, i, f"z{n}.{j}")
                        V.done(dve.tensor_copy(w.ZT[:], w.b4(2)), f"vz{n}.{j}")
                    for j in range(2):
                        w = lane[j]
                        PE.wait(dve, i, f"m{n}.{j}")
                        if n < 2:
                            step.then(tt(w.T[:], w.T[:], w.b4(1), ALU.add))
                        V.done(tt(w.TT[:], w.TT[:], w.b4(3), ALU.add), f"vm{n}.{j}")
                for j in range(2):
                    w = lane[j]
                    f = lambda n: w.fs[:].rearrange("p (a b) -> p b a", b=2)[:, n].unsqueeze(2).to_broadcast([P, 2, BD])
                    V.done(tt(w.Sc[:], St[:], f(0), ALU.mult), f"Sc.{j}")
                    PE.wait(dve, i, f"U.{j}")
                    step.then(dve.tensor_copy(by_parity(w.Us, 0), w.bank_pair(1)))
                    V.done(dve.tensor_copy(by_parity(w.Us, 1), w.bank_pair(2)), f"U.{j}")
                    PE.wait(dve, i, f"state.{j}")
                    step.then(tt(w.Sc[:], w.Sc[:], w.bank[1][:, 0:2 * BD].rearrange("p (a d) -> p a d", a=2), ALU.add))
                    V.done(tt(St[:], w.Sc[:], f(1), ALU.mult), f"state.{j}")
                    V.wait(dve, i, f"state.{j}")
                for j in range(2):
                    w = lane[j]
                    C.wait(dve, i, f"y.{j}")
                    step.then(dve.tensor_reduce(w.s4[:, 3, :], h3(w.ys[:]), AX.X, ALU.add))
                    step.then(dve.tensor_scalar(w.s4[:, 3, :], w.s4[:, 3, :], -1.0 / BD, None, ALU.mult))
                    step.then(tt(h3(w.ys[:]), h3(w.ys[:]), bc(w.s4[:, 3, :]), ALU.add))
                    step.then(tt(w.yq[:], w.ys[:], w.ys[:], ALU.mult))
                    V.done(dve.tensor_reduce(w.s4[:, 5, :], h3(w.yq[:]), AX.X, ALU.add), f"var.{j}")
                for j in range(2):
                    w = lane[j]
                    step.then(tt(h3(w.tmp[:]), h3(w.p[:, 2 * BW:3 * BW]), bc(w.s4[:, 4, :]), ALU.mult))
                    C.wait(dve, i, f"rstd.{j}")
                    step.then(tt(h3(w.ys[:]), h3(w.ys[:]), bc(w.s4[:, 7, :]), ALU.mult))
                    step.then(tt(w.ys[:], w.ys[:], lnx_g[:], ALU.mult))
                    step.then(tt(w.ys[:], w.ys[:], lnx_b[:], ALU.add))
                    step.then(tt(w.ys[:], w.ys[:], w.tmp[:], ALU.add))
                    dve.wait_ge(y_free[j], i + 1)
                    V.done(tt(w.yo[:], w.ys[:], w.g[:], ALU.mult), f"y.{j}")
                V.wait(dve, i, "y.1")
                step.restart()

        @block.tensor
        def _(pe):
            PE.start(pe)
            pe.sem_inc(pool_done, 10)
            pe.wait_ge(consts_in, 16 * 15)
            mm = pe.matmul
            with pe.Fori(0, TURNS) as i:
                for j in range(2):
                    w = lane[j]
                    V.wait(pe, i, f"lr.{j}")
                    for n in range(2):
                        q = pe.transpose(w.bank[0][:, n * P:(n + 1) * P], w.lr[:, n * P:(n + 1) * P], ident[:])
                    PE.done(q, f"lr_T.{j}")
                for j in range(2):
                    w = lane[j]
                    C.wait(pe, i, f"lrT.{j}")
                    mm(w.bank[1][:, 0:BW], w.lrT[0:64, 0:P], wa2[0:64, :], start=True, stop=True)
                    mm(w.bank[2][:, 0:BW], w.lrT[64:128, 0:P], wa2[64:128, :], start=True, stop=True)
                    PE.done(mm(w.bank[3][:, 0:BW], w.lrT[:, P:2 * P], g2[:], start=True, stop=True), f"lora.{j}")
                for j in range(2):
                    w = lane[j]
                    V.wait(pe, i, f"logw.{j}")
                    mm(w.bank[1][:, 0:BW], cum_m[:], w.lw[:], start=True, stop=True)
                    for a in range(2):
                        q = mm(w.bank[2][:, 2 * a:2 * a + 2], w.lw[:, a * P:(a + 1) * P], halves_m[:], start=True, stop=True)
                    PE.done(q, f"cum.{j}")
                for j in range(2):
                    w = lane[j]
                    V.wait(pe, i, f"operands.{j}")
                    C.wait(pe, i, f"g.{j}")
                    for a in range(2):
                        for x in range(2):
                            c = slice((2 * a + x) * P, (2 * a + x + 1) * P)
                            pe.transpose(w.bank[0][:, c], w.ops[:, x, a * P:(a + 1) * P], ident[:])
                            q = pe.transpose(w.bank[3][:, c], w.ops[:, 2 + x, a * P:(a + 1) * P], ident[:])
                    PE.done(q, f"operands_T.{j}")
                for j in range(2):
                    w = lane[j]
                    C.wait(pe, i, f"opsT.{j}")
                    for h in (0, 2, 1, 3):
                        r, a = half(h), h // 2
                        mm(w.bank[h][:, 0:2 * P], w.bkT[r, a, 0, :], w.arT[r, a, :, :], start=True, stop=True)
                        q = mm(w.bank[h][:, 2 * P:4 * P], w.bkT[r, a, 1, :], w.arT[r, a, :, :], start=True, stop=True)
                    PE.done(q, f"grams.{j}")
                for j in range(2):
                    w = lane[j]
                    V.wait(pe, i, f"masked.{j}")
                    for h in (0, 2, 1, 3):
                        r, a = half(h), h // 2
                        q = mm(w.bank[h % 2][:, a * P:(a + 1) * P], w.arT[r, a, 0, :], w.bkT[r, a, 0, :], start=True, stop=True)
                    PE.done(q, f"A.{j}")
                for j in range(2):
                    w = lane[j]
                    for h in range(BH):
                        q = mm(w.bank[3][:, hc(h)], w.gm[:, h, 2, :], w.p[:, 2 * BW + h * BD:2 * BW + (h + 1) * BD], start=True, stop=True)
                    PE.done(q, f"X.{j}")
                for n in range(4):
                    for j in range(2):
                        w = lane[j]
                        if n == 0:
                            V.wait(pe, i, f"D0.{j}")
                        else:
                            V.wait(pe, i, f"v{n - 1}.{j}")
                            C.wait(pe, i, f"c{n - 1}.{j}")
                        for h in range(BH):
                            c = slice(h * P, (h + 1) * P)
                            if n < 3:
                                mm(w.bank[0][:, c], w.DT[:, h, :], w.Dm[:, h, :], start=True, stop=True)
                                q = mm(w.bank[2][:, c], w.Dm[:, h, :], w.DT[:, h, :], start=True, stop=True)
                            if n > 0:
                                mm(w.bank[1][:, c], w.DT[:, h, :], w.T[:, h, :], start=True, stop=True)
                                q = mm(w.bank[3][:, c], w.Dm[:, h, :], w.TT[:, h, :], start=True, stop=True)
                        PE.done(q, f"sq{n}.{j}")
                for n in range(3):
                    for j in range(2):
                        w = lane[j]
                        if n == 0:
                            pe.wait_ge(pool_done, i * 10 + 5 * j + 15)
                            V.wait(pe, i, f"v3.{j}")
                        else:
                            V.wait(pe, i, f"vm{n - 1}.{j}")
                        for h in range(BH):
                            c = slice(h * P, (h + 1) * P)
                            if n < 2:
                                mm(w.bank[0][:, c], w.OT[n][:, h, :], w.T[:, h, :], start=True, stop=True)
                            q = mm(w.bank[2][:, c], w.O[n][:, h, :], w.TT[:, h, :], start=True, stop=True)
                        PE.done(q, f"z{n}.{j}")
                    for j in range(2):
                        w = lane[j]
                        V.wait(pe, i, f"vz{n}.{j}")
                        if n < 2:
                            C.wait(pe, i, f"cz{n}.{j}")
                        for h in range(BH):
                            c = slice(h * P, (h + 1) * P)
                            if n < 2:
                                mm(w.bank[1][:, c], w.TT[:, h, :], w.Z[:, h, :], start=True, stop=True)
                            q = mm(w.bank[3][:, c], w.T[:, h, :], w.ZT[:, h, :], start=True, stop=True)
                        PE.done(q, f"m{n}.{j}")
                for j in range(2):
                    w = lane[j]
                    V.wait(pe, i, f"vm2.{j}")
                    C.wait(pe, i, f"X.{j}")
                    for h in range(BH):
                        q = mm(w.bank[0][half(h), (h // 2) * P:(h // 2 + 1) * P], w.ops[:, 0, hc(h)], w.TT[:, h, :], start=True, stop=True)
                    PE.done(q, f"ta.{j}")
                for j in range(2):
                    w = lane[j]
                    v = lambda h: w.p[:, 2 * BW + h * BD:2 * BW + (h + 1) * BD]
                    C.wait(pe, i, f"ta.{j}")
                    V.wait(pe, i, f"Sc.{j}")
                    for h in range(BH):
                        o = w.bank[(1, 2)[h % 2]][:, hc(h // 2)]
                        mm(o, w.TT[:, h, :], w.Xs[:, hc(h)], start=True, stop=False)
                        q = mm(o, w.taT[half(h), h // 2, :], w.Sc[half(h), h // 2, :], start=False, stop=True)
                    PE.done(q, f"U.{j}")
                    V.wait(pe, i, f"U.{j}")
                    for h in range(BH):
                        o = w.bank[(3, 0)[h % 2]][:, hc(h // 2)]
                        mm(o, w.gm[:, h, 3, :], v(h), start=True, stop=False)
                        mm(o, w.gm[:, h, 1, :], w.Us[:, hc(h)], start=False, stop=False)
                        q = mm(o, w.arT[half(h), h // 2, 1, :], w.Sc[half(h), h // 2, :], start=False, stop=True)
                    PE.done(q, f"Y.{j}")
                    for h in range(BH):
                        o = w.bank[1][half(h), (h // 2) * BD:(h // 2 + 1) * BD]
                        mm(o, w.ops[:, 3, hc(h)], v(h), start=True, stop=False)
                        q = mm(o, w.ops[:, 2, hc(h)], w.Us[:, hc(h)], start=False, stop=True)
                    PE.done(q, f"state.{j}")


E, F, TOP_K, NG, TOPK_GROUPS = 64, 256, 8, 8, 4
EG = E // NG
FC = F // P
ROUTED_SCALE = 2.5
BLOCKS = E + (S * TOP_K - E) // P
NB = BLOCKS + 6
DROP = -3.0e38


def norm_route(nc, io, dr, keep):
    with ExitStack() as ctx:
        sb = lambda n, s: ctx.enter_context(nc.sbuf_tensor(n, s, F32))
        sem = lambda n: ctx.enter_context(nc.semaphore(n))
        bank = [ctx.enter_context(nc.psum_tensor(f"rbank{n}", [P, BANK], F32)) for n in range(8)]
        ident = keep["ident"]
        w_out = sb("w_out", [P, KC, D])
        w_r = sb("router_w", [P, KC, E])
        ws13, ws2 = sb("shared_w13", [P, 2, KC, F]), sb("shared_w2", [P, FC, D])
        post, scale, shift = sb("post_scale", [P, D]), sb("scale2", [P, D]), sb("shift2", [P, D])
        e_bias = sb("router_bias", [P, E])
        ones, strict, before = sb("ones", [P, P]), sb("strict", [P, P]), sb("group_before", [P, NG, NG])
        ym, x, x2, h2 = sb("ymix_tile", [P, D]), sb("x_in", [P, D]), sb("x2_tile", [P, D]), sb("h2_tile", [P, D])
        yT, h2T = sb("ymixT", [P, KC, P]), sb("h2T", [P, KC, P])
        sq = sb("sq", [P, D])
        st = sb("norm_stats", [P, 8])
        sc, bi, cand, left = sb("scores", [P, E]), sb("biased", [P, E]), sb("candidates", [P, E]), sb("left", [P, E])
        sel, rw = sb("selected", [P, E]), sb("route_w", [P, E])
        g8 = sb("group_top", [P, NG, 8])
        gs, gr, gq, gk = sb("group_score", [P, NG]), sb("group_rank", [P, NG]), sb("group_cmp", [P, NG, NG]), sb("group_eq", [P, NG, NG])
        top, ws = sb("top8", [P, 8]), sb("weight_sum", [P, 4])
        sg, acts, aT, ysh = sb("sh_sig", [P, F]), sb("sh_act", [P, F]), sb("sh_actT", [P, FC, P]), sb("y_shared", [P, D])
        posm, W, seen = keep["posm"], keep["W"], keep["seen"]
        consts_in, load_in, zero_done, outs, out_free = (sem(n) for n in ("r_consts_in", "ymix_in", "r_zero_done", "r_outs", "r_out_free"))
        dve_step, act_step = sem("r_dve_step"), sem("r_act_step")
        PE = Stages(sem("r_pe_done"), ["yT", "proj", "h2T", "route", "up", "pos", "aT", "down"])
        V = Stages(sem("r_dve_done"), ["ss", "xn", "x2", "h2", "logit", "sh_arg", "sh_act", "sel", "aT", "pos"])
        C = Stages(sem("r_act_done"), ["yT", "sq", "rstd", "rstd2", "h2T", "score_exp", "sh_exp", "down"])
        k4 = lambda x: x.rearrange("p (k n) -> p k n", k=4)
        row = lambda n: dr["rows"][:, n * D:(n + 1) * D].partition_broadcast(P)
        kp = lambda x: x.rearrange("(k p) n -> p k n", p=P)
        CONSTS = 12
        block = ctx.enter_context(nc.Block())

        @block.sync
        def _(sp):
            for dst, src in ((w_out[:], kp(io["w_out"][0])), (w_r[:], kp(io["router_w"][0])),
                             (ws13[:, 0], kp(io["shared_w1"][0])), (ws13[:, 1], kp(io["shared_w3"][0])), (ws2[:], kp(io["shared_w2"][0])),
                             (post[:], row(2)), (scale[:], row(4)), (shift[:], row(3)),
                             (e_bias[:], io["router_bias"][0:1, :].partition_broadcast(P)),
                             (ones[:], io["c_ones"]), (strict[:], io["c_strict"]), (before[:], io["c_before"])):
                sp.dma_start(dst, src).then_inc(consts_in, 16)
            sp.wait_ge(zero_done, 1)
            sp.dma_start(dr["h2"][S:S + P, :], sq[:]).then_inc(outs, 16)
            sp.dma_start(dr["acc"][S:S + P, :], sq[:]).then_inc(outs, 16)
            sp.wait_ge(outs, 32)
            sp.sem_inc(out_free, 3)
            with sp.Fori(0, NT) as t:
                rows = bass.ds(t * P, P)
                PE.wait_before(sp, t, "yT")
                sp.dma_start(ym[:], dr["ymix"][rows, :]).then_inc(load_in, 16)
                V.wait_before(sp, t, "x2")
                sp.dma_start(x[:], io["x"][0][rows, :]).then_inc(load_in, 16)
                V.wait(sp, t, "x2")
                sp.dma_start(dr["x2"][rows, :], x2[:]).then_inc(outs, 16)
                V.wait(sp, t, "h2")
                sp.dma_start(dr["h2"][rows, :], h2[:]).then_inc(outs, 16)
                sp.wait_ge(outs, t * 48 + 64)
                sp.sem_inc(out_free, 2)
                C.wait(sp, t, "down")
                sp.dma_start(dr["acc"][rows, :], ysh[:]).then_inc(outs, 16)
                sp.wait_ge(outs, t * 48 + 80)
                sp.sem_inc(out_free, 1)

        @block.scalar
        def _(act):
            load_exp_and_ln(nc, act)
            step = Steps(act, act_step)
            C.start(act)
            act.wait_ge(out_free, 3)
            with act.Fori(0, NT) as t:
                PE.wait(act, t, "yT")
                act.copy(yT[:, 0:4, :], k4(bank[0][:]))
                C.done(act.copy(yT[:, 4:8, :], k4(bank[1][:])), "yT")
                PE.wait(act, t, "proj")
                act.activation(sq[:, 0:BANK], bank[2][:], ACT.Square, accum_out=st[:, 0:1])
                C.done(act.activation(sq[:, BANK:], bank[3][:], ACT.Square, accum_out=st[:, 1:2]), "sq")
                V.wait(act, t, "ss")
                step.then(act.activation(st[:, 3:4], st[:, 2:3], ACT.Ln, scale=1.0 / D, bias=keep["eps"][:, 0:1]))
                C.done(act.activation(st[:, 4:5], st[:, 3:4], ACT.Exp, scale=-0.5), "rstd")
                V.wait(act, t, "x2")
                step.then(act.activation(sq[:], x2[:], ACT.Square, accum_out=st[:, 5:6]))
                step.then(act.activation(st[:, 6:7], st[:, 5:6], ACT.Ln, scale=1.0 / D, bias=keep["eps"][:, 0:1]))
                C.done(act.activation(st[:, 7:8], st[:, 6:7], ACT.Exp, scale=-0.5), "rstd2")
                PE.wait(act, t, "h2T")
                act.copy(h2T[:, 0:4, :], k4(bank[0][:]))
                C.done(act.copy(h2T[:, 4:8, :], k4(bank[1][:])), "h2T")
                V.wait(act, t, "logit")
                C.done(act.activation(sc[:], sc[:], ACT.Exp, scale=-1.0), "score_exp")
                V.wait(act, t, "sh_arg")
                C.done(act.activation(sg[:], sg[:], ACT.Exp, scale=-1.0), "sh_exp")
                PE.wait(act, t, "down")
                act.wait_ge(out_free, t * 3 + 3)
                act.copy(ysh[:, 0:BANK], bank[2][:])
                C.done(act.copy(ysh[:, BANK:], bank[3][:]), "down")
                step.restart()

        @block.vector
        def _(dve):
            step = Steps(dve, dve_step)
            tt, ts, stt = dve.tensor_tensor, dve.tensor_scalar, dve.scalar_tensor_tensor
            V.start(dve)
            dve.memset(sq[:], 0.0).then_inc(zero_done, 1)
            step.then(dve.memset(seen[:], 0.0))
            dve.wait_ge(consts_in, 16 * CONSTS)
            step.restart()
            with dve.Fori(0, NT) as t:
                C.wait(dve, t, "sq")
                V.done(tt(st[:, 2:3], st[:, 0:1], st[:, 1:2], ALU.add), "ss")
                C.wait(dve, t, "rstd")
                dve.wait_ge(out_free, t * 3 + 3)
                for n in range(2):
                    c = slice(n * BANK, (n + 1) * BANK)
                    q = stt(x2[:, c], bank[2 + n][:], st[:, 4:5], post[:, c], ALU.mult, ALU.mult)
                V.done(q, "xn")
                V.wait(dve, t, "xn")
                dve.wait_ge(load_in, t * 32 + 32)
                V.done(tt(x2[:], x2[:], x[:], ALU.add), "x2")
                C.wait(dve, t, "rstd2")
                step.then(stt(h2[:], x2[:], st[:, 7:8], scale[:], ALU.mult, ALU.mult))
                V.done(tt(h2[:], h2[:], shift[:], ALU.add), "h2")
                PE.wait(dve, t, "route")
                V.done(ts(sc[:], bank[4][:, 0:E], -80.0, None, ALU.max), "logit")
                PE.wait(dve, t, "up")
                V.done(ts(sg[:], bank[5][:, 0:F], -80.0, None, ALU.max), "sh_arg")
                C.wait(dve, t, "score_exp")
                step.then(ts(sc[:], sc[:], 1.0, None, ALU.add))
                step.then(dve.reciprocal(sc[:], sc[:]))
                C.wait(dve, t, "sh_exp")
                step.then(ts(sg[:], sg[:], 1.0, None, ALU.add))
                step.then(dve.reciprocal(sg[:], sg[:]))
                step.then(tt(sg[:], sg[:], bank[5][:, 0:F], ALU.mult))
                PE.wait_before(dve, t, "aT")
                V.done(tt(acts[:], sg[:], bank[5][:, F:2 * F], ALU.mult), "sh_act")
                step.then(tt(bi[:], sc[:], e_bias[:], ALU.add))
                for n in range(NG):
                    q = dve.max(g8[:, n, :], bi[:, n * EG:(n + 1) * EG])
                step.then(q)
                step.then(tt(gs[:], g8[:, :, 0], g8[:, :, 1], ALU.add))
                mine, other = gs[:].unsqueeze(2).to_broadcast([P, NG, NG]), gs[:].unsqueeze(1).to_broadcast([P, NG, NG])
                step.then(tt(gk[:], other, mine, ALU.is_equal))
                step.then(tt(gk[:], gk[:], before[:], ALU.mult))
                step.then(tt(gq[:], other, mine, ALU.is_gt))
                step.then(tt(gq[:], gq[:], gk[:], ALU.add))
                step.then(dve.tensor_reduce(gr[:], gq[:], AX.X, ALU.add))
                step.then(ts(gr[:], gr[:], TOPK_GROUPS - 0.5, None, ALU.is_lt))
                step.then(ts(gs[:], gr[:], -NEG, NEG, ALU.mult, ALU.add))
                g3 = lambda x: x.rearrange("p (g e) -> p g e", g=NG)
                gb = lambda x: x.unsqueeze(2).to_broadcast([P, NG, EG])
                step.then(tt(g3(cand[:]), g3(bi[:]), gb(gr[:]), ALU.mult))
                step.then(tt(g3(cand[:]), g3(cand[:]), gb(gs[:]), ALU.add))
                step.then(dve.max(top[:], cand[:]))
                step.then(dve.match_replace(left[:], top[:], cand[:], DROP))
                PE.wait_before(dve, t, "pos")
                V.done(ts(sel[:], left[:], DROP, None, ALU.is_equal), "sel")
                V.wait(dve, t, "sel")
                step.then(tt(rw[:], sc[:], sel[:], ALU.mult))
                step.then(dve.tensor_reduce(ws[:, 0:1], rw[:], AX.X, ALU.add))
                step.then(ts(ws[:, 1:2], ws[:, 0:1], 1e-20, None, ALU.add))
                step.then(dve.reciprocal(ws[:, 2:3], ws[:, 1:2]))
                step.then(ts(W[:, bass.ds(t, 1), :].squeeze(1), rw[:], ws[:, 2:3], ROUTED_SCALE, ALU.mult, ALU.mult))
                PE.wait(dve, t, "aT")
                V.done(dve.tensor_copy(aT[:], bank[6][:, 0:F].rearrange("p (k n) -> p k n", k=FC)), "aT")
                PE.wait(dve, t, "pos")
                step.then(tt(seen[:], seen[:], sel[:], ALU.add))
                step.then(stt(left[:], bank[7][:, 0:E], 1.0, sel[:], ALU.add, ALU.mult))
                V.done(ts(posm[:, bass.ds(t, 1), :].squeeze(1), left[:], -1.0, None, ALU.add), "pos")
                V.wait(dve, t, "pos")
                step.restart()

        @block.tensor
        def _(pe):
            PE.start(pe)
            mm = pe.matmul
            pe.wait_ge(consts_in, 16 * CONSTS)
            with pe.Fori(0, NT) as t:
                pe.wait_ge(load_in, t * 32 + 32)
                for k in range(KC):
                    q = pe.transpose(bank[k // 4][:, (k % 4) * P:(k % 4 + 1) * P], ym[:, k * P:(k + 1) * P], ident[:])
                PE.done(q, "yT")
                C.wait(pe, t, "yT")
                C.wait_before(pe, t, "down")
                for n in range(2):
                    for k in range(KC):
                        q = mm(bank[2 + n][:], yT[:, k, :], w_out[:, k, n * BANK:(n + 1) * BANK], start=(k == 0), stop=(k == KC - 1))
                PE.done(q, "proj")
                V.wait(pe, t, "h2")
                for k in range(KC):
                    q = pe.transpose(bank[k // 4][:, (k % 4) * P:(k % 4 + 1) * P], h2[:, k * P:(k + 1) * P], ident[:])
                PE.done(q, "h2T")
                C.wait(pe, t, "h2T")
                for k in range(KC):
                    q = mm(bank[4][:, 0:E], h2T[:, k, :], w_r[:, k, :], start=(k == 0), stop=(k == KC - 1))
                PE.done(q, "route")
                for k in range(KC):
                    q = mm(bank[5][:].rearrange("p (a n) -> p a n", a=2), h2T[:, k, :], ws13[:, :, k, :], start=(k == 0), stop=(k == KC - 1))
                PE.done(q, "up")
                V.wait(pe, t, "sel")
                mm(bank[7][:, 0:E], ones[:], seen[:], start=True, stop=False)
                PE.done(mm(bank[7][:, 0:E], strict[:], sel[:], start=False, stop=True), "pos")
                V.wait(pe, t, "sh_act")
                for k in range(FC):
                    q = pe.transpose(bank[6][:, k * P:(k + 1) * P], acts[:, k * P:(k + 1) * P], ident[:])
                PE.done(q, "aT")
                V.wait(pe, t, "aT")
                for n in range(2):
                    for k in range(FC):
                        q = mm(bank[2 + n][:], aT[:, k, :], ws2[:, k, n * BANK:(n + 1) * BANK], start=(k == 0), stop=(k == FC - 1))
                PE.done(q, "down")


def schedule(nc, io, dr, keep):
    with ExitStack() as ctx:
        sb = lambda n, s: ctx.enter_context(nc.sbuf_tensor(n, s, F32))
        sem = lambda n: ctx.enter_context(nc.semaphore(n))
        ps_a, ps_b = (ctx.enter_context(nc.psum_tensor(n, [P, BANK], F32)) for n in ("sched_a", "sched_b"))
        ones, upper, thr, iota_b, step3 = sb("s_ones", [P, P]), sb("s_upper", [P, P]), sb("thresholds", [E, 8]), sb("iota_b", [P, NB]), sb("step3", [E, P])
        cnt, more, nblk, end, ind, nbc = sb("counts", [E, 1]), sb("more", [E, 8]), sb("n_blocks", [E, 1]), sb("end", [E, 1]), sb("ended", [E, NB]), sb("nbc", [E, P])
        over, first = sb("over", [P, NB]), sb("first", [P, NB])
        tab, base = keep["tab"], keep["base"]
        consts_in, dve_done, pe_done = sem("s_consts_in"), sem("s_dve_done"), sem("s_pe_done")
        block = ctx.enter_context(nc.Block())

        @block.sync
        def _(sp):
            for dst, src in ((ones[:], io["c_ones"]), (upper[:], io["c_upper"]), (thr[:], io["c_thresholds"]),
                             (iota_b[:], io["c_iota_b"].partition_broadcast(P)), (step3[:], io["c_step3"])):
                sp.dma_start(dst, src).then_inc(consts_in, 16)
            sp.wait_ge(consts_in, 80)

        @block.vector
        def _(dve):
            step = Steps(dve, dve_done)
            dve.wait_ge(consts_in, 80)
            dve.wait_ge(pe_done, 1)
            step.then(dve.tensor_copy(cnt[:], ps_a[0:E, 0:1]))
            step.then(dve.tensor_scalar(more[:], thr[:], cnt[:], None, ALU.is_lt))
            step.then(dve.tensor_reduce(nblk[:], more[:], AX.X, ALU.add))
            step.then(dve.tensor_copy(nbc[:], nblk[:].to_broadcast([E, P])))
            dve.wait_ge(pe_done, 2)
            step.then(dve.tensor_copy(end[:], ps_b[0:E, 0:1]))
            step.then(dve.tensor_scalar(ind[:], iota_b[0:E, :], end[:], None, ALU.is_ge))
            dve.wait_ge(pe_done, 3)
            e_raw, start, w3 = (ps_a[:, n * NB:(n + 1) * NB] for n in range(3))
            step.then(dve.tensor_scalar(over[:], e_raw, E - 0.5, 4096.0, ALU.is_gt, ALU.mult))
            step.then(dve.tensor_tensor(first[:], iota_b[:], start, ALU.subtract))
            step.then(dve.scalar_tensor_tensor(base[:], first[:], float(P), over[:], ALU.mult, ALU.add))
            step.then(dve.tensor_scalar(tab[0:1, 0, :], e_raw[0:1, :], E - 1.0, None, ALU.min))
            step.then(dve.tensor_copy(tab[0:1, 1, :], w3[0:1, :]))
            step.then(dve.tensor_copy(tab[0:1, 2, 0:E], ps_b[0:1, E:2 * E]))

        @block.tensor
        def _(pe):
            mm = pe.matmul
            pe.wait_ge(consts_in, 80)
            mm(ps_a[0:E, 0:1], keep["seen"][:], ones[:, 0:1], start=True, stop=True).then_inc(pe_done, 1)
            pe.wait_ge(dve_done, 4)
            mm(ps_b[0:E, 0:1], upper[0:E, 0:E], nblk[:], start=True, stop=True).then_inc(pe_done, 1)
            pe.wait_ge(dve_done, 6)
            mm(ps_b[:, E:2 * E], nbc[:], upper[0:E, 0:E], start=True, stop=True)
            mm(ps_a[:, 0:NB], ones[0:E, :], ind[:], start=True, stop=True)
            mm(ps_a[:, NB:2 * NB], nbc[:], ind[:], start=True, stop=True)
            mm(ps_a[:, 2 * NB:3 * NB], step3[:], ind[:], start=True, stop=True).then_inc(pe_done, 1)


def experts(nc, io, dr, keep):
    I32 = mybir.dt.int32
    with ExitStack() as ctx:
        sb = lambda n, s, dt=F32: ctx.enter_context(nc.sbuf_tensor(n, s, dt))
        sem = lambda n: ctx.enter_context(nc.semaphore(n))
        pt = lambda n: ctx.enter_context(nc.psum_tensor(n, [P, BANK], F32))
        ident, posm, W, tab, base = keep["ident"], keep["posm"], keep["W"], keep["tab"], keep["base"]
        w13, w2 = sb("w13", [P, 3, 2, KC, F]), sb("w2", [P, 3, FC, D])
        iota, vals, empty = sb("iota_p", [P, P]), sb("id_and_weight", [P, NT, 2]), sb("empty_row", [P, 1])
        pcol, onehot = sb("place", [P, NT]), sb("onehot_p", [P, NT, P])
        nid, isn = sb("list_id", [P, 4]), sb("is_empty", [P, 2])
        wslot = [sb(f"slot_w{j}", [P, 1]) for j in range(4)]
        idx = [sb(f"idx{j}", [P, 1], I32) for j in range(4)]
        sidx = [sb(f"scatter_idx{j}", [P, 1], I32) for j in range(2)]
        xg = [sb(f"gathered{j}", [P, D]) for j in range(2)]
        y = [sb(f"y_rows{j}", [P, D]) for j in range(2)]
        xT, sg, acts, aT = sb("xT", [P, KC, P]), sb("silu_g", [P, F]), sb("act", [P, F]), sb("actT", [P, FC, P])
        ps_x, ps_y = [pt(f"ps_x{n}") for n in range(2)], [pt(f"ps_y{n}") for n in range(2)]
        ps_h, ps_a, ps_l = pt("ps_h"), pt("ps_a"), pt("ps_l")
        held = sem("held")
        consts_in, w_ready, dve_step = sem("e_consts_in"), sem("w_ready"), sem("e_dve_step")
        piece_in = [sem(f"piece_in{n}") for n in range(3)]
        xg_in = [sem(f"xg_in{n}") for n in range(2)]
        onehot_ready, list_mm, idx_ready, x_mm, x_copied, up_mm, silu_done, act_ready, at_mm, aT_ready, dn_mm, y_ready, y_out, y_free = (
            sem(n) for n in ("onehot_ready", "list_mm", "idx_ready", "x_mm", "x_copied", "up_mm", "silu_done", "act_ready",
                             "at_mm", "aT_ready", "dn_mm", "y_ready", "e_y_out", "e_y_free"))
        views = [io[n][0].rearrange("e (p k) f -> e p k f", p=P) for n in ("exp_w1", "exp_w3")]
        view2 = io["exp_w2"][0].rearrange("e (p k) d -> e p k d", p=P)
        TURNS = (BLOCKS + 3) // 4
        block = ctx.enter_context(nc.Block())

        def n_blocks(eng):
            return eng.value_load(tab[0:1, 2, E - 1:E], min_val=E, max_val=BLOCKS)

        @block.sync
        def _(sp):
            for dst, src in ((iota[:], io["c_iota_p"].partition_broadcast(P)), (vals[:, :, 0:1], io["c_ids"]), (empty[:], io["c_empty"])):
                sp.dma_start(dst, src, allow_slow_non_contiguous=True).then_inc(consts_in, 16)

            def load(e, s, turn, after=None):
                for n in range(6):
                    if s or n >= 3 or after is not None:
                        sp.wait_ge(piece_in[n % 3], turn * 96 + (s * 6 + n) // 3 * 16)
                    if n == 3 and (s or after is not None):
                        sp.sem_inc(w_ready, 1)
                    if n == 0 and after is not None:
                        sp.wait_ge(dn_mm, sp.value_load(tab[0:1, 2, bass.ds(after, 1)], min_val=1, max_val=BLOCKS) + 1)
                    which, half = n // 2, n % 2
                    if which < 2:
                        k = slice(half * KC // 2, (half + 1) * KC // 2)
                        sp.dma_start(w13[:, s, which, k], views[which][bass.ds(e, 1)].squeeze(0)[:, k, :]).then_inc(piece_in[n % 3], 16)
                    else:
                        sp.dma_start(w2[:, s, half], view2[bass.ds(e, 1)].squeeze(0)[:, half, :]).then_inc(piece_in[n % 3], 16)

            for s in range(3):
                load(s, s, 0)
            with sp.Fori(1, E // 3) as i:
                for s in range(3):
                    load(i * 3 + s, s, i, i * 3 + s - 3)
            load(E - 1, 0, E // 3, E - 4)
            for n in range(3):
                sp.wait_ge(piece_in[n], E * 32)
            sp.sem_inc(w_ready, 1)

        @block.gpsimd
        def _(pool):
            nb = n_blocks(pool)
            pool.sem_inc(y_free, 2)

            def gather(n, j):
                par = j % 2
                pool.wait_ge(idx_ready, n + 1)
                pool.sem_inc(held, 1)
                pool.indirect_dma_start(xg[par][:], None, dr["h2"], bass.IndirectOffsetOnAxis(ap=idx[j][:], axis=0)).then_inc(xg_in[par], 16)

            for n in range(3):
                if n == 2:
                    pool.wait_ge(x_mm, 1)
                gather(n, n)
            with pool.Fori(0, TURNS) as i:
                with pool.If(nb > i * 4):
                    for j in range(4):
                        b = i * 4 + j
                        pool.wait_ge(x_mm, b + 2)
                        gather(b + 3, (j + 3) % 4)
                        pool.wait_ge(y_ready, b + 2)
                        pool.sem_inc(held, 1)
                        pool.indirect_dma_start(dr["acc"], bass.IndirectOffsetOnAxis(ap=sidx[j % 2][:], axis=0), y[j % 2][:], None,
                                                compute_op=ALU.add).then_inc(y_out, 16)
                        pool.wait_ge(y_out, b * 16 + 16)
                        pool.sem_inc(y_free, 1)

        @block.scalar
        def _(act):
            nb = n_blocks(act)
            act.sem_inc(y_ready, 1)

            def x_copy(n):
                act.wait_ge(x_mm, n + 1)
                act.copy(xT[:, 0:4, :], ps_x[0][:].rearrange("p (k n) -> p k n", k=4))
                act.copy(xT[:, 4:8, :], ps_x[1][:].rearrange("p (k n) -> p k n", k=4)).then_inc(x_copied, 1)

            def silu(n):
                act.wait_ge(up_mm, n + 1)
                act.activation(sg[:], ps_h[:, 0:F], ACT.Silu).then_inc(silu_done, 1)

            x_copy(0)
            silu(0)
            with act.Fori(0, TURNS) as i:
                with act.If(nb > i * 4):
                    for j in range(4):
                        b = i * 4 + j
                        x_copy(b + 1)
                        act.wait_ge(act_ready, b + 1)
                        silu(b + 1)
                        act.wait_ge(y_free, b + 1)
                        act.wait_ge(dn_mm, b + 2)
                        act.copy(y[j % 2][:, 0:BANK], ps_y[0][:])
                        act.copy(y[j % 2][:, BANK:], ps_y[1][:]).then_inc(y_ready, 1)

        @block.vector
        def _(dve):
            step = Steps(dve, dve_step)
            nb = n_blocks(dve)
            dve.wait_ge(consts_in, 48)

            def make_onehot(n, e):
                step.then(dve.tensor_scalar(pcol[:], posm[:, :, bass.ds(e, 1)].squeeze(2), base[:, bass.ds(n, 1)], None, ALU.subtract))
                step.then(dve.tensor_copy(vals[:, :, 1:2], W[:, :, bass.ds(e, 1)]))
                for k in range(NT):
                    q = dve.tensor_scalar(onehot[:, k, :], iota[:], pcol[:, k:k + 1], None, ALU.is_equal)
                q.then_inc(onehot_ready, 1)

            def expert_of(n):
                return dve.value_load(tab[0:1, 0, bass.ds(n, 1)], min_val=0, max_val=E - 1)

            def make_index(n, par):
                dve.wait_ge(list_mm, n + 1)
                step.then(dve.tensor_copy(nid[:, 0:2], ps_l[:, 0:2]))
                step.then(dve.tensor_scalar(isn[:, 0:1], nid[:, 0:1], 0.0, None, ALU.is_equal))
                step.then(dve.tensor_copy(wslot[par][:], nid[:, 1:2]))
                step.then(dve.tensor_tensor(isn[:, 1:2], isn[:, 0:1], empty[:], ALU.mult))
                dve.scalar_tensor_tensor(idx[par][:], nid[:, 0:1], -1.0, isn[:, 1:2], ALU.add, ALU.add).then_inc(idx_ready, 1)

            def activate(n, par):
                dve.wait_ge(silu_done, n + 1)
                dve.scalar_tensor_tensor(acts[:], sg[:], wslot[par][:], ps_h[:, F:2 * F], ALU.mult, ALU.mult).then_inc(act_ready, 1)

            for n in range(3):
                make_onehot(n, expert_of(n))
                make_index(n, n)
            make_onehot(3, expert_of(3))
            activate(0, 0)
            step.restart()
            with dve.Fori(0, TURNS) as i:
                with dve.If(nb > i * 4):
                    for j in range(4):
                        b = i * 4 + j
                        dve.wait_ge(at_mm, b + 1)
                        dve.wait_ge(dn_mm, b + 1)
                        dve.tensor_copy(aT[:], ps_a[:, 0:F].rearrange("p (k n) -> p k n", k=FC)).then_inc(aT_ready, 1)
                        dve.wait_ge(y_free, b + 1)
                        dve.wait_ge(idx_ready, b + 1)
                        step.then(dve.tensor_copy(sidx[j % 2][:], idx[j][:]))
                        dve.wait_ge(x_mm, b + 1)
                        make_index(b + 3, (j + 3) % 4)
                        make_onehot(b + 4, expert_of(b + 4))
                        activate(b + 1, (j + 1) % 4)
                    step.restart()

        @block.tensor
        def _(pe):
            nb = n_blocks(pe)
            pe.sem_inc(dn_mm, 1)

            def list_of(n):
                pe.wait_ge(onehot_ready, n + 1)
                for k in range(NT):
                    q = pe.matmul(ps_l[:, 0:2], onehot[:, k, :], vals[:, k, :], start=(k == 0), stop=(k == NT - 1))
                q.then_inc(list_mm, 1)

            def x_transpose(n, par, turn):
                pe.wait_ge(xg_in[par], turn * 16 + 16)
                for k in range(KC):
                    q = pe.transpose(ps_x[k // 4][:, (k % 4) * P:(k % 4 + 1) * P], xg[par][:].rearrange("p (c k) -> p k c", k=KC)[:, k, :], ident[:])
                q.then_inc(x_mm, 1)

            def entry(which, n, hi):
                return pe.value_load(tab[0:1, which, bass.ds(n, 1)], min_val=0, max_val=hi)

            def up(n):
                e, w = entry(0, n, E - 1), entry(1, n, 2)
                pe.wait_ge(w_ready, e + 1)
                pe.wait_ge(x_copied, n + 1)
                for k in range(KC):
                    q = pe.matmul(ps_h[:].rearrange("p (a n) -> p a n", a=2), xT[:, k, :], w13[:, bass.ds(w, 1), :, k, :].squeeze(1),
                                  start=(k == 0), stop=(k == KC - 1))
                q.then_inc(up_mm, 1)

            for n in range(3):
                if n:
                    pe.wait_ge(idx_ready, n)
                list_of(n)
            x_transpose(0, 0, 0)
            up(0)
            with pe.Fori(0, TURNS) as i:
                with pe.If(nb > i * 4):
                    for j in range(4):
                        b = i * 4 + j
                        x_transpose(b + 1, (j + 1) % 2, i * 2 + (j + 1) // 2)
                        pe.wait_ge(act_ready, b + 1)
                        for k in range(FC):
                            q = pe.transpose(ps_a[:, k * P:(k + 1) * P], acts[:].rearrange("p (c k) -> p k c", k=FC)[:, k, :], ident[:])
                        q.then_inc(at_mm, 1)
                        pe.wait_ge(idx_ready, b + 3)
                        list_of(b + 3)
                        up(b + 1)
                        w = entry(1, b, 2)
                        pe.wait_ge(aT_ready, b + 1)
                        pe.wait_ge(y_ready, b + 1)
                        for n in range(2):
                            for k in range(FC):
                                q = pe.matmul(ps_y[n][:], aT[:, k, :], w2[:, bass.ds(w, 1), k, n * BANK:(n + 1) * BANK].squeeze(1),
                                              start=(k == 0), stop=(k == FC - 1))
                        q.then_inc(dn_mm, 1)


def finish(nc, io, dr, keep, out):
    with ExitStack() as ctx:
        sb = lambda n, s: ctx.enter_context(nc.sbuf_tensor(n, s, F32))
        sem = lambda n: ctx.enter_context(nc.semaphore(n))
        post = sb("post2", [P, D])
        a, x2, junk = ([sb(f"{n}{j}", [P, D]) for j in range(2)] for n in ("acc_tile", "x2_in", "sq2"))
        st = [sb(f"f_stats{j}", [P, 3]) for j in range(2)]
        post_in, dve_step = sem("post_in"), sem("f_dve_step")
        tile_in = [sem(f"tile_in{j}") for j in range(2)]
        rstd, sums, ready, outs, act_step = sem("f_rstd"), sem("f_sums"), sem("f_ready"), sem("f_outs"), sem("f_act_step")
        block = ctx.enter_context(nc.Block())

        @block.sync
        def _(sp):
            sp.dma_start(post[:], dr["rows"][:, 5 * D:6 * D].partition_broadcast(P)).then_inc(post_in, 16)
            with sp.Fori(0, NT // 2) as i:
                for j in range(2):
                    rows = bass.ds((i * 2 + j) * P, P)
                    sp.wait_ge(ready, i * 2 + j + 1)
                    sp.dma_start(a[j][:], dr["acc"][rows, :]).then_inc(tile_in[j], 16)
                    sp.dma_start(x2[j][:], dr["x2"][rows, :]).then_inc(tile_in[j], 16)

        @block.scalar
        def _(act):
            load_exp_and_ln(nc, act)
            step = Steps(act, act_step)
            with act.Fori(0, NT // 2) as i:
                for j in range(2):
                    act.wait_ge(tile_in[j], i * 32 + 32)
                    step.then(act.activation(junk[j][:], a[j][:], ACT.Square, accum_out=st[j][:, 0:1]))
                    step.then(act.activation(st[j][:, 1:2], st[j][:, 0:1], ACT.Ln, scale=1.0 / D, bias=keep["eps"][:, 0:1]))
                    act.activation(st[j][:, 2:3], st[j][:, 1:2], ACT.Exp, scale=-0.5).then_inc(rstd, 1)
                step.restart()

        @block.vector
        def _(dve):
            step = Steps(dve, dve_step)
            dve.wait_ge(post_in, 16)
            with dve.Fori(0, NT // 2) as i:
                for j in range(2):
                    dve.wait_ge(rstd, i * 2 + j + 1)
                    step.then(dve.scalar_tensor_tensor(a[j][:], a[j][:], st[j][:, 2:3], post[:], ALU.mult, ALU.mult))
                    step.then(dve.tensor_tensor(x2[j][:], x2[j][:], a[j][:], ALU.add))
                    dve.sem_inc(sums, 1)
                step.restart()

        @block.gpsimd
        def _(pool):
            pool.sem_inc(ready, 2)
            with pool.Fori(0, NT // 2) as i:
                for j in range(2):
                    t = i * 2 + j
                    pool.wait_ge(sums, t + 1)
                    pool.dma_start(out[0][bass.ds(t * P, P), :], x2[j][:]).then_inc(outs, 16)
                    pool.wait_ge(outs, t * 16 + 16)
                    pool.sem_inc(ready, 1)


def t5_buckets(n):
    exact = N_BUCKETS // 2
    nf = np.maximum(n, 1).astype(np.float32)
    large = exact + (np.log(nf / exact) / math.log(MAX_DISTANCE / exact) * (N_BUCKETS - exact)).astype(np.int32)
    return np.where(n < exact, n, np.minimum(large, N_BUCKETS - 1))


def constants():
    s, t = np.arange(P)[:, None], np.arange(P)[None, :]
    f = lambda x: np.ascontiguousarray(x, dtype=np.float32)
    dist = 2 * P - 1 - np.arange(3 * P)
    onehot = np.zeros((N_BUCKETS + 1, 3 * P), np.float32)
    onehot[np.where(dist >= 0, t5_buckets(np.maximum(dist, 0)), N_BUCKETS), np.arange(3 * P)] = 1
    lower, upper = s > t, s < t
    blocks = [s // b == t // b for b in (16, 32, 64, 128)]
    masks = [lower, lower & blocks[0], upper & blocks[0]]
    for n in range(3):
        masks += [lower & blocks[n + 1] & ~blocks[n], upper & blocks[n + 1] & ~blocks[n]]
    mid = P // 2 - 1
    return {
        "c_ident": f(s == t),
        "c_upper": f(s <= t),
        "c_onehot": onehot,
        "c_mask4": f(np.stack([upper, s <= t, upper, s <= t], 1)),
        "c_masks": f(np.stack(masks, 1)),
        "c_cum": f((s <= t).astype(int) - (s <= mid).astype(int)),
        "c_ones": f(np.ones((P, P))),
        "c_strict": f(upper),
        "c_before": f(np.broadcast_to(np.tril(np.ones((NG, NG)), -1), (P, NG, NG))),
        "c_thresholds": f(np.broadcast_to([-1] + [P * n for n in range(1, S // P)], (E, 8))),
        "c_iota_b": f(np.arange(NB)[None, :]),
        "c_step3": f(np.broadcast_to([[(e + 1) % 3 - e % 3] for e in range(E)], (E, P))),
        "c_iota_p": f(np.arange(P)[None, :]),
        "c_ids": f((np.arange(NT)[None, :] * P + np.arange(P)[:, None] + 1)[:, :, None]),
        "c_empty": f(S + 1 + np.arange(P)[:, None]),
        "c_halves": f(np.concatenate([s <= mid, s > mid], 1)),
    }


def build(nc, io, out, dr):
    with ExitStack() as ctx:
        sb = lambda n, s: ctx.enter_context(nc.sbuf_tensor(n, s, F32))
        keep = {"ident": sb("ident", [P, P]), "upper": sb("upper", [P, P]), "eps": sb("eps", [P, 4])}
        consts_in = ctx.enter_context(nc.semaphore("masks_in"))
        eps_done = ctx.enter_context(nc.semaphore("eps_done"))
        with nc.Block() as block:
            @block.sync
            def _(sp):
                sp.dma_start(keep["ident"][:], io["c_ident"]).then_inc(consts_in, 16)
                sp.dma_start(keep["upper"][:], io["c_upper"]).then_inc(consts_in, 16)
                sp.wait_ge(consts_in, 32)

            @block.vector
            def _(dve):
                dve.memset(keep["eps"][:, 0:1], RMS_EPS)
                dve.memset(keep["eps"][:, 1:2], LN_EPS)
                dve.memset(keep["eps"][:, 2:3], 64e-5).then_inc(eps_done, 1)
                dve.wait_ge(eps_done, 1)
        make_rows(nc, io, dr)
        with ExitStack() as qkv:
            for n, s in (("qT", [P, AH, S]), ("kT", [P, AH, S]), ("v", [P, NT, AW])):
                keep[n] = qkv.enter_context(nc.sbuf_tensor(n, s, F32))
            project(nc, io, dr, keep)
            attend(nc, io, dr, keep)
        rwkv(nc, io, dr, keep)
        for n, s in (("posm", [P, NT, E]), ("W", [P, NT, E]), ("seen", [P, E]), ("base", [P, NB])):
            keep[n] = sb(n, s)
        keep["tab"] = ctx.enter_context(nc.sbuf_tensor("tab", [1, 3, NB], mybir.dt.int32))
        norm_route(nc, io, dr, keep)
        schedule(nc, io, dr, keep)
        experts(nc, io, dr, keep)
        finish(nc, io, dr, keep, out)


DUMP = ["rows", "pb", "ymix", "x2", "h2", "acc", "out_x"]
_INS = ['x', 'c', 'w_ada', 'b_ada', 'norm_pre_mix', 'norm_post_mix', 'norm_pre_ffn', 'norm_post_ffn',
        'w_in', 'w_out', 'rel_bias_table', 'diff_lambda', 'diff_subln', 'rwkv_mu', 'rwkv_w0', 'rwkv_w2', 'rwkv_a0', 'rwkv_a2',
        'rwkv_g2', 'rwkv_k_k', 'rwkv_k_a', 'rwkv_r_k', 'rwkv_lnx_g', 'rwkv_lnx_b', 'gmlp_ln_g', 'gmlp_ln_b', 'gmlp_w_s', 'gmlp_b_s',
        'router_w', 'router_bias', 'exp_w1', 'exp_w3', 'exp_w2', 'shared_w1', 'shared_w3', 'shared_w2']


def kernel(**inputs):
    import concourse.bacc as bacc
    from concourse.bass_utils import run_bass_kernel_spmd

    nc = bacc.Bacc("TRN2", target_bir_lowering=False, num_devices=1)
    arrays, io = {}, {}
    for name, a in [(n, np.ascontiguousarray(inputs[n])) for n in _INS] + list(constants().items()):
        arrays[f"in_{name}"] = a
        io[name] = nc.dram_tensor(f"in_{name}", a.shape, mybir.dt.from_np(a.dtype), kind="ExternalInput").ap()
    out = nc.dram_tensor("out_x", (1, S, D), F32, kind="ExternalOutput").ap()
    dr = {
        "rows": nc.dram_tensor("rows", (1, 6 * D), F32).ap(),
        "pb": nc.dram_tensor("pb", (S + 1, B_COLS), F32).ap(),
        "bias_by_dist": nc.dram_tensor("bias_by_dist", (AH, P, 3 * P), F32).ap(),
        "x2": nc.dram_tensor("x2", (S, D), F32).ap(),
        "h2": nc.dram_tensor("h2", (S + P, D), F32).ap(),
        "acc": nc.dram_tensor("acc", (S + P, D), F32).ap(),
        "ymix": nc.dram_tensor("ymix", (S, D), F32).ap(),
    }
    build(nc, io, out, dr)
    r = run_bass_kernel_spmd(nc, [arrays], core_ids=[0])
    return r.results[0]["out_x"]
```

```python
import concourse.bass as bass
from concourse import mybir
from contextlib import ExitStack
import math
import numpy as np

F32 = mybir.dt.float32
F32R = mybir.dt.float32r
ALU = mybir.AluOpType
ACT = mybir.ActivationFunctionType
AX = mybir.AxisListType

P = 128
D = 1024
S = 1024
NT = S // P
KC = D // P
BANK = 512
AH, AQK = 4, 64
AW = AH * 2 * AQK
BH, BD = 4, 64
BW = BH * BD
CG, CD = 4, 64
CW = CG * CD
A_COLS, B_COLS = 3 * AW, 3 * BW + 64 + 64 + 128
RMS_EPS = 1e-6
LN_EPS = 1e-5
EXP_AND_LN = 6
GELU_1 = 2.0 * math.sqrt(2.0 / math.pi)
GELU_3 = GELU_1 * 0.044715


class Steps:

    def __init__(self, eng, sem):
        self.eng, self.sem, self.n = eng, sem, 0

    def then(self, ins):
        self.n += 1
        ins.then_inc(self.sem, 1)
        self.eng.wait_ge(self.sem, self.n)

    def restart(self):
        self.eng.sem_inc(self.sem, 1)
        self.eng.sem_clear(self.sem)
        self.n = 0


def make_rows(nc, io, dr, keep):
    NCH = 6 * D // BANK
    with ExitStack() as ctx:
        sb = lambda n, s: ctx.enter_context(nc.sbuf_tensor(n, s, F32))
        sem = lambda n: ctx.enter_context(nc.semaphore(n))
        c_col = sb("c_col", [P, KC])
        e_col = sb("e_col", [P, KC])
        cond = sb("cond", [P, KC, P])
        w = [sb(f"w_ada{j}", [P, KC, BANK]) for j in range(2)]
        mod = sb("mod", [P, 6 * D])
        gains = keep["qT"]
        ps = [ctx.enter_context(nc.psum_tensor(f"ps_mod{j}", [P, BANK], F32)) for j in range(2)]
        c_in, gains_in, cond_ready = sem("c_in"), sem("gains_in"), sem("cond_ready")
        w_in = [sem(f"w_ada_in{j}") for j in range(2)]
        mod_mm = [sem(f"mod_mm{j}") for j in range(2)]
        mod_read = [sem(f"mod_read{j}") for j in range(2)]
        c_low = sem("c_low")
        exp_done, dve_step, rows_ready, rows_out = sem("exp_done"), sem("dve_step"), sem("rows_ready"), sem("rows_out")
        w_view = io["w_ada"][0].rearrange("(k p) n -> p k n", p=P)
        block = ctx.enter_context(nc.Block())

        @block.sync
        def _(sp):
            sp.dma_start(c_col[:], io["c"].rearrange("a (k p) -> p (a k)", p=P), allow_slow_non_contiguous=True).then_inc(c_in, 16)
            sp.dma_start(mod[:], io["b_ada"][0:1, :].partition_broadcast(P)).then_inc(gains_in, 16)
            for n, name in enumerate(("norm_pre_mix", "norm_post_mix", "norm_pre_ffn", "norm_post_ffn")):
                sp.dma_start(gains[:, n, :], io[name][0:1, :].partition_broadcast(P)).then_inc(gains_in, 16)
            with sp.Fori(0, NCH // 2) as i:
                for j in range(2):
                    sp.wait_ge(mod_mm[j], i + 1)
                    sp.dma_start(w[j][:], w_view[:, :, bass.ds((i * 2 + j) * BANK, BANK)]).then_inc(w_in[j], 16)
            for k in range(KC // 2):
                sp.dma_start(keep["w_in"][:, k, :], io["w_in"][0].rearrange("(k p) n -> p k n", p=P)[:, k, :]).then_inc(keep["w_loaded"], 16)
            sp.wait_ge(rows_ready, 1)
            sp.dma_start(dr["rows"], mod[0:1, :]).then_inc(rows_out, 16)
            sp.wait_ge(rows_out, 16)

        @block.scalar
        def _(act):
            act.wait_ge(c_low, 1)
            act.activation(e_col[:], e_col[:], ACT.Exp, scale=-1.0).then_inc(exp_done, 1)

        @block.tensor
        def _(pe):
            pe.sem_inc(mod_mm[0], 1)
            pe.sem_inc(mod_mm[1], 1)
            pe.wait_ge(cond_ready, 1)
            with pe.Fori(0, NCH // 2) as i:
                for j in range(2):
                    pe.wait_ge(w_in[j], i * 16 + 16)
                    pe.wait_ge(mod_read[j], i + 1)
                    for k in range(KC):
                        mm = pe.matmul(ps[j][:], cond[:, k, :], w[j][:, k, :], start=(k == 0), stop=(k == KC - 1))
                    mm.then_inc(mod_mm[j], 1)

        @block.vector
        def _(dve):
            step = Steps(dve, dve_step)
            dve.sem_inc(mod_read[0], 1)
            dve.sem_inc(mod_read[1], 1)
            dve.wait_ge(c_in, 16)
            dve.tensor_scalar(e_col[:], c_col[:], -80.0, None, ALU.max).then_inc(c_low, 1)
            dve.wait_ge(exp_done, 1)
            step.then(dve.tensor_scalar(e_col[:], e_col[:], 1.0, None, ALU.add))
            step.then(dve.reciprocal(e_col[:], e_col[:]))
            step.then(dve.tensor_tensor(c_col[:], c_col[:], e_col[:], ALU.mult))
            dve.tensor_copy(cond[:], c_col[:].unsqueeze(2).to_broadcast([P, KC, P])).then_inc(cond_ready, 1)
            dve.wait_ge(gains_in, 16 * 5)
            with dve.Fori(0, NCH // 2) as i:
                for j in range(2):
                    dve.wait_ge(mod_mm[j], i + 2)
                    m = mod[:, bass.ds((i * 2 + j) * BANK, BANK)]
                    dve.tensor_tensor(m, ps[j][:], m, ALU.add).then_inc(mod_read[j], 1)
            for j in range(2):
                dve.wait_ge(mod_read[j], NCH // 2 + 1)
            row = lambda n: mod[:, n * D:(n + 1) * D]
            for half in range(2):
                step.then(dve.scalar_tensor_tensor(row(3 * half + 1), row(3 * half + 1), 1.0, gains[:, 2 * half, :], ALU.add, ALU.mult))
                step.then(dve.tensor_tensor(row(3 * half + 2), row(3 * half + 2), gains[:, 2 * half + 1, :], ALU.mult))
            dve.sem_inc(rows_ready, 1)


def project(nc, io, dr, keep):
    GROUPS = 6
    with ExitStack() as ctx:
        sb = lambda n, s: ctx.enter_context(nc.sbuf_tensor(n, s, F32))
        sem = lambda n: ctx.enter_context(nc.semaphore(n))
        pt = lambda n: ctx.enter_context(nc.psum_tensor(n, [P, BANK], F32))
        w, w_loaded = keep["w_in"], keep["w_loaded"]
        shift, scale = sb("shift1", [P, D]), sb("scale1", [P, D])
        ln_g, ln_b, b_s = sb("ln_g", [P, CW]), sb("ln_b", [P, CW]), sb("b_s", [P, CG])
        w_s, w_sT = sb("w_s", [P, CG, P]), sb("w_sT", [P, CG, P])
        x = sb("x_tile", [P, D])
        h = sb("h_tile", [P, D])
        hT = [sb(f"hT{j}", [P, KC, P]) for j in range(2)]
        pb = sb("pb_tile", [P, 2 * BANK])
        z, zt = sb("z", [P, 2 * CW]), sb("zt", [P, 2 * CW])
        st = sb("stats", [P, 8])
        yc = sb("yc", [P, CW])
        ident, upper = keep["ident"], keep["upper"]
        ps_t = [pt(f"ps_t{n}") for n in range(2)]
        ps_p = [pt(f"ps_p{n}") for n in range(4)]
        ps_s = pt("ps_s")
        consts_in, x_in, ss_ready = sem("consts_in"), sem("x_in"), sem("ss_ready")
        act_step, dve_step = sem("act_step"), sem("dve_step")
        rstd_ready, h_ready, tr_done, hT_ready = sem("rstd_ready"), sem("h_ready"), sem("tr_done"), sem("hT_ready")
        proj_mm, proj_read, pb_out, x_read = sem("proj_mm"), sem("proj_read"), sem("pb_out"), sem("x_read")
        arg_ready, e_ready, var_in, v_rstd = sem("arg_ready"), sem("e_ready"), sem("var_in"), sem("v_rstd")
        v_ready, sv_mm, yc_ready, yc_out, wsT_done, wsT_mm = sem("v_ready"), sem("sv_mm"), sem("yc_ready"), sem("yc_out"), sem("wsT_done"), sem("wsT_mm")
        z_read, pb_free, yc_free = sem("z_read"), sem("pb_free"), sem("yc_free")
        x_view = io["x"][0]
        block = ctx.enter_context(nc.Block())

        @block.sync
        def _(sp):
            sp.dma_start(shift[:], dr["rows"][:, 0:D].partition_broadcast(P)).then_inc(consts_in, 16)
            sp.dma_start(scale[:], dr["rows"][:, D:2 * D].partition_broadcast(P)).then_inc(consts_in, 16)
            sp.dma_start(w_s[:], io["gmlp_w_s"][0].rearrange("g t s -> t g s")).then_inc(consts_in, 16)
            sp.dma_start(ln_g[:], io["gmlp_ln_g"][0:1, :].partition_broadcast(P)).then_inc(consts_in, 16)
            sp.dma_start(ln_b[:], io["gmlp_ln_b"][0:1, :].partition_broadcast(P)).then_inc(consts_in, 16)
            sp.dma_start(b_s[:], io["gmlp_b_s"][0].rearrange("g t -> t g"), allow_slow_non_contiguous=True).then_inc(consts_in, 16)
            sp.dma_start(x[:], x_view[0:P, :]).then_inc(x_in, 16)
            for k in range(KC // 2, KC):
                sp.dma_start(w[:, k, :], io["w_in"][0].rearrange("(k p) n -> p k n", p=P)[:, k, :]).then_inc(w_loaded, 16)
            with sp.Fori(1, NT) as t:
                sp.wait_ge(x_read, t + 1)
                sp.dma_start(x[:], x_view[bass.ds(t * P, P), :]).then_inc(x_in, 16)
            sp.wait_ge(x_in, 16 * NT)

        @block.gpsimd
        def _(pool):
            pool.sem_inc(pb_free, 1)
            pool.sem_inc(yc_free, 1)
            with pool.Fori(0, NT) as t:
                pool.wait_ge(proj_read, t * GROUPS + 4 + 6)
                pool.dma_start(dr["pb"][bass.ds(t * P + 1, P), :], pb[:]).then_inc(pb_out, 16)
                pool.wait_ge(pb_out, t * 16 + 16)
                pool.sem_inc(pb_free, 1)
                pool.wait_ge(yc_ready, t + 1)
                pool.dma_start(dr["ymix"][bass.ds(t * P, P), AW + BW:D], yc[:]).then_inc(yc_out, 16)
                pool.wait_ge(yc_out, t * 16 + 16)
                pool.sem_inc(yc_free, 1)

        @block.scalar
        def _(act):
            load_exp_and_ln(nc, act)
            step = Steps(act, act_step)
            act.sem_inc(proj_read, 4)

            def norm(t):
                act.wait_ge(x_in, t * 16 + 16)
                act.wait_ge(h_ready, t + 1)
                act.wait_ge(tr_done, t + 1)
                step.then(act.activation(h[:], x[:], ACT.Square, accum_out=st[:, 0:1]))
                step.then(act.activation(st[:, 1:2], st[:, 0:1], ACT.Ln, scale=1.0 / D, bias=keep["eps"][:, 0:1]))
                act.activation(st[:, 2:3], st[:, 1:2], ACT.Exp, scale=-0.5).then_inc(rstd_ready, 1)

            def pair(i, last):
                for j in range(2):
                    t = i * 2 + j
                    if not (last and j):
                        norm(t + 1)
                    for g in range(GROUPS):
                        act.wait_ge(proj_mm, i * (2 * GROUPS) + j * GROUPS + g + 1)
                        src = ps_p[(j * GROUPS + g) % 4]
                        if g == 0:
                            act.wait_ge(z_read, t + 1)
                            act.copy(z[:], src[:]).then_inc(proj_read, 1)
                        elif g < 3:
                            dst = (keep["qT"], keep["kT"])[g - 1]
                            act.copy(dst[:, :, bass.ds(t * P, P)], src[:].rearrange("p (h n) -> p h n", h=AH)).then_inc(proj_read, 1)
                        elif g == 3:
                            act.copy(keep["v"][:, bass.ds(t, 1), :], src[:].unsqueeze(1)).then_inc(proj_read, 1)
                        else:
                            act.wait_ge(pb_free, t + 1)
                            act.copy(pb[:, (g - 4) * BANK:(g - 3) * BANK], src[:]).then_inc(proj_read, 1)
                        if g == 1:
                            act.wait_ge(arg_ready, t + 1)
                            act.activation(zt[:], zt[:], ACT.Exp, scale=-1.0).then_inc(e_ready, 1)
                        if g == 2:
                            act.wait_ge(var_in, t + 1)
                            step.then(act.activation(zt[:, 0:CW], z[:, CW:2 * CW], ACT.Square, accum_out=st[:, 5:6]))
                            step.then(act.activation(st[:, 6:7], st[:, 5:6], ACT.Ln, scale=1.0 / CW, bias=keep["eps"][:, 1:2]))
                            act.activation(st[:, 7:8], st[:, 6:7], ACT.Exp, scale=-0.5).then_inc(v_rstd, 1)
                step.restart()

            norm(0)
            step.restart()
            with act.Fori(0, NT // 2 - 1) as i:
                pair(i, False)
            pair(NT // 2 - 1, True)

        @block.vector
        def _(dve):
            step = Steps(dve, dve_step)
            for s in (h_ready, x_read, z_read):
                dve.sem_inc(s, 1)
            dve.sem_inc(hT_ready, 2)
            dve.wait_ge(consts_in, 16 * 6)
            dve.wait_ge(wsT_mm, 1)
            dve.tensor_tensor(w_sT[:], ps_t[0][:].rearrange("p (g n) -> p g n", g=CG),
                              upper[:].unsqueeze(1).to_broadcast([P, CG, P]), ALU.mult).then_inc(wsT_done, 1)

            def scale_shift(t):
                dve.wait_ge(rstd_ready, t + 1)
                dve.scalar_tensor_tensor(h[:], x[:], st[:, 2:3], scale[:], ALU.mult, ALU.mult).then_inc(x_read, 1)
                dve.wait_ge(x_read, t + 2)
                dve.tensor_tensor(h[:], h[:], shift[:], ALU.add).then_inc(h_ready, 1)

            def copy_transposed(t, j):
                dve.wait_ge(tr_done, t + 2)
                for half in range(2):
                    dve.tensor_copy(hT[j][:, 4 * half:4 * half + 4, :], ps_t[half][:].rearrange("p (k n) -> p k n", k=4)).then_inc(hT_ready, 1)

            def pair(i, last):
                for j in range(2):
                    t = i * 2 + j
                    if not (last and j):
                        scale_shift(t + 1)
                    dve.wait_ge(proj_read, i * (2 * GROUPS) + j * GROUPS + 1 + 4)
                    step.then(dve.tensor_tensor(zt[:], z[:], z[:], ALU.mult))
                    step.then(dve.tensor_scalar(zt[:], zt[:], GELU_3, GELU_1, ALU.mult, ALU.add))
                    step.then(dve.tensor_tensor(zt[:], zt[:], z[:], ALU.mult))
                    dve.tensor_scalar(zt[:], zt[:], -80.0, None, ALU.max).then_inc(arg_ready, 1)
                    dve.wait_ge(e_ready, t + 1)
                    step.then(dve.tensor_scalar(zt[:], zt[:], 1.0, None, ALU.add))
                    step.then(dve.reciprocal(zt[:], zt[:]))
                    step.then(dve.tensor_tensor(z[:], z[:], zt[:], ALU.mult))
                    v = z[:, CW:2 * CW]
                    step.then(dve.tensor_reduce(st[:, 3:4], v, AX.X, ALU.add))
                    step.then(dve.tensor_scalar(st[:, 4:5], st[:, 3:4], -1.0 / CW, None, ALU.mult))
                    dve.tensor_scalar(v, v, st[:, 4:5], None, ALU.add).then_inc(var_in, 1)
                    dve.wait_ge(v_rstd, t + 1)
                    step.then(dve.scalar_tensor_tensor(v, v, st[:, 7:8], ln_g[:], ALU.mult, ALU.mult))
                    dve.tensor_tensor(v, v, ln_b[:], ALU.add).then_inc(v_ready, 1)
                    if not (last and j):
                        copy_transposed(t + 1, 1 - j)
                    dve.wait_ge(sv_mm, t + 1)
                    dve.wait_ge(yc_free, t + 1)
                    for g in range(CG):
                        c = slice(g * CD, (g + 1) * CD)
                        step.then(dve.scalar_tensor_tensor(yc[:, c], ps_s[:, c], b_s[:, g:g + 1], z[:, c], ALU.add, ALU.mult))
                    dve.sem_inc(z_read, 1)
                    dve.sem_inc(yc_ready, 1)
                step.restart()

            scale_shift(0)
            copy_transposed(0, 0)
            with dve.Fori(0, NT // 2 - 1) as i:
                pair(i, False)
            pair(NT // 2 - 1, True)

        @block.tensor
        def _(pe):
            for s in (tr_done,):
                pe.sem_inc(s, 1)
            pe.wait_ge(consts_in, 16 * 6)
            for g in range(CG):
                mm = pe.transpose(ps_t[0][:, g * P:(g + 1) * P], w_s[:, g, :], ident[:])
            mm.then_inc(wsT_mm, 1)
            pe.wait_ge(wsT_done, 1)
            cols = [A_COLS + B_COLS, 0, AW, 2 * AW, A_COLS, A_COLS + BANK]

            def transposes(t):
                pe.wait_ge(h_ready, t + 2)
                pe.wait_ge(hT_ready, t * 2 + 2)
                for k in range(KC):
                    tr = pe.transpose(ps_t[k // 4][:, (k % 4) * P:(k % 4 + 1) * P], h[:, k * P:(k + 1) * P], ident[:])
                tr.then_inc(tr_done, 1)

            def pair(i, last):
                for j in range(2):
                    t = i * 2 + j
                    pe.wait_ge(hT_ready, t * 2 + 4)
                    for g in range(GROUPS):
                        out = ps_p[(j * GROUPS + g) % 4]
                        pe.wait_ge(proj_read, i * (2 * GROUPS) + j * GROUPS + g + 1)
                        if g in (1, 2):
                            for c in range(AH):
                                for k in range(KC):
                                    mm = pe.matmul(out[:, c * P:(c + 1) * P], w[:, k, cols[g] + c * P:cols[g] + (c + 1) * P], hT[j][:, k, :],
                                                   start=(k == 0), stop=(k == KC - 1))
                        else:
                            for k in range(KC):
                                mm = pe.matmul(out[:], hT[j][:, k, :], w[:, k, cols[g]:cols[g] + BANK], start=(k == 0), stop=(k == KC - 1))
                        mm.then_inc(proj_mm, 1)
                        if g == 2 and not (last and j):
                            transposes(t + 1)
                    pe.wait_ge(v_ready, t + 1)
                    pe.wait_ge(z_read, t + 1)
                    for g in range(CG):
                        mm = pe.matmul(ps_s[:, g * CD:(g + 1) * CD], w_sT[:, g, :], z[:, CW + g * CD:CW + (g + 1) * CD], start=True, stop=True)
                    mm.then_inc(sv_mm, 1)

            transposes(0)
            pe.wait_ge(w_loaded, 16 * KC)
            with pe.Fori(0, NT // 2 - 1) as i:
                pair(i, False)
            pair(NT // 2 - 1, True)


LAMBDA_INIT = 0.8 - 0.6 * math.exp(-0.3 * 0)
N_BUCKETS, MAX_DISTANCE = 32, 128
NEG = -1e30


def load_exp_and_ln(nc, act):
    act.add_instruction(mybir.InstLoadActFuncSet(act_func_set_id=EXP_AND_LN, name=nc.get_next_instruction_name(),
                                                 engine=mybir.EngineType.Activation))


class Stages:

    def __init__(self, sem, names):
        self.sem, self.names, self.n = sem, names, len(names)
        self.built = 0

    def start(self, eng):
        eng.sem_inc(self.sem, self.n)

    def done(self, ins, name):
        assert self.names[self.built % self.n] == name, (name, self.names[self.built % self.n])
        self.built += 1
        return ins.then_inc(self.sem, 1)

    def wait(self, eng, turn, name):
        eng.wait_ge(self.sem, turn * self.n + self.n + self.names.index(name) + 1)

    def wait_before(self, eng, turn, name):
        eng.wait_ge(self.sem, turn * self.n + self.names.index(name) + 1)


def attend(nc, io, dr, keep):
    with ExitStack() as ctx:
        sb = lambda n, s: ctx.enter_context(nc.sbuf_tensor(n, s, F32))
        sem = lambda n: ctx.enter_context(nc.semaphore(n))
        pt = lambda n, b=1: ctx.enter_context(nc.psum_tensor(n, [P, b * BANK], F32))
        ident = keep["ident"]
        table, oh = sb("table", [N_BUCKETS + 1, AH]), sb("onehot", [N_BUCKETS + 1, 3 * P])
        rv = sb("bias_rows", [P, AH, 3 * P])
        table_b = sb("table_b", [N_BUCKETS + 1, AH, P])
        bias = sb("bias", [P, AH, 2 * P])
        lp, lam = sb("lambda_par", [P, 4, AQK]), sb("lambda", [P, 4])
        gain = sb("subln", [P, 2 * AQK])
        q, k, v = sb("q_head", [P, S]), sb("k_head", [P, S]), sb("v_head", [P, NT, P])
        p = [[sb(f"p{b}{m}", [P, S]) for m in range(2)] for b in range(2)]
        attn = [sb(f"attn{b}", [P, S]) for b in range(2)]
        aT = [sb(f"attnT{b}", [P, NT, P]) for b in range(2)]
        o = [sb(f"o{b}", [P, P]) for b in range(2)]
        junk = sb("squares", [P, P])
        st = [sb(f"soft_stats{b}", [P, 12]) for b in range(4)]
        ps_s = [pt(f"ps_scores{m}", 2) for m in range(2)]
        ps_t = [pt(f"ps_attnT{b}") for b in range(2)]
        ps_o = [pt(f"ps_o{b}") for b in range(2)]
        consts_in, table_done, rv_mm, rv_ready, rv_out, bias_in = (sem(n) for n in (
            "att_consts_in", "table_done", "rv_mm", "rv_ready", "rv_out", "bias_in"))
        lam_dot, lam_exp, gain_done, dve_step, act_step, o_out = (sem(n) for n in (
            "lam_dot", "lam_exp", "gain_done", "att_dve_step", "att_act_step", "o_out"))
        qk_in, v_in = sem("qk_copied"), sem("v_copied")
        s_mm = sem("scores_mm")
        s_max = sem("scores_max")
        s_exp = sem("scores_exp")
        a_ready = sem("attn_ready")
        t_mm = sem("attnT_mm")
        t_read = sem("attnT_copied")
        o_mm = sem("o_mm")
        o_rstd = sem("o_rstd")
        o_free = sem("o_free")
        o_ready = sem("o_ready")
        halves = lambda n: [(a, min(a + 4, n + 1)) for a in range(0, n + 1, 4)]
        T_HEAD = sum(len(halves(n)) for n in range(NT))
        t_before = lambda n: sum(len(halves(m)) for m in range(n))
        block = ctx.enter_context(nc.Block())

        @block.sync
        def _(sp):
            sp.dma_start(table[0:N_BUCKETS, :], io["rel_bias_table"]).then_inc(consts_in, 16)
            sp.dma_start(oh[:], io["c_onehot"]).then_inc(consts_in, 16)
            sp.dma_start(lp[:], io["diff_lambda"].rearrange("l a b -> l (a b)").partition_broadcast(P)).then_inc(consts_in, 16)
            sp.dma_start(gain[:], io["diff_subln"][0:1, :].partition_broadcast(P)).then_inc(consts_in, 16)
            sp.wait_ge(rv_ready, 1)
            sp.dma_start(dr["bias_by_dist"].rearrange("h p n -> p h n"), rv[:]).then_inc(rv_out, 16)
            sp.wait_ge(rv_out, 16)
            t = dr["bias_by_dist"]
            for h in range(AH):
                src = bass.AP(t.tensor, h * P * 3 * P + P - 1, [[3 * P - 1, P], [1, 2 * P]])
                sp.dma_start(bias[:, h, :], src).then_inc(bias_in, 16)
            sp.sem_inc(o_free, 2)
            with sp.Fori(0, AH) as h:
                for n in range(NT):
                    sp.wait_ge(o_ready, h * NT + n + 1)
                    sp.dma_start(dr["ymix"][n * P:(n + 1) * P, bass.ds(h * P, P)], o[n % 2][:]).then_inc(o_out, 16)
                    sp.wait_ge(o_out, (h * NT + n) * 16 + 16)
                    sp.sem_inc(o_free, 1)

        @block.scalar
        def _(act):
            load_exp_and_ln(nc, act)
            step = Steps(act, act_step)
            act.sem_inc(t_read, 2)
            act.sem_inc(s_exp, 2)
            act.wait_ge(lam_dot, 1)
            act.activation(lam[:, 2:4], lam[:, 0:2], ACT.Exp).then_inc(lam_exp, 1)

            def copy_qk(h):
                act.mul(q[:], keep["qT"][:, bass.ds(h, 1), :].squeeze(1), AQK ** -0.5).then_inc(qk_in, 1)
                act.copy(k[:], keep["kT"][:, bass.ds(h, 1), :].squeeze(1)).then_inc(qk_in, 1)

            def exponentials(h, n, m):
                L = (n + 1) * P
                act.wait_ge(s_max, h * (2 * NT) + 2 * n + m + 1)
                act.activation(p[n % 2][m][:, 0:L], ps_s[m][:, 0:L], ACT.Exp, bias=st[n % 4][:, m:m + 1],
                               accum_out=st[n % 4][:, 2 + m:3 + m]).then_inc(s_exp, 1)

            copy_qk(0)
            with act.Fori(0, AH) as h:
                for it in range(NT + 3):
                    if it == 1:
                        act.wait_ge(o_mm, h * NT + 1)
                        act.copy(v[:], keep["v"][:, :, bass.ds(h * P, P)]).then_inc(v_in, 1)
                    if it == NT:
                        with act.If(h < AH - 1):
                            act.wait_ge(s_mm, h * (2 * NT) + 2 * NT)
                            copy_qk(nc.s_assert_within(h + 1, 1, AH - 1, skip_runtime_bounds_check_because="the branch is taken below the last head"))
                    if it < NT:
                        if it >= 2:
                            act.wait_ge(a_ready, h * NT + it - 1)
                        exponentials(h, it, 0)
                    if 2 <= it <= NT + 1:
                        n = it - 2
                        if n >= 2:
                            act.wait_ge(o_mm, h * NT + n - 1 + 1)
                        for x, (a, z) in enumerate(halves(n)):
                            c = t_before(n) + x
                            act.wait_ge(t_mm, h * T_HEAD + c + 1)
                            act.copy(aT[n % 2][:, a:z, :], ps_t[c % 2][:, 0:(z - a) * P].rearrange("p (a n) -> p a n", n=P)).then_inc(t_read, 1)
                    if it < NT:
                        exponentials(h, it, 1)
                    if it >= 3:
                        n = it - 3
                        s = st[n % 4]
                        act.wait_ge(o_mm, h * NT + n + 1 + 1)
                        step.then(act.activation(junk[:], ps_o[n % 2][:, 0:P], ACT.Square, accum_out=s[:, 8:9]))
                        step.then(act.activation(s[:, 9:10], s[:, 8:9], ACT.Ln, scale=1.0 / P, bias=keep["eps"][:, 0:1]))
                        act.activation(s[:, 10:11], s[:, 9:10], ACT.Exp, scale=-0.5).then_inc(o_rstd, 1)
                step.restart()

        @block.vector
        def _(dve):
            step = Steps(dve, dve_step)
            dve.memset(table[N_BUCKETS:N_BUCKETS + 1, :], NEG).then_inc(table_done, 1)
            dve.wait_ge(consts_in, 64)
            dve.wait_ge(table_done, 1)
            dve.tensor_copy(table_b[:], table[:].unsqueeze(2).to_broadcast([N_BUCKETS + 1, AH, P])).then_inc(table_done, 1)
            step.then(dve.tensor_tensor(lp[:, 0, :], lp[:, 0, :], lp[:, 1, :], ALU.mult))
            step.then(dve.tensor_tensor(lp[:, 2, :], lp[:, 2, :], lp[:, 3, :], ALU.mult))
            step.then(dve.tensor_reduce(lam[:, 0:1], lp[:, 0, :], AX.X, ALU.add))
            dve.tensor_reduce(lam[:, 1:2], lp[:, 2, :], AX.X, ALU.add).then_inc(lam_dot, 1)
            dve.wait_ge(lam_exp, 1)
            step.then(dve.tensor_tensor(lam[:, 0:1], lam[:, 3:4], lam[:, 2:3], ALU.subtract))
            step.then(dve.tensor_scalar(lam[:, 0:1], lam[:, 0:1], -LAMBDA_INIT, None, ALU.add))
            step.then(dve.tensor_scalar(gain[:], gain[:], 1.0 - LAMBDA_INIT, None, ALU.mult))
            dve.wait_ge(rv_mm, 1)
            rv_ps = [ps_s[0][:, 0:BANK], ps_s[0][:, BANK:], ps_s[1][:, 0:BANK], ps_s[1][:, BANK:]]
            for h in range(AH):
                q = dve.tensor_copy(rv[:, h, :], rv_ps[h][:, 0:3 * P])
            step.then(q)
            for h in range(AH):
                q = dve.tensor_scalar(rv[:, h, 1:], rv[:, h, 1:], rv[:, h, 0:1], None, ALU.subtract)
            step.then(q)
            dve.memset(rv[:, :, 0:1], 0.0).then_inc(rv_ready, 1)
            dve.wait_ge(bias_in, 16 * AH)
            step.restart()
            with dve.Fori(0, AH) as h:
                for it in range(NT + 3):
                    if it < NT:
                        n, s, L = it, st[it % 4], (it + 1) * P
                        w = min(L, 2 * P)
                        if n >= 4:
                            dve.wait_ge(o_ready, h * NT + n - 3)
                        for m in range(2):
                            dve.wait_ge(s_mm, h * (2 * NT) + 2 * n + m + 1)
                            near = ps_s[m][:, L - w:L]
                            step.then(dve.tensor_tensor(near, near, bias[:, bass.ds(h, 1), 2 * P - w:2 * P].squeeze(1), ALU.add))
                            dve.tensor_reduce(s[:, m:m + 1], ps_s[m][:, 0:L], AX.X, ALU.max, negate=True).then_inc(s_max, 1)
                    if 1 <= it <= NT:
                        n, b, s, L = it - 1, (it - 1) % 2, st[(it - 1) % 4], it * P
                        dve.wait_ge(s_exp, h * (2 * NT) + 2 * n + 2 + 2)
                        if n >= 2:
                            dve.wait_ge(t_mm, h * T_HEAD + t_before(n - 1))
                        step.then(dve.reciprocal(s[:, 4:6], s[:, 2:4]))
                        step.then(dve.tensor_tensor(s[:, 6:7], s[:, 5:6], lam[:, 0:1], ALU.mult))
                        step.then(dve.tensor_scalar(attn[b][:, 0:L], p[b][0][:, 0:L], s[:, 4:5], None, ALU.mult))
                        dve.scalar_tensor_tensor(attn[b][:, 0:L], p[b][1][:, 0:L], s[:, 6:7], attn[b][:, 0:L], ALU.mult, ALU.add).then_inc(a_ready, 1)
                    if it >= 3:
                        n = it - 3
                        dve.wait_ge(o_rstd, h * NT + n + 1)
                        dve.wait_ge(o_free, h * NT + n + 1)
                        dve.scalar_tensor_tensor(o[n % 2][:], ps_o[n % 2][:, 0:P], st[n % 4][:, 10:11], gain[:], ALU.mult, ALU.mult).then_inc(o_ready, 1)
                step.restart()

        @block.tensor
        def _(pe):
            pe.sem_inc(o_mm, 1)
            pe.wait_ge(consts_in, 64)
            pe.wait_ge(table_done, 2)
            for h in range(AH):
                mm = pe.matmul(ps_s[h // 2][:, (h % 2) * BANK:(h % 2) * BANK + 3 * P], table_b[:, h, :], oh[:], start=True, stop=True)
            mm.then_inc(rv_mm, 1)
            pe.wait_ge(rv_ready, 1)
            with pe.Fori(0, AH) as h:
                pe.wait_ge(qk_in, h * 2 + 2)
                for it in range(NT + 2):
                    if it < NT:
                        n, L = it, (it + 1) * P
                        for m in range(2):
                            pe.wait_ge(s_exp, h * (2 * NT) + 2 * n + m - 2 + 1 + 2)
                            r = slice(m * AQK, (m + 1) * AQK)
                            for a in range(0, L, BANK):
                                z = min(a + BANK, L)
                                mm = pe.matmul(ps_s[m][:, a:z], q[r, n * P:(n + 1) * P], k[r, a:z], start=True, stop=True)
                            mm.then_inc(s_mm, 1)
                    if it >= 2:
                        n = it - 2
                        if n == 0:
                            pe.wait_ge(v_in, h + 1)
                        pe.wait_ge(a_ready, h * NT + n + 1)
                        for x, (a, z) in enumerate(halves(n)):
                            c = t_before(n) + x
                            pe.wait_ge(t_read, h * T_HEAD + c + 1)
                            for kt in range(a, z):
                                tr = pe.transpose(ps_t[c % 2][:, (kt - a) * P:(kt - a + 1) * P], attn[n % 2][:, kt * P:(kt + 1) * P], ident[:])
                            tr.then_inc(t_mm, 1)
                        if n >= 2:
                            pe.wait_ge(o_ready, h * NT + n - 1)
                        for x, (a, z) in enumerate(halves(n)):
                            pe.wait_ge(t_read, h * T_HEAD + t_before(n) + x + 1 + 2)
                            for kt in range(a, z):
                                mm = pe.matmul(ps_o[n % 2][:, 0:P], aT[n % 2][:, kt, :], v[:, kt, :], start=(kt == 0), stop=(kt == n))
                        mm.then_inc(o_mm, 1)


class Lane:

    def __init__(self, sb, bank, j):
        f = lambda n, *s: sb(f"{n}{j}", [P, *s])
        self.bank = bank[4 * j:4 * j + 4]
        self.cur, self.prev, self.p = f("pb_cur", B_COLS), f("pb_prev", B_COLS), f("p_mixed", B_COLS)
        self.lr, self.lrT = f("low_rank", 2 * P), f("low_rankT", 2 * P)
        self.wa, self.g, self.lw, self.cx = f("w_a", 2 * BW), f("gate", BW), f("log_decay", BW), f("cum_before", BW)
        self.kk, self.k2, self.tmp = f("kk", BW), f("k2", BW), f("tmp", BW)
        self.s4 = f("per_head", 8, BH)
        self.dec = f("decays", 3, BW)
        self.fs = f("state_factors", 4)
        self.ops = f("operands", 4, BW)
        self.arT, self.bkT = f("arT", 2, 2, P), f("bkT", 2, 2, P)
        self.gm = f("grams", BH, 4, P)
        self.A = f("A_ab", BH, P)
        self.Dm, self.DT, self.T, self.TT, self.Z, self.ZT = (f(n, BH, P) for n in ("pow", "powT", "T", "TT", "Z", "ZT"))
        self.O, self.OT = [f(f"off{n}_", BH, P) for n in range(3)], [f(f"offT{n}_", BH, P) for n in range(2)]
        self.Xs, self.Us, self.taT = f("X", BW), f("U", BW), f("taT", 2, P)
        self.Sc = f("state_mid", 2, BD)
        self.ys, self.yq, self.yo = f("y", BW), f("y_sq", BW), f("y_out", BW)

    def b4(self, n):
        return self.bank[n][:].rearrange("p (h n) -> p h n", h=BH)

    def bank_pair(self, n):
        return self.bank[n][:, 0:2 * BD].rearrange("p (a d) -> p a d", d=BD)


def in_lanes(*groups):
    return [f"{n}.{j}" for group in groups for j in range(2) for n in group.split()]


def rwkv(nc, io, dr, keep):
    HALF = math.exp(-0.5)
    TURNS = NT // 2
    with ExitStack() as ctx:
        sb = lambda n, s: ctx.enter_context(nc.sbuf_tensor(n, s, F32))
        sem = lambda n: ctx.enter_context(nc.semaphore(n))
        bank = [ctx.enter_context(nc.psum_tensor(f"bank{n}", [P, BANK], F32)) for n in range(8)]
        ident = keep["ident"]
        H4 = [P, BH, P]
        mu = sb("mu", [P, B_COLS])
        wa0 = sb("w0_a0", [P, 2 * BW])
        k_k, k_a, r_k, lnx_g, lnx_b = (sb(n, [P, BW]) for n in ("k_k", "k_a", "r_k", "lnx_g", "lnx_b"))
        wa2, g2 = sb("w2_a2", [P, BW]), sb("g2", [P, BW])
        mask4 = sb("mask4", [P, 4, P])
        masks = sb("masks", [P, 9, P])
        cum_m, halves_m = sb("cum_m", [P, P]), sb("halves_m", [P, 2])
        lane = [Lane(sb, bank, j) for j in range(2)]
        St = sb("state", [P, 2, BD])
        one = sb("one", [P, 1])
        zero = sb("zero_row", [1, B_COLS])
        consts_in, zero_done, zero_out, pool_done, dve_step, act_step = (sem(n) for n in (
            "rwkv_consts_in", "zero_done", "zero_out", "offs_done", "rwkv_dve_step", "rwkv_act_step"))
        w_out_in = sem("w_out_in")
        mix = sem("mix_done")
        load_in, y_out = ([sem(f"{n}{j}") for j in range(2)] for n in ("pb_in", "y_out"))
        PE = Stages(sem("pe_done"), in_lanes("lr_T", "lora", "cum", "operands_T", "grams", "A", "X", "sq0", "sq1", "sq2", "sq3",
                                             "z0", "m0", "z1", "m1", "z2", "m2", "ta", "U Y state"))
        V = Stages(sem("dve_done"), in_lanes("mixed lr_args", "lr", "wa", "logw", "kk_ss", "cx", "operands", "masked", "D0",
                                             "v0", "v1", "v2", "v3", "vz0", "vm0", "vz1", "vm1", "vz2", "vm2", "Sc U state", "var", "y"))
        C = Stages(sem("act_done"), in_lanes("lr_sig", "lrT", "g", "wa_sig", "kk_rstd", "decays", "opsT", "X", "c0", "c1", "c2",
                                             "cz0", "cz1", "ta", "y", "rstd"))
        h3 = lambda x: x.rearrange("p (h d) -> p h d", h=BH)
        hc = lambda h: slice(h * BD, (h + 1) * BD)
        half = lambda h: slice(64 * (h % 2), 64 * (h % 2) + 64)
        bc = lambda col: col.unsqueeze(2).to_broadcast([P, BH, BD])
        mb = lambda n: masks[:, n, :].unsqueeze(1).to_broadcast(H4)
        ib = ident[:].unsqueeze(1).to_broadcast(H4)
        by_parity = lambda x, e: x[:].rearrange("p (a e d) -> p e a d", e=2, d=BD)[:, e]
        pr = lambda n: io[n][0:1, :].partition_broadcast(P)
        block = ctx.enter_context(nc.Block())

        @block.sync
        def _(sp):
            for dst, src in ((mu[:], pr("rwkv_mu")), (wa0[:, 0:BW], pr("rwkv_w0")), (wa0[:, BW:], pr("rwkv_a0")),
                             (k_k[:], pr("rwkv_k_k")), (k_a[:], pr("rwkv_k_a")),
                             (r_k[:], io["rwkv_r_k"].rearrange("l a b -> l (a b)").partition_broadcast(P)),
                             (lnx_g[:], pr("rwkv_lnx_g")), (lnx_b[:], pr("rwkv_lnx_b")),
                             (wa2[0:64, :], io["rwkv_w2"][0]), (wa2[64:128, :], io["rwkv_a2"][0]), (g2[:], io["rwkv_g2"][0]),
                             (mask4[:], io["c_mask4"]), (masks[:], io["c_masks"]), (cum_m[:], io["c_cum"]), (halves_m[:], io["c_halves"])):
                sp.dma_start(dst, src).then_inc(consts_in, 16)
            sp.wait_ge(zero_done, 1)
            sp.dma_start(dr["pb"][0:1, :], zero[:]).then_inc(zero_out, 16)
            sp.wait_ge(zero_out, 16)
            with sp.Fori(0, TURNS) as i:
                for j in range(2):
                    V.wait_before(sp, i, f"mixed.{j}")
                    sp.dma_start(lane[j].cur[:], dr["pb"][bass.ds((i * 2 + j) * P + 1, P), :]).then_inc(load_in[j], 16)
                    sp.dma_start(lane[j].prev[:], dr["pb"][bass.ds((i * 2 + j) * P, P), :]).then_inc(load_in[j], 16)
            sp.dma_start(keep["w_out"][:], io["w_out"][0].rearrange("(k p) n -> p k n", p=P)).then_inc(w_out_in, 16)
            for j in range(2):
                sp.wait_ge(load_in[j], 32 * TURNS)
            sp.wait_ge(w_out_in, 16)

        @block.gpsimd
        def _(pool):
            pool.wait_ge(consts_in, 16 * 15)
            with pool.Fori(0, TURNS) as i:
                for j in range(2):
                    w = lane[j]
                    pool.wait_ge(load_in[j], i * 32 + 32)
                    pool.tensor_tensor(w.prev[:], w.prev[:], w.cur[:], ALU.subtract).then_inc(mix, 1)
                    pool.wait_ge(mix, i * 4 + 2 * j + 1)
                    pool.tensor_tensor(w.prev[:], w.prev[:], mu[:], ALU.mult).then_inc(mix, 1)
                for j in range(2):
                    w = lane[j]
                    V.wait(pool, i, f"D0.{j}")
                    PE.wait_before(pool, i, f"m2.{j}")
                    for n in range(3):
                        pool.tensor_tensor(w.O[n][:], w.A[:], mb(3 + 2 * n), ALU.mult).then_inc(pool_done, 1)
                        if n < 2:
                            pool.tensor_tensor(w.OT[n][:], w.gm[:, :, 0, :], mb(4 + 2 * n), ALU.mult).then_inc(pool_done, 1)

        @block.scalar
        def _(act):
            load_exp_and_ln(nc, act)
            step = Steps(act, act_step)
            C.start(act)

            def sigmoid(x, name):
                step.then(act.activation(x[:], x[:], ACT.Exp, scale=-1.0))
                step.then(act.activation(x[:], x[:], ACT.Ln, bias=one[:]))
                C.done(act.activation(x[:], x[:], ACT.Exp, scale=-1.0), name)

            with act.Fori(0, TURNS) as i:
                for j in range(2):
                    w = lane[j]
                    V.wait(act, i, f"lr_args.{j}")
                    sigmoid(w.lr, f"lr_sig.{j}")
                for j in range(2):
                    w = lane[j]
                    PE.wait(act, i, f"lr_T.{j}")
                    C.done(act.copy(w.lrT[:], w.bank[0][:, 0:2 * P]), f"lrT.{j}")
                for j in range(2):
                    w = lane[j]
                    PE.wait(act, i, f"lora.{j}")
                    V.wait_before(act, i, f"y.{j}")
                    C.done(act.copy(w.g[:], w.bank[3][:, 0:BW]), f"g.{j}")
                for j in range(2):
                    w = lane[j]
                    V.wait(act, i, f"wa.{j}")
                    sigmoid(w.wa, f"wa_sig.{j}")
                for j in range(2):
                    w = lane[j]
                    V.wait(act, i, f"kk_ss.{j}")
                    step.then(act.activation(w.s4[:, 1, :], w.s4[:, 0, :], ACT.Ln))
                    C.done(act.activation(w.s4[:, 2, :], w.s4[:, 1, :], ACT.Exp, scale=-0.5), f"kk_rstd.{j}")
                for j in range(2):
                    w = lane[j]
                    V.wait(act, i, f"cx.{j}")
                    PE.wait(act, i, f"cum.{j}")
                    act.activation(w.dec[:, 0, :], w.bank[1][:, 0:BW], ACT.Exp)
                    act.activation(w.dec[:, 1, :], w.bank[1][:, 0:BW], ACT.Exp, scale=-1.0)
                    act.activation(w.dec[:, 2, :], w.cx[:], ACT.Exp)
                    C.done(act.activation(w.fs[:], w.bank[2][:, 0:4], ACT.Exp), f"decays.{j}")
                for j in range(2):
                    w = lane[j]
                    PE.wait(act, i, f"operands_T.{j}")
                    act.copy(w.arT[:], w.bank[0][:].rearrange("p (a b n) -> p a b n", a=2, b=2))
                    C.done(act.copy(w.bkT[:], w.bank[3][:].rearrange("p (a b n) -> p a b n", a=2, b=2)), f"opsT.{j}")
                for j in range(2):
                    w = lane[j]
                    PE.wait(act, i, f"X.{j}")
                    C.done(act.copy(w.Xs[:], w.bank[3][:, 0:BW]), f"X.{j}")
                for n in range(3):
                    for j in range(2):
                        w = lane[j]
                        PE.wait(act, i, f"sq{n}.{j}")
                        C.done(act.copy(w.Dm[:], w.b4(0)), f"c{n}.{j}")
                for n in range(2):
                    for j in range(2):
                        w = lane[j]
                        PE.wait(act, i, f"z{n}.{j}")
                        C.done(act.copy(w.Z[:], w.b4(0)), f"cz{n}.{j}")
                for j in range(2):
                    w = lane[j]
                    PE.wait(act, i, f"ta.{j}")
                    C.done(act.copy(w.taT[:], w.bank[0][:, 0:2 * P].rearrange("p (a n) -> p a n", a=2)), f"ta.{j}")
                for j in range(2):
                    w = lane[j]
                    PE.wait(act, i, f"Y.{j}")
                    step.then(act.copy(by_parity(w.ys, 0), w.bank_pair(3)))
                    C.done(act.copy(by_parity(w.ys, 1), w.bank_pair(0)), f"y.{j}")
                for j in range(2):
                    w = lane[j]
                    V.wait(act, i, f"var.{j}")
                    step.then(act.activation(w.s4[:, 6, :], w.s4[:, 5, :], ACT.Ln, scale=1.0 / BD, bias=keep["eps"][:, 2:3]))
                    C.done(act.activation(w.s4[:, 7, :], w.s4[:, 6, :], ACT.Exp, scale=-0.5), f"rstd.{j}")
                for j in range(2):
                    V.wait(act, i, f"y.{j}")
                    act.dma_start(dr["ymix"][bass.ds((i * 2 + j) * P, P), AW:AW + BW], lane[j].yo[:]).then_inc(y_out[j], 16)
                step.restart()
            for j in range(2):
                act.wait_ge(y_out[j], 16 * TURNS)

        @block.vector
        def _(dve):
            step = Steps(dve, dve_step)
            tt = dve.tensor_tensor
            V.start(dve)
            dve.memset(zero[:], 0.0).then_inc(zero_done, 1)
            step.then(dve.memset(St[:], 0.0))
            step.then(dve.memset(one[:], 1.0))
            dve.wait_ge(consts_in, 16 * 15)
            step.restart()
            def both(op):
                for w in lane:
                    q = op(w)
                step.then(q)

            with dve.Fori(0, TURNS) as i:
                for j in range(2):
                    w = lane[j]
                    dve.wait_ge(mix, i * 4 + 2 * j + 2)
                    PE.wait_before(dve, i, f"state.{j}")
                    V.done(tt(w.p[:], w.prev[:], w.cur[:], ALU.add), f"mixed.{j}")
                    V.wait(dve, i, f"mixed.{j}")
                    PE.wait_before(dve, i, f"lr_T.{j}")
                    step.then(dve.tensor_scalar(w.lr[:, 0:64], w.p[:, 3 * BW:3 * BW + 64], 2.0, -80.0, ALU.mult, ALU.max))
                    step.then(dve.tensor_scalar(w.lr[:, 64:128], w.p[:, 3 * BW + 64:3 * BW + 128], 0.0, None, ALU.mult))
                    V.done(dve.tensor_scalar(w.lr[:, 128:256], w.p[:, 3 * BW + 128:], -80.0, None, ALU.max), f"lr_args.{j}")
                for j in range(2):
                    w = lane[j]
                    C.wait(dve, i, f"lr_sig.{j}")
                    step.then(dve.tensor_scalar(w.lr[:, 0:64], w.lr[:, 0:64], 2.0, -1.0, ALU.mult, ALU.add))
                    V.done(dve.tensor_copy(w.lr[:, 64:128], w.p[:, 3 * BW + 64:3 * BW + 128]), f"lr.{j}")
                for j in range(2):
                    w = lane[j]
                    PE.wait(dve, i, f"lora.{j}")
                    step.then(tt(w.wa[:, 0:BW], w.bank[1][:, 0:BW], wa0[:, 0:BW], ALU.add))
                    step.then(tt(w.wa[:, BW:], w.bank[2][:, 0:BW], wa0[:, BW:], ALU.add))
                    V.done(dve.tensor_scalar(w.wa[:], w.wa[:], -80.0, None, ALU.max), f"wa.{j}")
                for j in range(2):
                    w = lane[j]
                    C.wait(dve, i, f"wa_sig.{j}")
                    V.done(dve.tensor_scalar(w.lw[:], w.wa[:, 0:BW], -HALF, None, ALU.mult), f"logw.{j}")
                both(lambda w: tt(w.kk[:], w.p[:, BW:2 * BW], k_k[:], ALU.mult))
                both(lambda w: tt(w.tmp[:], w.kk[:], w.kk[:], ALU.mult))
                both(lambda w: dve.tensor_reduce(w.s4[:, 3, :], h3(w.tmp[:]), AX.X, ALU.add))
                for j in range(2):
                    w = lane[j]
                    V.done(dve.tensor_scalar(w.s4[:, 0, :], w.s4[:, 3, :], 1e-24, None, ALU.max), f"kk_ss.{j}")
                for j in range(2):
                    w = lane[j]
                    PE.wait(dve, i, f"cum.{j}")
                    V.done(tt(w.cx[:], w.bank[1][:, 0:BW], w.lw[:], ALU.subtract), f"cx.{j}")
                a_, r_, k_ = lambda w: w.wa[:, BW:], lambda w: w.p[:, 0:BW], lambda w: w.p[:, BW:2 * BW]
                both(lambda w: dve.scalar_tensor_tensor(w.k2[:], a_(w), -1.0, k_a[:], ALU.add, ALU.mult))
                both(lambda w: dve.scalar_tensor_tensor(w.k2[:], w.k2[:], 1.0, k_(w), ALU.add, ALU.mult))
                for j in range(2):
                    C.wait(dve, i, f"kk_rstd.{j}")
                both(lambda w: tt(h3(w.kk[:]), h3(w.kk[:]), bc(w.s4[:, 2, :]), ALU.mult))
                both(lambda w: tt(w.tmp[:], w.kk[:], a_(w), ALU.mult))
                for j in range(2):
                    w = lane[j]
                    C.wait(dve, i, f"decays.{j}")
                    dve.scalar_tensor_tensor(w.ops[:, 0, :], w.kk[:], -1.0, w.dec[:, 2, :], ALU.mult, ALU.mult)
                    tt(w.ops[:, 1, :], r_(w), w.dec[:, 0, :], ALU.mult)
                    tt(w.ops[:, 2, :], w.tmp[:], w.dec[:, 1, :], ALU.mult)
                    V.done(tt(w.ops[:, 3, :], w.k2[:], w.dec[:, 1, :], ALU.mult), f"operands.{j}")
                for j in range(2):
                    w = lane[j]
                    PE.wait(dve, i, f"grams.{j}")
                    dve.wait_ge(pool_done, i * 10 + 5 * j + 5)
                    for h in range(BH):
                        q = tt(w.gm[:, h, :, :], w.b4(h), mask4[:], ALU.mult)
                    V.done(q, f"masked.{j}")
                for j in range(2):
                    w = lane[j]
                    V.wait(dve, i, f"masked.{j}")
                    step.then(tt(w.DT[:], w.gm[:, :, 0, :], mb(2), ALU.mult))
                    step.then(tt(w.TT[:], w.DT[:], ib, ALU.add))
                    PE.wait(dve, i, f"A.{j}")
                    ho = lambda x, e: x.rearrange("p (a e) n -> p e a n", e=2)[:, e]
                    ml = masks[:, 0, :].unsqueeze(1).to_broadcast([P, 2, P])
                    for e in range(2):
                        step.then(tt(ho(w.A[:], e), w.bank[e][:, 0:2 * P].rearrange("p (a n) -> p a n", a=2), ml, ALU.mult))
                    step.then(tt(w.Dm[:], w.A[:], mb(1), ALU.mult))
                    V.done(tt(w.T[:], w.Dm[:], ib, ALU.add), f"D0.{j}")
                for n in range(4):
                    for j in range(2):
                        w = lane[j]
                        PE.wait(dve, i, f"sq{n}.{j}")
                        if n > 0:
                            step.then(tt(w.T[:], w.T[:], w.b4(1), ALU.add))
                            q = tt(w.TT[:], w.TT[:], w.b4(3), ALU.add)
                        if n < 3:
                            if n > 0:
                                step.then(q)
                            q = dve.tensor_copy(w.DT[:], w.b4(2))
                        V.done(q, f"v{n}.{j}")
                    if n == 0:
                        both(lambda w: tt(w.tmp[:], r_(w), w.k2[:], ALU.mult))
                        both(lambda w: tt(w.tmp[:], w.tmp[:], r_k[:], ALU.mult))
                        both(lambda w: dve.tensor_reduce(w.s4[:, 4, :], h3(w.tmp[:]), AX.X, ALU.add))
                for n in range(3):
                    for j in range(2):
                        w = lane[j]
                        PE.wait(dve, i, f"z{n}.{j}")
                        V.done(dve.tensor_copy(w.ZT[:], w.b4(2)), f"vz{n}.{j}")
                    for j in range(2):
                        w = lane[j]
                        PE.wait(dve, i, f"m{n}.{j}")
                        if n < 2:
                            step.then(tt(w.T[:], w.T[:], w.b4(1), ALU.add))
                        V.done(tt(w.TT[:], w.TT[:], w.b4(3), ALU.add), f"vm{n}.{j}")
                for j in range(2):
                    w = lane[j]
                    f = lambda n: w.fs[:].rearrange("p (a b) -> p b a", b=2)[:, n].unsqueeze(2).to_broadcast([P, 2, BD])
                    V.done(tt(w.Sc[:], St[:], f(0), ALU.mult), f"Sc.{j}")
                    PE.wait(dve, i, f"U.{j}")
                    step.then(dve.tensor_copy(by_parity(w.Us, 0), w.bank_pair(1)))
                    V.done(dve.tensor_copy(by_parity(w.Us, 1), w.bank_pair(2)), f"U.{j}")
                    PE.wait(dve, i, f"state.{j}")
                    step.then(tt(w.Sc[:], w.Sc[:], w.bank[1][:, 0:2 * BD].rearrange("p (a d) -> p a d", a=2), ALU.add))
                    V.done(tt(St[:], w.Sc[:], f(1), ALU.mult), f"state.{j}")
                    V.wait(dve, i, f"state.{j}")
                for j in range(2):
                    C.wait(dve, i, f"y.{j}")
                both(lambda w: dve.tensor_reduce(w.s4[:, 3, :], h3(w.ys[:]), AX.X, ALU.add))
                both(lambda w: dve.tensor_scalar(w.s4[:, 3, :], w.s4[:, 3, :], -1.0 / BD, None, ALU.mult))
                both(lambda w: tt(h3(w.ys[:]), h3(w.ys[:]), bc(w.s4[:, 3, :]), ALU.add))
                both(lambda w: tt(w.yq[:], w.ys[:], w.ys[:], ALU.mult))
                for j in range(2):
                    w = lane[j]
                    V.done(dve.tensor_reduce(w.s4[:, 5, :], h3(w.yq[:]), AX.X, ALU.add), f"var.{j}")
                both(lambda w: tt(h3(w.tmp[:]), h3(w.p[:, 2 * BW:3 * BW]), bc(w.s4[:, 4, :]), ALU.mult))
                for j in range(2):
                    C.wait(dve, i, f"rstd.{j}")
                both(lambda w: tt(h3(w.ys[:]), h3(w.ys[:]), bc(w.s4[:, 7, :]), ALU.mult))
                both(lambda w: tt(w.ys[:], w.ys[:], lnx_g[:], ALU.mult))
                both(lambda w: tt(w.ys[:], w.ys[:], lnx_b[:], ALU.add))
                both(lambda w: tt(w.ys[:], w.ys[:], w.tmp[:], ALU.add))
                for j in range(2):
                    w = lane[j]
                    dve.wait_ge(y_out[j], i * 16)
                    V.done(tt(w.yo[:], w.ys[:], w.g[:], ALU.mult), f"y.{j}")
                V.wait(dve, i, "y.1")
                step.restart()

        @block.tensor
        def _(pe):
            PE.start(pe)
            pe.sem_inc(pool_done, 10)
            pe.wait_ge(consts_in, 16 * 15)
            mm = pe.matmul
            with pe.Fori(0, TURNS) as i:
                for j in range(2):
                    w = lane[j]
                    V.wait(pe, i, f"lr.{j}")
                    for n in range(2):
                        q = pe.transpose(w.bank[0][:, n * P:(n + 1) * P], w.lr[:, n * P:(n + 1) * P], ident[:])
                    PE.done(q, f"lr_T.{j}")
                for j in range(2):
                    w = lane[j]
                    C.wait(pe, i, f"lrT.{j}")
                    mm(w.bank[1][:, 0:BW], w.lrT[0:64, 0:P], wa2[0:64, :], start=True, stop=True)
                    mm(w.bank[2][:, 0:BW], w.lrT[64:128, 0:P], wa2[64:128, :], start=True, stop=True)
                    PE.done(mm(w.bank[3][:, 0:BW], w.lrT[:, P:2 * P], g2[:], start=True, stop=True), f"lora.{j}")
                for j in range(2):
                    w = lane[j]
                    V.wait(pe, i, f"logw.{j}")
                    mm(w.bank[1][:, 0:BW], cum_m[:], w.lw[:], start=True, stop=True)
                    for a in range(2):
                        q = mm(w.bank[2][:, 2 * a:2 * a + 2], w.lw[:, a * P:(a + 1) * P], halves_m[:], start=True, stop=True)
                    PE.done(q, f"cum.{j}")
                for j in range(2):
                    w = lane[j]
                    V.wait(pe, i, f"operands.{j}")
                    C.wait(pe, i, f"g.{j}")
                    for a in range(2):
                        for x in range(2):
                            c = slice((2 * a + x) * P, (2 * a + x + 1) * P)
                            pe.transpose(w.bank[0][:, c], w.ops[:, x, a * P:(a + 1) * P], ident[:])
                            q = pe.transpose(w.bank[3][:, c], w.ops[:, 2 + x, a * P:(a + 1) * P], ident[:])
                    PE.done(q, f"operands_T.{j}")
                for j in range(2):
                    w = lane[j]
                    C.wait(pe, i, f"opsT.{j}")
                    for h in (0, 2, 1, 3):
                        r, a = half(h), h // 2
                        mm(w.bank[h][:, 0:2 * P], w.bkT[r, a, 0, :], w.arT[r, a, :, :], start=True, stop=True)
                        q = mm(w.bank[h][:, 2 * P:4 * P], w.bkT[r, a, 1, :], w.arT[r, a, :, :], start=True, stop=True)
                    PE.done(q, f"grams.{j}")
                for j in range(2):
                    w = lane[j]
                    V.wait(pe, i, f"masked.{j}")
                    for h in (0, 2, 1, 3):
                        r, a = half(h), h // 2
                        q = mm(w.bank[h % 2][:, a * P:(a + 1) * P], w.arT[r, a, 0, :], w.bkT[r, a, 0, :], start=True, stop=True)
                    PE.done(q, f"A.{j}")
                for j in range(2):
                    w = lane[j]
                    for h in range(BH):
                        q = mm(w.bank[3][:, hc(h)], w.gm[:, h, 2, :], w.p[:, 2 * BW + h * BD:2 * BW + (h + 1) * BD], start=True, stop=True)
                    PE.done(q, f"X.{j}")
                for n in range(4):
                    for j in range(2):
                        w = lane[j]
                        if n == 0:
                            V.wait(pe, i, f"D0.{j}")
                        else:
                            V.wait(pe, i, f"v{n - 1}.{j}")
                            C.wait(pe, i, f"c{n - 1}.{j}")
                        for h in range(BH):
                            c = slice(h * P, (h + 1) * P)
                            if n < 3:
                                mm(w.bank[0][:, c], w.DT[:, h, :], w.Dm[:, h, :], start=True, stop=True)
                                q = mm(w.bank[2][:, c], w.Dm[:, h, :], w.DT[:, h, :], start=True, stop=True)
                            if n > 0:
                                mm(w.bank[1][:, c], w.DT[:, h, :], w.T[:, h, :], start=True, stop=True)
                                q = mm(w.bank[3][:, c], w.Dm[:, h, :], w.TT[:, h, :], start=True, stop=True)
                        PE.done(q, f"sq{n}.{j}")
                for n in range(3):
                    for j in range(2):
                        w = lane[j]
                        if n == 0:
                            pe.wait_ge(pool_done, i * 10 + 5 * j + 15)
                            V.wait(pe, i, f"v3.{j}")
                        else:
                            V.wait(pe, i, f"vm{n - 1}.{j}")
                        for h in range(BH):
                            c = slice(h * P, (h + 1) * P)
                            if n < 2:
                                mm(w.bank[0][:, c], w.OT[n][:, h, :], w.T[:, h, :], start=True, stop=True)
                            q = mm(w.bank[2][:, c], w.O[n][:, h, :], w.TT[:, h, :], start=True, stop=True)
                        PE.done(q, f"z{n}.{j}")
                    for j in range(2):
                        w = lane[j]
                        V.wait(pe, i, f"vz{n}.{j}")
                        if n < 2:
                            C.wait(pe, i, f"cz{n}.{j}")
                        for h in range(BH):
                            c = slice(h * P, (h + 1) * P)
                            if n < 2:
                                mm(w.bank[1][:, c], w.TT[:, h, :], w.Z[:, h, :], start=True, stop=True)
                            q = mm(w.bank[3][:, c], w.T[:, h, :], w.ZT[:, h, :], start=True, stop=True)
                        PE.done(q, f"m{n}.{j}")
                for j in range(2):
                    w = lane[j]
                    V.wait(pe, i, f"vm2.{j}")
                    C.wait(pe, i, f"X.{j}")
                    for h in range(BH):
                        q = mm(w.bank[0][half(h), (h // 2) * P:(h // 2 + 1) * P], w.ops[:, 0, hc(h)], w.TT[:, h, :], start=True, stop=True)
                    PE.done(q, f"ta.{j}")
                for j in range(2):
                    w = lane[j]
                    v = lambda h: w.p[:, 2 * BW + h * BD:2 * BW + (h + 1) * BD]
                    C.wait(pe, i, f"ta.{j}")
                    V.wait(pe, i, f"Sc.{j}")
                    for h in range(BH):
                        o = w.bank[(1, 2)[h % 2]][:, hc(h // 2)]
                        mm(o, w.TT[:, h, :], w.Xs[:, hc(h)], start=True, stop=False)
                        q = mm(o, w.taT[half(h), h // 2, :], w.Sc[half(h), h // 2, :], start=False, stop=True)
                    PE.done(q, f"U.{j}")
                    V.wait(pe, i, f"U.{j}")
                    for h in range(BH):
                        o = w.bank[(3, 0)[h % 2]][:, hc(h // 2)]
                        mm(o, w.gm[:, h, 3, :], v(h), start=True, stop=False)
                        mm(o, w.gm[:, h, 1, :], w.Us[:, hc(h)], start=False, stop=False)
                        q = mm(o, w.arT[half(h), h // 2, 1, :], w.Sc[half(h), h // 2, :], start=False, stop=True)
                    PE.done(q, f"Y.{j}")
                    for h in range(BH):
                        o = w.bank[1][half(h), (h // 2) * BD:(h // 2 + 1) * BD]
                        mm(o, w.ops[:, 3, hc(h)], v(h), start=True, stop=False)
                        q = mm(o, w.ops[:, 2, hc(h)], w.Us[:, hc(h)], start=False, stop=True)
                    PE.done(q, f"state.{j}")


E, F, TOP_K, NG, TOPK_GROUPS = 64, 256, 8, 8, 4
EG = E // NG
FC = F // P
ROUTED_SCALE = 2.5
BLOCKS = E + (S * TOP_K - E) // P
NB = BLOCKS + 6
SLOTS = 4
DROP = -3.0e38


class RouteLane:

    def __init__(self, sb, bank, j):
        f = lambda n, *s: sb(f"{n}{j}", [P, *s])
        self.t0, self.t1, self.p0, self.p1 = bank[4 * j:4 * j + 4]
        self.ym, self.x, self.x2, self.h2, self.ysh = (f(n, D) for n in ("ymix_tile", "x_in", "x2_tile", "h2_tile", "y_shared"))
        self.yT, self.h2T = f("ymixT", KC, P), f("h2T", KC, P)
        self.sq = f("squares", D)
        self.st = f("norm_stats", 8)
        self.sc, self.bi, self.cand, self.left, self.sel, self.rw = (f(n, E) for n in (
            "scores", "biased", "candidates", "left", "selected", "route_w"))
        self.g8 = f("group_top", NG, 8)
        self.gs, self.gr, self.gq, self.gk = f("group_score", NG), f("group_rank", NG), f("group_cmp", NG, NG), f("group_eq", NG, NG)
        self.top, self.ws = f("top8", 8), f("weight_sum", 4)
        self.sg, self.acts, self.aT = f("sh_sig", F), f("sh_act", F), f("sh_actT", FC, P)


def norm_route(nc, io, dr, keep):
    TURNS = NT // 2
    with ExitStack() as ctx:
        sb = lambda n, s: ctx.enter_context(nc.sbuf_tensor(n, s, F32))
        sem = lambda n: ctx.enter_context(nc.semaphore(n))
        bank = [ctx.enter_context(nc.psum_tensor(f"rbank{n}", [P, BANK], F32)) for n in range(8)]
        ident, w_out = keep["ident"], keep["w_out"]
        w_r = sb("router_w", [P, KC, E])
        ws13, ws2 = sb("shared_w13", [P, 2, KC, F]), sb("shared_w2", [P, FC, D])
        post, scale, shift = sb("post_scale", [P, D]), sb("scale2", [P, D]), sb("shift2", [P, D])
        e_bias = sb("router_bias", [P, E])
        ones, strict, before = sb("ones", [P, P]), sb("strict", [P, P]), sb("group_before", [P, NG, NG])
        lane = [RouteLane(sb, bank, j) for j in range(2)]
        posm, W, seen = keep["posm"], keep["W"], keep["seen"]
        consts_in, weights_in, zero_done, zero_out, dve_step, act_step = (sem(n) for n in (
            "r_consts_in", "r_weights_in", "r_zero_done", "r_zero_out", "r_dve_step", "r_act_step"))
        ym_in, x_in, x2_out, h2_out, acc_out = ([sem(f"{n}{j}") for j in range(2)] for n in ("ymix_in", "r_x_in", "x2_out", "h2_out", "acc_out"))
        PE = Stages(sem("r_pe_done"), ["h2T.0", "route.0", "up.0", "h2T.1", "route.1", "aT.0", "up.1", "down.0", "aT.1", "down.1", "pos.0", "pos.1"])
        V = Stages(sem("r_dve_done"), in_lanes("ss xn x2 h2") + ["logit.0", "sh_arg.0", "sh_act.0", "logit.1", "aT.0", "sh_arg.1", "sh_act.1", "aT.1"]
                   + in_lanes("sel", "pos"))
        C = Stages(sem("r_act_done"), in_lanes("sq rstd rstd2 h2T", "score_exp sh_sig", "down"))
        PE_AHEAD = Stages(sem("r_pe_ahead"), in_lanes("yT", "proj"))
        C_AHEAD = Stages(sem("r_act_ahead"), in_lanes("yT"))
        k4 = lambda x: x.rearrange("p (k n) -> p k n", k=4)
        row = lambda n: dr["rows"][:, n * D:(n + 1) * D].partition_broadcast(P)
        kp = lambda x: x.rearrange("(k p) n -> p k n", p=P)
        rows = lambda i, j: bass.ds((i * 2 + j) * P, P)
        block = ctx.enter_context(nc.Block())

        @block.sync
        def _(sp):
            for j in range(2):
                sp.dma_start(lane[j].ym[:], dr["ymix"][rows(0, j), :]).then_inc(ym_in[j], 16)
            for dst, src in ((post[:], row(2)), (scale[:], row(4)), (shift[:], row(3)),
                             (e_bias[:], io["router_bias"][0:1, :].partition_broadcast(P)),
                             (ones[:], io["c_ones"]), (strict[:], io["c_strict"]), (before[:], io["c_before"])):
                sp.dma_start(dst, src).then_inc(consts_in, 16)
            for j in range(2):
                sp.dma_start(lane[j].x[:], io["x"][0][rows(0, j), :]).then_inc(x_in[j], 16)
            for dst, src in ((w_r[:], kp(io["router_w"][0])), (ws13[:, 0], kp(io["shared_w1"][0])),
                             (ws13[:, 1], kp(io["shared_w3"][0])), (ws2[:], kp(io["shared_w2"][0]))):
                sp.dma_start(dst, src).then_inc(weights_in, 16)
            sp.wait_ge(zero_done, 1)
            sp.dma_start(dr["h2"][S:S + P, :], lane[0].sq[:]).then_inc(zero_out, 16)
            sp.dma_start(dr["acc"][S:S + P, :], lane[0].sq[:]).then_inc(zero_out, 16)

            def turn(i, last):
                for j in range(2):
                    if not last:
                        PE_AHEAD.wait(sp, i, f"yT.{j}")
                        sp.dma_start(lane[j].ym[:], dr["ymix"][rows(i + 1, j), :]).then_inc(ym_in[j], 16)
                for j in range(2):
                    V.wait(sp, i, f"x2.{j}")
                    sp.dma_start(dr["x2"][rows(i, j), :], lane[j].x2[:]).then_inc(x2_out[j], 16)
                    if not last:
                        sp.dma_start(lane[j].x[:], io["x"][0][rows(i + 1, j), :]).then_inc(x_in[j], 16)
                    V.wait(sp, i, f"h2.{j}")
                    sp.dma_start(dr["h2"][rows(i, j), :], lane[j].h2[:]).then_inc(h2_out[j], 16)
                for j in range(2):
                    C.wait(sp, i, f"down.{j}")
                    sp.dma_start(dr["acc"][rows(i, j), :], lane[j].ysh[:]).then_inc(acc_out[j], 16)

            with sp.Fori(0, TURNS - 1) as i:
                turn(i, False)
            turn(TURNS - 1, True)
            for out in (*x2_out, *h2_out, *acc_out):
                sp.wait_ge(out, 16 * TURNS)
            sp.wait_ge(zero_out, 32)

        @block.scalar
        def _(act):
            load_exp_and_ln(nc, act)
            step = Steps(act, act_step)
            C.start(act)
            C_AHEAD.start(act)
            act.wait_ge(zero_out, 32)

            def project_copy(i, j):
                w = lane[j]
                PE_AHEAD.wait(act, i, f"yT.{j}")
                act.copy(w.yT[:, 0:4, :], k4(w.t0[:]))
                C_AHEAD.done(act.copy(w.yT[:, 4:8, :], k4(w.t1[:])), f"yT.{j}")

            def turn(i, last):
                for j in range(2):
                    w = lane[j]
                    PE_AHEAD.wait(act, i, f"proj.{j}")
                    act.activation(w.sq[:, 0:BANK], w.p0[:], ACT.Square, accum_out=w.st[:, 0:1])
                    C.done(act.activation(w.sq[:, BANK:], w.p1[:], ACT.Square, accum_out=w.st[:, 1:2]), f"sq.{j}")
                    V.wait(act, i, f"ss.{j}")
                    step.then(act.activation(w.st[:, 3:4], w.st[:, 2:3], ACT.Ln, scale=1.0 / D, bias=keep["eps"][:, 0:1]))
                    C.done(act.activation(w.st[:, 4:5], w.st[:, 3:4], ACT.Exp, scale=-0.5), f"rstd.{j}")
                    V.wait(act, i, f"x2.{j}")
                    step.then(act.activation(w.sq[:], w.x2[:], ACT.Square, accum_out=w.st[:, 5:6]))
                    step.then(act.activation(w.st[:, 6:7], w.st[:, 5:6], ACT.Ln, scale=1.0 / D, bias=keep["eps"][:, 0:1]))
                    C.done(act.activation(w.st[:, 7:8], w.st[:, 6:7], ACT.Exp, scale=-0.5), f"rstd2.{j}")
                    PE.wait(act, i, f"h2T.{j}")
                    act.copy(w.h2T[:, 0:4, :], k4(w.t0[:]))
                    C.done(act.copy(w.h2T[:, 4:8, :], k4(w.t1[:])), f"h2T.{j}")
                for j in range(2):
                    w = lane[j]
                    V.wait(act, i, f"logit.{j}")
                    C.done(act.activation(w.sc[:], w.sc[:], ACT.Exp, scale=-1.0), f"score_exp.{j}")
                    V.wait(act, i, f"sh_arg.{j}")
                    step.then(act.activation(w.sg[:], w.sg[:], ACT.Exp, scale=-1.0))
                    step.then(act.activation(w.sg[:], w.sg[:], ACT.Ln, bias=ones[:, 0:1]))
                    C.done(act.activation(w.sg[:], w.sg[:], ACT.Exp, scale=-1.0), f"sh_sig.{j}")
                for j in range(2):
                    w = lane[j]
                    PE.wait(act, i, f"down.{j}")
                    act.wait_ge(acc_out[j], i * 16)
                    act.copy(w.ysh[:, 0:BANK], w.t0[:])
                    C.done(act.copy(w.ysh[:, BANK:], w.t1[:]), f"down.{j}")
                    if not last:
                        project_copy(i + 1, j)

            for j in range(2):
                project_copy(0, j)
            with act.Fori(0, TURNS - 1) as i:
                turn(i, False)
                step.restart()
            turn(TURNS - 1, True)

        @block.vector
        def _(dve):
            step = Steps(dve, dve_step)
            tt, ts, stt = dve.tensor_tensor, dve.tensor_scalar, dve.scalar_tensor_tensor
            V.start(dve)
            dve.memset(lane[0].sq[:], 0.0).then_inc(zero_done, 1)
            step.then(dve.memset(seen[:], 0.0))
            dve.wait_ge(consts_in, 16 * 7)
            step.restart()

            def turn(i):
                for j in range(2):
                    w = lane[j]
                    C.wait(dve, i, f"sq.{j}")
                    V.done(tt(w.st[:, 2:3], w.st[:, 0:1], w.st[:, 1:2], ALU.add), f"ss.{j}")
                    C.wait(dve, i, f"rstd.{j}")
                    dve.wait_ge(x2_out[j], i * 16)
                    stt(w.x2[:, 0:BANK], w.p0[:], w.st[:, 4:5], post[:, 0:BANK], ALU.mult, ALU.mult)
                    V.done(stt(w.x2[:, BANK:], w.p1[:], w.st[:, 4:5], post[:, BANK:], ALU.mult, ALU.mult), f"xn.{j}")
                    V.wait(dve, i, f"xn.{j}")
                    dve.wait_ge(x_in[j], i * 16 + 16)
                    V.done(tt(w.x2[:], w.x2[:], w.x[:], ALU.add), f"x2.{j}")
                    C.wait(dve, i, f"rstd2.{j}")
                    dve.wait_ge(h2_out[j], i * 16)
                    step.then(stt(w.h2[:], w.x2[:], w.st[:, 7:8], scale[:], ALU.mult, ALU.mult))
                    V.done(tt(w.h2[:], w.h2[:], shift[:], ALU.add), f"h2.{j}")

                def router_arg(j):
                    PE.wait(dve, i, f"route.{j}")
                    V.done(ts(lane[j].sc[:], lane[j].p0[:, 0:E], -80.0, None, ALU.max), f"logit.{j}")

                def shared_act(j):
                    w = lane[j]
                    PE.wait(dve, i, f"up.{j}")
                    V.done(ts(w.sg[:], w.p1[:, 0:F], -80.0, None, ALU.max), f"sh_arg.{j}")
                    C.wait(dve, i, f"sh_sig.{j}")
                    step.then(tt(w.sg[:], w.sg[:], w.p1[:, 0:F], ALU.mult))
                    V.done(tt(w.acts[:], w.sg[:], w.p1[:, F:2 * F], ALU.mult), f"sh_act.{j}")

                def copy_act(j):
                    w = lane[j]
                    PE.wait(dve, i, f"aT.{j}")
                    V.done(dve.tensor_copy(w.aT[:], w.p0[:, F:2 * F].rearrange("p (k n) -> p k n", k=FC)), f"aT.{j}")

                router_arg(0)
                shared_act(0)
                router_arg(1)
                copy_act(0)
                shared_act(1)
                copy_act(1)
                def both(op):
                    for w in lane:
                        q = op(w)
                    step.then(q)

                for j in range(2):
                    C.wait(dve, i, f"score_exp.{j}")
                both(lambda w: ts(w.sc[:], w.sc[:], 1.0, None, ALU.add))
                both(lambda w: dve.reciprocal(w.sc[:], w.sc[:]))
                both(lambda w: tt(w.bi[:], w.sc[:], e_bias[:], ALU.add))
                for n in range(NG - 1):
                    for w in lane:
                        dve.max(w.g8[:, n, :], w.bi[:, n * EG:(n + 1) * EG])
                both(lambda w: dve.max(w.g8[:, NG - 1, :], w.bi[:, (NG - 1) * EG:NG * EG]))
                both(lambda w: tt(w.gs[:], w.g8[:, :, 0], w.g8[:, :, 1], ALU.add))
                mine = lambda w: w.gs[:].unsqueeze(2).to_broadcast([P, NG, NG])
                other = lambda w: w.gs[:].unsqueeze(1).to_broadcast([P, NG, NG])
                both(lambda w: tt(w.gk[:], other(w), mine(w), ALU.is_equal))
                both(lambda w: tt(w.gk[:], w.gk[:], before[:], ALU.mult))
                both(lambda w: tt(w.gq[:], other(w), mine(w), ALU.is_gt))
                both(lambda w: tt(w.gq[:], w.gq[:], w.gk[:], ALU.add))
                both(lambda w: dve.tensor_reduce(w.gr[:], w.gq[:], AX.X, ALU.add))
                both(lambda w: ts(w.gr[:], w.gr[:], TOPK_GROUPS - 0.5, None, ALU.is_lt))
                both(lambda w: ts(w.gs[:], w.gr[:], -NEG, NEG, ALU.mult, ALU.add))
                g3 = lambda x: x.rearrange("p (g e) -> p g e", g=NG)
                gb = lambda x: x.unsqueeze(2).to_broadcast([P, NG, EG])
                both(lambda w: tt(g3(w.cand[:]), g3(w.bi[:]), gb(w.gr[:]), ALU.mult))
                both(lambda w: tt(g3(w.cand[:]), g3(w.cand[:]), gb(w.gs[:]), ALU.add))
                both(lambda w: dve.max(w.top[:], w.cand[:]))
                both(lambda w: dve.match_replace(w.left[:], w.top[:], w.cand[:], DROP))
                for j in range(2):
                    V.done(ts(lane[j].sel[:], lane[j].left[:], DROP, None, ALU.is_equal), f"sel.{j}")
                V.wait(dve, i, "sel.1")
                both(lambda w: tt(w.rw[:], w.sc[:], w.sel[:], ALU.mult))
                both(lambda w: dve.tensor_reduce(w.ws[:, 0:1], w.rw[:], AX.X, ALU.add))
                both(lambda w: ts(w.ws[:, 1:2], w.ws[:, 0:1], 1e-20, None, ALU.add))
                both(lambda w: dve.reciprocal(w.ws[:, 2:3], w.ws[:, 1:2]))
                for j in range(2):
                    w = lane[j]
                    q = ts(W[:, bass.ds(i * 2 + j, 1), :].squeeze(1), w.rw[:], w.ws[:, 2:3], ROUTED_SCALE, ALU.mult, ALU.mult)
                step.then(q)
                for j in range(2):
                    w = lane[j]
                    PE.wait(dve, i, "pos.1")
                    step.then(tt(seen[:], seen[:], w.sel[:], ALU.add))
                    step.then(stt(w.left[:], w.t0[:, 0:E], 1.0, w.sel[:], ALU.add, ALU.mult))
                    V.done(ts(posm[:, bass.ds(i * 2 + j, 1), :].squeeze(1), w.left[:], -1.0, None, ALU.add), f"pos.{j}")
                V.wait(dve, i, "pos.1")

            with dve.Fori(0, TURNS) as i:
                turn(i)
                step.restart()

        @block.tensor
        def _(pe):
            PE.start(pe)
            PE_AHEAD.start(pe)
            mm = pe.matmul

            def transpose_y(i, j):
                w = lane[j]
                pe.wait_ge(ym_in[j], i * 16 + 16)
                for k in range(KC):
                    q = pe.transpose((w.t0, w.t1)[k // 4][:, (k % 4) * P:(k % 4 + 1) * P], w.ym[:, k * P:(k + 1) * P], ident[:])
                PE_AHEAD.done(q, f"yT.{j}")

            def project(i, j):
                w = lane[j]
                for n in range(2):
                    for k in range(KC):
                        q = mm((w.p0, w.p1)[n][:], w.yT[:, k, :], w_out[:, k, n * BANK:(n + 1) * BANK], start=(k == 0), stop=(k == KC - 1))
                PE_AHEAD.done(q, f"proj.{j}")

            def turn(i, last):
                def transpose_h(j):
                    w = lane[j]
                    V.wait(pe, i, f"h2.{j}")
                    for k in range(KC):
                        q = pe.transpose((w.t0, w.t1)[k // 4][:, (k % 4) * P:(k % 4 + 1) * P], w.h2[:, k * P:(k + 1) * P], ident[:])
                    PE.done(q, f"h2T.{j}")

                def route(j):
                    w = lane[j]
                    C.wait(pe, i, f"h2T.{j}")
                    for k in range(KC):
                        q = mm(w.p0[:, 0:E], w.h2T[:, k, :], w_r[:, k, :], start=(k == 0), stop=(k == KC - 1))
                    PE.done(q, f"route.{j}")

                def up(j):
                    w = lane[j]
                    for k in range(KC):
                        q = mm(w.p1[:].rearrange("p (a n) -> p a n", a=2), w.h2T[:, k, :], ws13[:, :, k, :], start=(k == 0), stop=(k == KC - 1))
                    PE.done(q, f"up.{j}")

                def transpose_act(j):
                    w = lane[j]
                    V.wait(pe, i, f"sh_act.{j}")
                    for k in range(FC):
                        q = pe.transpose(w.p0[:, F + k * P:F + (k + 1) * P], w.acts[:, k * P:(k + 1) * P], ident[:])
                    PE.done(q, f"aT.{j}")

                def down(j):
                    w = lane[j]
                    V.wait(pe, i, f"aT.{j}")
                    for n in range(2):
                        for k in range(FC):
                            q = mm((w.t0, w.t1)[n][:], w.aT[:, k, :], ws2[:, k, n * BANK:(n + 1) * BANK], start=(k == 0), stop=(k == FC - 1))
                    PE.done(q, f"down.{j}")

                def places():
                    for j in range(2):
                        w = lane[j]
                        V.wait(pe, i, f"sel.{j}")
                        mm(w.t0[:, 0:E], ones[:], seen[:], start=True, stop=False)
                        if j == 1:
                            mm(w.t0[:, 0:E], ones[:], lane[0].sel[:], start=False, stop=False)
                        PE.done(mm(w.t0[:, 0:E], strict[:], w.sel[:], start=False, stop=True), f"pos.{j}")

                transpose_h(0)
                route(0)
                up(0)
                transpose_h(1)
                route(1)
                transpose_act(0)
                up(1)
                down(0)
                transpose_act(1)
                C.wait(pe, i, "down.0")
                if not last:
                    transpose_y(i + 1, 0)
                down(1)
                C.wait(pe, i, "down.1")
                if not last:
                    transpose_y(i + 1, 1)
                    for j in range(2):
                        C_AHEAD.wait(pe, i + 1, f"yT.{j}")
                    project(i + 1, 0)
                places()
                if not last:
                    project(i + 1, 1)

            for j in range(2):
                transpose_y(0, j)
            for j in range(2):
                C_AHEAD.wait(pe, 0, f"yT.{j}")
                project(0, j)
            pe.wait_ge(consts_in, 16 * 7)
            pe.wait_ge(weights_in, 16 * 4)
            with pe.Fori(0, TURNS - 1) as i:
                turn(i, False)
            turn(TURNS - 1, True)


def schedule(nc, io, dr, keep):
    with ExitStack() as ctx:
        sb = lambda n, s: ctx.enter_context(nc.sbuf_tensor(n, s, F32))
        sem = lambda n: ctx.enter_context(nc.semaphore(n))
        ps_a, ps_b = (ctx.enter_context(nc.psum_tensor(n, [P, BANK], F32)) for n in ("sched_a", "sched_b"))
        ones, upper, thr, iota_b, slot_step = sb("s_ones", [P, P]), sb("s_upper", [P, P]), sb("thresholds", [E, 8]), sb("iota_b", [P, NB]), sb("slot_step", [E, P])
        cnt, more, nblk, end, ind, nbc = sb("counts", [E, 1]), sb("more", [E, 8]), sb("n_blocks", [E, 1]), sb("end", [E, 1]), sb("ended", [E, NB]), sb("nbc", [E, P])
        over, first = sb("over", [P, NB]), sb("first", [P, NB])
        tab, base = keep["tab"], keep["base"]
        consts_in, dve_done, pe_done = sem("s_consts_in"), sem("s_dve_done"), sem("s_pe_done")
        block = ctx.enter_context(nc.Block())

        @block.sync
        def _(sp):
            for dst, src in ((ones[:], io["c_ones"]), (upper[:], io["c_upper"]), (thr[:], io["c_thresholds"]),
                             (iota_b[:], io["c_iota_b"].partition_broadcast(P)), (slot_step[:], io["c_slot_step"])):
                sp.dma_start(dst, src).then_inc(consts_in, 16)
            sp.wait_ge(consts_in, 80)

        @block.vector
        def _(dve):
            step = Steps(dve, dve_done)
            dve.wait_ge(consts_in, 80)
            dve.wait_ge(pe_done, 1)
            step.then(dve.tensor_copy(cnt[:], ps_a[0:E, 0:1]))
            step.then(dve.tensor_scalar(more[:], thr[:], cnt[:], None, ALU.is_lt))
            step.then(dve.tensor_reduce(nblk[:], more[:], AX.X, ALU.add))
            step.then(dve.tensor_copy(nbc[:], nblk[:].to_broadcast([E, P])))
            dve.wait_ge(pe_done, 2)
            step.then(dve.tensor_copy(end[:], ps_b[0:E, 0:1]))
            step.then(dve.tensor_scalar(ind[:], iota_b[0:E, :], end[:], None, ALU.is_ge))
            dve.wait_ge(pe_done, 3)
            e_raw, start, slot = (ps_a[:, n * NB:(n + 1) * NB] for n in range(3))
            step.then(dve.tensor_scalar(over[:], e_raw, E - 0.5, 4096.0, ALU.is_gt, ALU.mult))
            step.then(dve.tensor_tensor(first[:], iota_b[:], start, ALU.subtract))
            step.then(dve.scalar_tensor_tensor(base[:], first[:], float(P), over[:], ALU.mult, ALU.add))
            step.then(dve.tensor_scalar(tab[0:1, 0, :], e_raw[0:1, :], E - 1.0, None, ALU.min))
            step.then(dve.tensor_copy(tab[0:1, 1, :], slot[0:1, :]))
            step.then(dve.tensor_copy(tab[0:1, 2, 0:E], ps_b[0:1, E:2 * E]))

        @block.tensor
        def _(pe):
            mm = pe.matmul
            pe.wait_ge(consts_in, 80)
            mm(ps_a[0:E, 0:1], keep["seen"][:], ones[:, 0:1], start=True, stop=True).then_inc(pe_done, 1)
            pe.wait_ge(dve_done, 4)
            mm(ps_b[0:E, 0:1], upper[0:E, 0:E], nblk[:], start=True, stop=True).then_inc(pe_done, 1)
            pe.wait_ge(dve_done, 6)
            mm(ps_b[:, E:2 * E], nbc[:], upper[0:E, 0:E], start=True, stop=True)
            mm(ps_a[:, 0:NB], ones[0:E, :], ind[:], start=True, stop=True)
            mm(ps_a[:, NB:2 * NB], nbc[:], ind[:], start=True, stop=True)
            mm(ps_a[:, 2 * NB:3 * NB], slot_step[:], ind[:], start=True, stop=True).then_inc(pe_done, 1)


def experts(nc, io, dr, keep):
    I32 = mybir.dt.int32
    with ExitStack() as ctx:
        sb = lambda n, s, dt=F32: ctx.enter_context(nc.sbuf_tensor(n, s, dt))
        sem = lambda n: ctx.enter_context(nc.semaphore(n))
        pt = lambda n: ctx.enter_context(nc.psum_tensor(n, [P, BANK], F32))
        ident, posm, W, tab, base = keep["ident"], keep["posm"], keep["W"], keep["tab"], keep["base"]
        w13, w2 = sb("w13", [P, SLOTS, 2, KC, F]), sb("w2", [P, SLOTS, FC, D])
        w13_s = [[sb(f"w13_{n}{j}", [P, 2, KC, F], F32R) for n in ("high", "low")] for j in range(2)]
        iota, vals, empty = sb("iota_p", [P, P]), sb("id_and_weight", [P, NT, 4], F32R), sb("empty_row", [P, 1])
        ids, W_high, W_low = sb("ids", [P, NT, 1]), sb("W_high", [P, NT, E], F32R), sb("W_low", [P, NT, E], F32R)
        pcol, onehot = sb("place", [P, NT]), sb("onehot_p", [P, NT, P], F32R)
        nid, isn = sb("list_id", [P, 4]), sb("is_empty", [P, 2])
        wslot = [sb(f"slot_w{j}", [P, 1]) for j in range(4)]
        idx = [sb(f"idx{j}", [P, 1], I32) for j in range(4)]
        sidx = [sb(f"scatter_idx{j}", [P, 1], I32) for j in range(2)]
        xg = [sb(f"gathered{j}", [P, D]) for j in range(2)]
        y = [sb(f"y_rows{j}", [P, D]) for j in range(2)]
        sg, acts, aT = sb("silu_g", [P, F]), sb("act", [P, F]), sb("actT", [P, FC, P])
        xT = [sb(f"xT_{n}", [P, KC, P], F32R) for n in ("high", "low")]
        PASSES = ((0, 0), (0, 1), (1, 0))
        PIECES = [(which, slice(half * KC // 2, (half + 1) * KC // 2)) for which in range(2) for half in range(2)]
        ps_x, ps_y = [pt(f"ps_x{n}") for n in range(2)], [pt(f"ps_y{n}") for n in range(2)]
        ps_h, ps_a, ps_l = pt("ps_h"), pt("ps_a"), pt("ps_l")
        held = sem("held")
        consts_in, w_ready, dve_step = sem("e_consts_in"), sem("w_ready"), sem("e_dve_step")
        w_high, w_low, x_low = sem("w_high"), sem("w_low"), sem("x_low")
        piece_in = [sem(f"piece_in{n}") for n in range(3)]
        xg_in = [sem(f"xg_in{n}") for n in range(2)]
        onehot_ready, list_mm, idx_ready, x_mm, x_copied, up_mm, silu_done, act_ready, at_mm, aT_ready, dn_mm, y_ready, y_out, y_free = (
            sem(n) for n in ("onehot_ready", "list_mm", "idx_ready", "x_mm", "x_copied", "up_mm", "silu_done", "act_ready",
                             "at_mm", "aT_ready", "dn_mm", "y_ready", "e_y_out", "e_y_free"))
        views = [io[n][0].rearrange("e (p k) f -> e p k f", p=P) for n in ("exp_w1", "exp_w3")]
        view2 = io["exp_w2"][0].rearrange("e (p k) d -> e p k d", p=P)
        TURNS = (BLOCKS + 3) // 4
        block = ctx.enter_context(nc.Block())

        def n_blocks(eng):
            return eng.value_load(tab[0:1, 2, E - 1:E], min_val=E, max_val=BLOCKS)

        def entry(eng, which, n, hi):
            return eng.value_load(tab[0:1, which, bass.ds(n, 1)], min_val=0, max_val=hi)

        @block.sync
        def _(sp):
            for dst, src in ((iota[:], io["c_iota_p"].partition_broadcast(P)), (ids[:], io["c_ids"]), (empty[:], io["c_empty"])):
                sp.dma_start(dst, src, allow_slow_non_contiguous=True).then_inc(consts_in, 16)

            def load(e, s, turn, after=None):
                if s or after is not None:
                    for n in range(3):
                        sp.wait_ge(piece_in[n], turn * (SLOTS * 32) + s * 32)
                    sp.sem_inc(w_ready, 1)
                if after is not None:
                    sp.wait_ge(dn_mm, sp.value_load(tab[0:1, 2, bass.ds(after, 1)], min_val=1, max_val=BLOCKS) + 1)
                for n in range(6):
                    if n >= 3:
                        sp.wait_ge(piece_in[n % 3], turn * (SLOTS * 32) + s * 32 + 16)
                    which, half = n // 2, n % 2
                    if which < 2:
                        k = slice(half * KC // 2, (half + 1) * KC // 2)
                        sp.dma_start(w13[:, s, which, k], views[which][bass.ds(e, 1)].squeeze(0)[:, k, :]).then_inc(piece_in[n % 3], 16)
                    else:
                        sp.dma_start(w2[:, s, half], view2[bass.ds(e, 1)].squeeze(0)[:, half, :]).then_inc(piece_in[n % 3], 16)

            for s in range(SLOTS):
                load(s, s, 0)
            with sp.Fori(1, E // SLOTS) as i:
                for s in range(SLOTS):
                    load(i * SLOTS + s, s, i, i * SLOTS + s - SLOTS)
            for n in range(3):
                sp.wait_ge(piece_in[n], E * 32)
            sp.sem_inc(w_ready, 1)

        @block.gpsimd
        def _(pool):
            nb = n_blocks(pool)
            pool.sem_inc(y_free, 2)

            def gather(n, j):
                par = j % 2
                pool.wait_ge(idx_ready, n + 1)
                pool.sem_inc(held, 1)
                pool.indirect_dma_start(xg[par][:], None, dr["h2"], bass.IndirectOffsetOnAxis(ap=idx[j][:], axis=0)).then_inc(xg_in[par], 16)

            for n in range(3):
                if n == 2:
                    pool.wait_ge(x_mm, 1)
                gather(n, n)
            with pool.Fori(0, TURNS) as i:
                with pool.If(nb > i * 4):
                    for j in range(4):
                        b = i * 4 + j
                        pool.wait_ge(x_mm, b + 2)
                        gather(b + 3, (j + 3) % 4)
                        pool.wait_ge(y_ready, b + 2)
                        pool.sem_inc(held, 1)
                        pool.indirect_dma_start(dr["acc"], bass.IndirectOffsetOnAxis(ap=sidx[j % 2][:], axis=0), y[j % 2][:], None,
                                                compute_op=ALU.add).then_inc(y_out, 16)
                        pool.wait_ge(y_out, b * 16 + 16)
                        pool.sem_inc(y_free, 1)

        @block.scalar
        def _(act):
            nb = n_blocks(act)
            act.sem_inc(y_ready, 1)

            def x_copy(n):
                act.wait_ge(x_mm, n + 1)
                act.copy(xT[0][:, 0:4, :], ps_x[0][:].rearrange("p (k n) -> p k n", k=4))
                act.copy(xT[0][:, 4:8, :], ps_x[1][:].rearrange("p (k n) -> p k n", k=4)).then_inc(x_copied, 1)

            def split(n, par):
                e, w = entry(act, 0, n, E - 1), entry(act, 1, n, SLOTS - 1)
                act.wait_ge(w_ready, e + 1)
                for which, k in PIECES:
                    act.copy(w13_s[par][0][:, which, k], w13[:, bass.ds(w, 1), which, k].squeeze(1)).then_inc(w_high, 1)

            def silu(n):
                act.wait_ge(up_mm, n + 1)
                act.activation(sg[:], ps_h[:, 0:F], ACT.Silu).then_inc(silu_done, 1)

            split(0, 0)
            x_copy(0)
            split(1, 1)
            silu(0)
            x_copy(1)
            with act.Fori(0, TURNS) as i:
                with act.If(nb > i * 4):
                    for j in range(4):
                        b = i * 4 + j
                        split(b + 2, j % 2)
                        act.wait_ge(act_ready, b + 1)
                        silu(b + 1)
                        x_copy(b + 2)
                        act.wait_ge(y_free, b + 1)
                        act.wait_ge(dn_mm, b + 2)
                        act.copy(y[j % 2][:, 0:BANK], ps_y[0][:])
                        act.copy(y[j % 2][:, BANK:], ps_y[1][:]).then_inc(y_ready, 1)

        @block.vector
        def _(dve):
            step = Steps(dve, dve_step)
            nb = n_blocks(dve)
            dve.wait_ge(consts_in, 48)

            def make_onehot(n, e):
                step.then(dve.tensor_scalar(pcol[:], posm[:, :, bass.ds(e, 1)].squeeze(2), base[:, bass.ds(n, 1)], None, ALU.subtract))
                step.then(dve.tensor_copy(vals[:, :, 1:2], W_high[:, :, bass.ds(e, 1)]))
                step.then(dve.tensor_copy(vals[:, :, 2:3], W_low[:, :, bass.ds(e, 1)]))
                dve.tensor_tensor(onehot[:], iota[:].unsqueeze(1).to_broadcast([P, NT, P]),
                                  pcol[:].unsqueeze(2).to_broadcast([P, NT, P]), ALU.is_equal).then_inc(onehot_ready, 1)

            def expert_of(n):
                return entry(dve, 0, n, E - 1)

            def split_rest(n, par):
                w = entry(dve, 1, n, SLOTS - 1)
                for m, (which, k) in enumerate(PIECES):
                    dve.wait_ge(w_high, n * 4 + m + 1)
                    dve.tensor_tensor(w13_s[par][1][:, which, k], w13[:, bass.ds(w, 1), which, k].squeeze(1),
                                      w13_s[par][0][:, which, k], ALU.subtract).then_inc(w_low, 1)

            def x_rest(n):
                dve.wait_ge(x_copied, n + 1)
                dve.tensor_tensor(xT[1][:, 0:4, :], ps_x[0][:].rearrange("p (k n) -> p k n", k=4), xT[0][:, 0:4, :], ALU.subtract)
                dve.tensor_tensor(xT[1][:, 4:8, :], ps_x[1][:].rearrange("p (k n) -> p k n", k=4), xT[0][:, 4:8, :], ALU.subtract).then_inc(x_low, 1)

            def make_index(n, par):
                dve.wait_ge(list_mm, n + 1)
                step.then(dve.tensor_copy(nid[:, 0:3], ps_l[:, 0:3]))
                step.then(dve.tensor_scalar(isn[:, 0:1], nid[:, 0:1], 0.0, None, ALU.is_equal))
                step.then(dve.tensor_tensor(wslot[par][:], nid[:, 1:2], nid[:, 2:3], ALU.add))
                step.then(dve.tensor_tensor(isn[:, 1:2], isn[:, 0:1], empty[:], ALU.mult))
                dve.scalar_tensor_tensor(idx[par][:], nid[:, 0:1], -1.0, isn[:, 1:2], ALU.add, ALU.add).then_inc(idx_ready, 1)

            def activate(n, par):
                dve.wait_ge(silu_done, n + 1)
                dve.scalar_tensor_tensor(acts[:], sg[:], wslot[par][:], ps_h[:, F:2 * F], ALU.mult, ALU.mult).then_inc(act_ready, 1)

            step.then(dve.tensor_copy(W_high[:], W[:]))
            step.then(dve.tensor_tensor(W_low[:], W[:], W_high[:], ALU.subtract))
            step.then(dve.tensor_copy(vals[:, :, 0:1], ids[:]))
            step.then(dve.tensor_copy(vals[:, :, 3:4], ids[:]))
            for n in range(3):
                make_onehot(n, expert_of(n))
                make_index(n, n)
            make_onehot(3, expert_of(3))
            split_rest(0, 0)
            x_rest(0)
            split_rest(1, 1)
            activate(0, 0)
            x_rest(1)
            step.restart()
            with dve.Fori(0, TURNS) as i:
                with dve.If(nb > i * 4):
                    for j in range(4):
                        b = i * 4 + j
                        dve.wait_ge(at_mm, b + 1)
                        dve.wait_ge(dn_mm, b + 1)
                        dve.tensor_copy(aT[:], ps_a[:, 0:F].rearrange("p (k n) -> p k n", k=FC)).then_inc(aT_ready, 1)
                        dve.wait_ge(y_free, b + 1)
                        dve.wait_ge(idx_ready, b + 1)
                        step.then(dve.tensor_copy(sidx[j % 2][:], idx[j][:]))
                        split_rest(b + 2, j % 2)
                        activate(b + 1, (j + 1) % 4)
                        dve.wait_ge(x_mm, b + 1)
                        make_index(b + 3, (j + 3) % 4)
                        x_rest(b + 2)
                        make_onehot(b + 4, expert_of(b + 4))
                    step.restart()

        @block.tensor
        def _(pe):
            nb = n_blocks(pe)
            pe.sem_inc(dn_mm, 1)

            def list_of(n):
                pe.wait_ge(onehot_ready, n + 1)
                for k in range(NT):
                    q = pe.matmul(ps_l[:, 0:4], onehot[:, k, :], vals[:, k, :], start=(k == 0), stop=(k == NT - 1))
                q.then_inc(list_mm, 1)

            def x_transpose(n, par, turn):
                pe.wait_ge(xg_in[par], turn * 16 + 16)
                for k in range(KC):
                    q = pe.transpose(ps_x[k // 4][:, (k % 4) * P:(k % 4 + 1) * P], xg[par][:].rearrange("p (c k) -> p k c", k=KC)[:, k, :], ident[:])
                q.then_inc(x_mm, 1)

            def up(n, par):
                pe.wait_ge(w_low, n * 4 + 4)
                pe.wait_ge(x_low, n + 1)
                for k in range(KC):
                    for m, (a, z) in enumerate(PASSES):
                        q = pe.matmul(ps_h[:].rearrange("p (a n) -> p a n", a=2), xT[a][:, k, :], w13_s[par][z][:, :, k, :],
                                      start=(k == 0 and m == 0), stop=(k == KC - 1 and m == 2))
                q.then_inc(up_mm, 1)

            for n in range(3):
                if n:
                    pe.wait_ge(idx_ready, n)
                list_of(n)
            x_transpose(0, 0, 0)
            up(0, 0)
            x_transpose(1, 1, 0)
            with pe.Fori(0, TURNS) as i:
                with pe.If(nb > i * 4):
                    for j in range(4):
                        b = i * 4 + j
                        pe.wait_ge(act_ready, b + 1)
                        for k in range(FC):
                            q = pe.transpose(ps_a[:, k * P:(k + 1) * P], acts[:].rearrange("p (c k) -> p k c", k=FC)[:, k, :], ident[:])
                        q.then_inc(at_mm, 1)
                        up(b + 1, (j + 1) % 2)
                        pe.wait_ge(idx_ready, b + 3)
                        list_of(b + 3)
                        x_transpose(b + 2, j % 2, i * 2 + 1 + j // 2)
                        w = entry(pe, 1, b, SLOTS - 1)
                        pe.wait_ge(aT_ready, b + 1)
                        pe.wait_ge(y_ready, b + 1)
                        for n in range(2):
                            for k in range(FC):
                                q = pe.matmul(ps_y[n][:], aT[:, k, :], w2[:, bass.ds(w, 1), k, n * BANK:(n + 1) * BANK].squeeze(1),
                                              start=(k == 0), stop=(k == FC - 1))
                        q.then_inc(dn_mm, 1)


def finish(nc, io, dr, keep, out):
    with ExitStack() as ctx:
        sb = lambda n, s: ctx.enter_context(nc.sbuf_tensor(n, s, F32))
        sem = lambda n: ctx.enter_context(nc.semaphore(n))
        AHEAD = 4
        post = sb("post2", [P, D])
        a, x2, junk = ([sb(f"{n}{j}", [P, D]) for j in range(AHEAD)] for n in ("acc_tile", "x2_in", "sq2"))
        st = [sb(f"f_stats{j}", [P, 3]) for j in range(AHEAD)]
        post_in, dve_step, act_step = sem("post_in"), sem("f_dve_step"), sem("f_act_step")
        tile_in, outs = ([sem(f"{n}{j}") for j in range(AHEAD)] for n in ("tile_in", "f_out"))
        rstd, sums = sem("f_rstd"), sem("f_sums")
        block = ctx.enter_context(nc.Block())

        @block.sync
        def _(sp):
            sp.dma_start(post[:], dr["rows"][:, 5 * D:6 * D].partition_broadcast(P)).then_inc(post_in, 16)
            with sp.Fori(0, NT // AHEAD) as i:
                for j in range(AHEAD):
                    rows = bass.ds((i * AHEAD + j) * P, P)
                    sp.wait_ge(outs[j], i * 16)
                    sp.dma_start(a[j][:], dr["acc"][rows, :]).then_inc(tile_in[j], 16)
                    sp.dma_start(x2[j][:], dr["x2"][rows, :]).then_inc(tile_in[j], 16)

        @block.scalar
        def _(act):
            load_exp_and_ln(nc, act)
            step = Steps(act, act_step)

            def store(t, j):
                act.wait_ge(sums, t + 1)
                act.dma_start(out[0][bass.ds(t * P, P), :], x2[j][:]).then_inc(outs[j], 16)

            with act.Fori(0, NT // AHEAD) as i:
                for j in range(AHEAD):
                    act.wait_ge(tile_in[j], i * 32 + 32)
                    step.then(act.activation(junk[j][:], a[j][:], ACT.Square, accum_out=st[j][:, 0:1]))
                    step.then(act.activation(st[j][:, 1:2], st[j][:, 0:1], ACT.Ln, scale=1.0 / D, bias=keep["eps"][:, 0:1]))
                    act.activation(st[j][:, 2:3], st[j][:, 1:2], ACT.Exp, scale=-0.5).then_inc(rstd, 1)
                    if j:
                        store(i * AHEAD + j - 1, j - 1)
                store(i * AHEAD + AHEAD - 1, AHEAD - 1)
                step.restart()
            for j in range(AHEAD):
                act.wait_ge(outs[j], NT // AHEAD * 16)

        @block.vector
        def _(dve):
            step = Steps(dve, dve_step)
            dve.wait_ge(post_in, 16)
            with dve.Fori(0, NT // AHEAD) as i:
                for j in range(AHEAD):
                    dve.wait_ge(rstd, i * AHEAD + j + 1)
                    step.then(dve.scalar_tensor_tensor(a[j][:], a[j][:], st[j][:, 2:3], post[:], ALU.mult, ALU.mult))
                    step.then(dve.tensor_tensor(x2[j][:], x2[j][:], a[j][:], ALU.add))
                    dve.sem_inc(sums, 1)
                step.restart()


def t5_buckets(n):
    exact = N_BUCKETS // 2
    nf = np.maximum(n, 1).astype(np.float32)
    large = exact + (np.log(nf / exact) / math.log(MAX_DISTANCE / exact) * (N_BUCKETS - exact)).astype(np.int32)
    return np.where(n < exact, n, np.minimum(large, N_BUCKETS - 1))


def constants():
    s, t = np.arange(P)[:, None], np.arange(P)[None, :]
    f = lambda x: np.ascontiguousarray(x, dtype=np.float32)
    dist = 2 * P - 1 - np.arange(3 * P)
    onehot = np.zeros((N_BUCKETS + 1, 3 * P), np.float32)
    onehot[np.where(dist >= 0, t5_buckets(np.maximum(dist, 0)), N_BUCKETS), np.arange(3 * P)] = 1
    lower, upper = s > t, s < t
    blocks = [s // b == t // b for b in (16, 32, 64, 128)]
    masks = [lower, lower & blocks[0], upper & blocks[0]]
    for n in range(3):
        masks += [lower & blocks[n + 1] & ~blocks[n], upper & blocks[n + 1] & ~blocks[n]]
    mid = P // 2 - 1
    return {
        "c_ident": f(s == t),
        "c_upper": f(s <= t),
        "c_onehot": onehot,
        "c_mask4": f(np.stack([upper, s <= t, upper, s <= t], 1)),
        "c_masks": f(np.stack(masks, 1)),
        "c_cum": f((s <= t).astype(int) - (s <= mid).astype(int)),
        "c_ones": f(np.ones((P, P))),
        "c_strict": f(upper),
        "c_before": f(np.broadcast_to(np.tril(np.ones((NG, NG)), -1), (P, NG, NG))),
        "c_thresholds": f(np.broadcast_to([-1] + [P * n for n in range(1, S // P)], (E, 8))),
        "c_iota_b": f(np.arange(NB)[None, :]),
        "c_slot_step": f(np.broadcast_to([[(e + 1) % SLOTS - e % SLOTS] for e in range(E)], (E, P))),
        "c_iota_p": f(np.arange(P)[None, :]),
        "c_ids": f((np.arange(NT)[None, :] * P + np.arange(P)[:, None] + 1)[:, :, None]),
        "c_empty": f(S + 1 + np.arange(P)[:, None]),
        "c_halves": f(np.concatenate([s <= mid, s > mid], 1)),
    }


def build(nc, io, out, dr):
    with ExitStack() as ctx:
        sb = lambda n, s: ctx.enter_context(nc.sbuf_tensor(n, s, F32))
        keep = {"ident": sb("ident", [P, P]), "upper": sb("upper", [P, P]), "eps": sb("eps", [P, 4])}
        consts_in = ctx.enter_context(nc.semaphore("masks_in"))
        eps_done = ctx.enter_context(nc.semaphore("eps_done"))
        with nc.Block() as block:
            @block.sync
            def _(sp):
                sp.dma_start(keep["ident"][:], io["c_ident"]).then_inc(consts_in, 16)
                sp.dma_start(keep["upper"][:], io["c_upper"]).then_inc(consts_in, 16)
                sp.wait_ge(consts_in, 32)

            @block.vector
            def _(dve):
                dve.memset(keep["eps"][:, 0:1], RMS_EPS)
                dve.memset(keep["eps"][:, 1:2], LN_EPS)
                dve.memset(keep["eps"][:, 2:3], 64e-5).then_inc(eps_done, 1)
                dve.wait_ge(eps_done, 1)
        with ExitStack() as qkv:
            for n, s in (("qT", [P, AH, S]), ("kT", [P, AH, S]), ("v", [P, NT, AW])):
                keep[n] = qkv.enter_context(nc.sbuf_tensor(n, s, F32))
            keep["w_loaded"] = ctx.enter_context(nc.semaphore("w_loaded"))
            with nc.sbuf_tensor("w_in", [P, KC, 3072], F32) as keep["w_in"]:
                make_rows(nc, io, dr, keep)
                project(nc, io, dr, keep)
            attend(nc, io, dr, keep)
        for n, s in (("posm", [P, NT, E]), ("W", [P, NT, E]), ("seen", [P, E]), ("base", [P, NB])):
            keep[n] = sb(n, s)
        keep["tab"] = ctx.enter_context(nc.sbuf_tensor("tab", [1, 3, NB], mybir.dt.int32))
        with nc.sbuf_tensor("w_out", [P, KC, D], F32) as keep["w_out"]:
            rwkv(nc, io, dr, keep)
            norm_route(nc, io, dr, keep)
        schedule(nc, io, dr, keep)
        experts(nc, io, dr, keep)
        finish(nc, io, dr, keep, out)


DUMP = ["rows", "pb", "ymix", "x2", "h2", "acc", "out_x"]
_INS = ['x', 'c', 'w_ada', 'b_ada', 'norm_pre_mix', 'norm_post_mix', 'norm_pre_ffn', 'norm_post_ffn',
        'w_in', 'w_out', 'rel_bias_table', 'diff_lambda', 'diff_subln', 'rwkv_mu', 'rwkv_w0', 'rwkv_w2', 'rwkv_a0', 'rwkv_a2',
        'rwkv_g2', 'rwkv_k_k', 'rwkv_k_a', 'rwkv_r_k', 'rwkv_lnx_g', 'rwkv_lnx_b', 'gmlp_ln_g', 'gmlp_ln_b', 'gmlp_w_s', 'gmlp_b_s',
        'router_w', 'router_bias', 'exp_w1', 'exp_w3', 'exp_w2', 'shared_w1', 'shared_w3', 'shared_w2']


def kernel(**inputs):
    import concourse.bacc as bacc
    from concourse.bass_utils import run_bass_kernel_spmd

    nc = bacc.Bacc("TRN2", target_bir_lowering=False, num_devices=1)
    arrays, io = {}, {}
    for name, a in [(n, np.ascontiguousarray(inputs[n])) for n in _INS] + list(constants().items()):
        arrays[f"in_{name}"] = a
        io[name] = nc.dram_tensor(f"in_{name}", a.shape, mybir.dt.from_np(a.dtype), kind="ExternalInput").ap()
    out = nc.dram_tensor("out_x", (1, S, D), F32, kind="ExternalOutput").ap()
    dr = {
        "rows": nc.dram_tensor("rows", (1, 6 * D), F32).ap(),
        "pb": nc.dram_tensor("pb", (S + 1, B_COLS), F32).ap(),
        "bias_by_dist": nc.dram_tensor("bias_by_dist", (AH, P, 3 * P), F32).ap(),
        "x2": nc.dram_tensor("x2", (S, D), F32).ap(),
        "h2": nc.dram_tensor("h2", (S + P, D), F32).ap(),
        "acc": nc.dram_tensor("acc", (S + P, D), F32).ap(),
        "ymix": nc.dram_tensor("ymix", (S, D), F32).ap(),
    }
    build(nc, io, out, dr)
    r = run_bass_kernel_spmd(nc, [arrays], core_ids=[0])
    return r.results[0]["out_x"]
```
